# Optimizing a Trainium2 kernel written in Bass

```python
import math
import jax, jax.numpy as jnp
from jax import lax
import numpy as np

D_MODEL = 1024
BATCH = 1
SEQ = 512
DEPTH = 1
DEC_BATCH = 8
DEC_SEQ = 1
PAST_LEN = 4096
PAGE_SIZE = 128

D_MIX = D_MODEL
D_NSA = D_MIX // 2
D_CONV = D_MIX - D_NSA
HEAD_DIM = 64
N_HEADS = D_NSA // HEAD_DIM
N_KV = 2
GQ = N_HEADS // N_KV
CONV_W = 3
CMP_STRIDE = 16
CMP_RATIO = 2
CMP_LEN = CMP_STRIDE * CMP_RATIO
CMP_HIDDEN = 2 * HEAD_DIM
SLC_LEN = 64
N_SELECT = 16
WINDOW = 512
WIN_QBLOCK = 128
SLC_QBLOCK = 32
N_BUCKETS = 32
MAX_DISTANCE = 128
N_GROUPS = 4
N_EXP = 8
TOP_K = 2
D_FF = 256
ALPHA = (2 * DEPTH) ** 0.25
BETA = (8 * DEPTH) ** -0.25
NEG = -1e30
FORCE = 1e6
N_IN = D_NSA + 6 * N_KV * HEAD_DIM + 3 * N_HEADS + 3 * D_CONV

kernel_name = 'hymba_conv_nsa_hmoe_decode_step'

def _layernorm(x, g, b, eps=1e-5):
    xf = x.astype(jnp.float32)
    mu = jnp.mean(xf, -1, keepdims=True)
    var = jnp.mean(jnp.square(xf - mu), -1, keepdims=True)
    return ((xf - mu) * lax.rsqrt(var + eps)).astype(x.dtype) * g + b

def _rmsnorm(x, g, eps=1e-6):
    xf = x.astype(jnp.float32)
    return (xf * lax.rsqrt(jnp.mean(jnp.square(xf), -1, keepdims=True) + eps)).astype(x.dtype) * g

def _t5_bucket(dist):
    n = jnp.maximum(dist, 0)
    max_exact = N_BUCKETS // 2
    nf = jnp.maximum(n, 1).astype(jnp.float32)
    large = max_exact + (jnp.log(nf / max_exact) / math.log(MAX_DISTANCE / max_exact)
                         * (N_BUCKETS - max_exact)).astype(jnp.int32)
    large = jnp.minimum(large, N_BUCKETS - 1)
    return jnp.where(n < max_exact, n, large)

def _masked_softmax(s, mask):
    s = jnp.where(mask, s, NEG)
    return jax.nn.softmax(s, axis=-1) * mask.astype(jnp.float32)

def _attend(q, k, v, dist, mask, rel_bias):
    sq, sk = dist.shape
    bias = rel_bias[_t5_bucket(dist)].astype(jnp.float32)
    bias = bias.reshape(sq, sk, N_KV, GQ).transpose(2, 3, 0, 1)
    s = jnp.einsum('bqgrd,bkgd->bgrqk', q, k).astype(jnp.float32) + bias
    p = _masked_softmax(s, mask)
    o = jnp.einsum('bgrqk,bkgd->bqgrd', p.astype(v.dtype), v)
    return o, p

def _compress(k, pe, w1, w2):
    b, L, g, hd = k.shape
    n_chunks = L // CMP_STRIDE
    n_cmp = n_chunks - CMP_RATIO + 1
    ch = k[:, :n_chunks * CMP_STRIDE].reshape(b, n_chunks, CMP_STRIDE, g, hd)
    pe_r = pe.reshape(CMP_RATIO, CMP_STRIDE, hd)
    w1_r = w1.reshape(CMP_RATIO, CMP_STRIDE, hd, CMP_HIDDEN)
    h = sum(jnp.einsum('bcjgd,jde->bcge', ch[:, r:r + n_cmp] + pe_r[r][None, None, :, None, :], w1_r[r])
            for r in range(CMP_RATIO))
    return jnp.einsum('bcge,ed->bcgd', jax.nn.gelu(h), w2)

def _selected(q, ks, vs, idx, q_pos, rel_bias):
    b, sq, g, r, hd = q.shape
    L = ks.shape[1]
    n_slc = -(-L // SLC_LEN)
    pad = n_slc * SLC_LEN - L

    def blocks(t):
        t = jnp.pad(t, ((0, 0), (0, pad), (0, 0), (0, 0)))
        return t.reshape(b, n_slc, SLC_LEN, g, hd).transpose(0, 3, 1, 2, 4)

    kb, vb = blocks(ks), blocks(vs)
    n_sel = idx.shape[-1]
    qb = math.gcd(sq, SLC_QBLOCK)
    nb = sq // qb
    tbl = rel_bias.reshape(N_BUCKETS, g, r).transpose(1, 0, 2)
    gather = jax.vmap(jax.vmap(lambda blk, ix: blk[ix]))
    offs = jnp.arange(SLC_LEN, dtype=jnp.int32)

    def one(args):
        qq, ii, pp = args
        flat = ii.reshape(b, g, qb * n_sel)
        kg = gather(kb, flat).reshape(b, g, qb, n_sel * SLC_LEN, hd)
        vg = gather(vb, flat).reshape(b, g, qb, n_sel * SLC_LEN, hd)
        kpos = (ii[..., None] * SLC_LEN + offs).reshape(b, g, qb, n_sel * SLC_LEN)
        dist = pp[None, None, :, None] - kpos
        bias = jax.vmap(lambda t, bk: t[bk], in_axes=(0, 1), out_axes=1)(tbl, _t5_bucket(dist))
        s = jnp.einsum('bqgrd,bgqkd->bgrqk', qq, kg).astype(jnp.float32) \
            + bias.transpose(0, 1, 4, 2, 3).astype(jnp.float32)
        p = _masked_softmax(s, (dist >= 0)[:, :, None])
        return jnp.einsum('bgrqk,bgqkd->bqgrd', p.astype(vg.dtype), vg)

    qs = q.reshape(b, nb, qb, g, r, hd).transpose(1, 0, 2, 3, 4, 5)
    ids = idx.reshape(b, g, nb, qb, n_sel).transpose(2, 0, 1, 3, 4)
    ps = q_pos.reshape(nb, qb)
    o = lax.map(one, (qs, ids, ps))
    return o.transpose(1, 0, 2, 3, 4, 5).reshape(b, sq, g, r, hd)

def _nsa_global(q, kv, q_pos, pe_k, pe_v, w_ck1, w_ck2, w_cv1, w_cv2, rel_bias):
    L = kv.shape[1]
    kcmp = _compress(kv[:, :, 0], pe_k, w_ck1, w_ck2)
    vcmp = _compress(kv[:, :, 1], pe_v, w_cv1, w_cv2)
    n_cmp = kcmp.shape[1]
    cidx = jnp.arange(n_cmp, dtype=jnp.int32)
    ends = cidx * CMP_STRIDE + CMP_LEN - 1
    dist = q_pos[:, None] - ends[None, :]
    o_cmp, p_cmp = _attend(q, kcmp, vcmp, dist, dist >= 0, rel_bias)
    n_slc = -(-L // SLC_LEN)
    sidx = jnp.arange(n_slc, dtype=jnp.int32)
    c0 = cidx[:, None] * CMP_STRIDE
    s0 = sidx[None, :] * SLC_LEN
    shared_pos = jnp.maximum(jnp.minimum(c0 + CMP_LEN, s0 + SLC_LEN) - jnp.maximum(c0, s0), 0).astype(jnp.float32)
    imp = jnp.einsum('bgrqc,cs->bgqs', p_cmp, shared_pos)
    qblk = q_pos // SLC_LEN
    valid = sidx[None, :] <= qblk[:, None]
    forced = (sidx[None, :] == 0) | (sidx[None, :] == qblk[:, None]) | (sidx[None, :] == qblk[:, None] - 1)
    score = jnp.where(valid, imp + jnp.where(forced, FORCE, 0.0), -FORCE)
    _, idx = lax.top_k(score, min(N_SELECT, n_slc))
    o_slc = _selected(q, kv[:, :, 2], kv[:, :, 3], idx.astype(jnp.int32), q_pos, rel_bias)
    return o_cmp, o_slc

def _window_prompt(q, kw, vw, rel_bias):
    b, s = q.shape[:2]
    qb = math.gcd(s, WIN_QBLOCK)
    nb = s // qb
    span = WINDOW + qb

    def one(args):
        qq, pos = args
        kpos = pos[0] - WINDOW + jnp.arange(span, dtype=jnp.int32)
        idx = jnp.clip(kpos, 0, s - 1)
        dist = pos[:, None] - kpos[None, :]
        mask = (dist >= 0) & (dist < WINDOW) & (kpos >= 0)[None, :]
        o, _ = _attend(qq, kw[:, idx], vw[:, idx], dist, mask, rel_bias)
        return o

    qs = q.reshape(b, nb, qb, *q.shape[2:]).transpose(1, 0, 2, 3, 4, 5)
    ps = jnp.arange(s, dtype=jnp.int32).reshape(nb, qb)
    o = lax.map(one, (qs, ps))
    return o.transpose(1, 0, 2, 3, 4, 5).reshape(q.shape)

def _short_conv(u_ext, w):
    s = u_ext.shape[1] - (CONV_W - 1)
    return sum(u_ext[:, j:j + s] * w[j] for j in range(CONV_W))

def _hmoe(x, w_rg, b_rg, w_re, b_re, w_eg, w_eu, w_ed):
    lg = (x @ w_rg + b_rg).astype(jnp.float32)
    pg = jax.nn.softmax(lg, -1)
    oh_g = jax.nn.one_hot(jnp.argmax(lg, -1), N_GROUPS, dtype=jnp.float32)
    le = (x @ w_re + b_re).astype(jnp.float32).reshape(-1, N_GROUPS, N_EXP)
    pe = jax.nn.softmax(jnp.einsum('tg,tge->te', oh_g, le), -1)
    tv, ti = lax.top_k(pe, TOP_K)
    w = tv / jnp.sum(tv, -1, keepdims=True) * jnp.sum(pg * oh_g, -1, keepdims=True)
    gate_e = jnp.sum(jax.nn.one_hot(ti, N_EXP, dtype=jnp.float32) * w[..., None], 1)
    gate = (oh_g[:, :, None] * gate_e[:, None, :]).astype(x.dtype)
    out = jnp.zeros_like(x)
    for gi in range(N_GROUPS):
        h = jax.nn.silu(jnp.einsum('td,edf->tef', x, w_eg[gi])) * jnp.einsum('td,edf->tef', x, w_eu[gi])
        out = out + jnp.einsum('tef,efd->td', h * gate[:, gi, :, None], w_ed[gi])
    return out

def setup_inputs(seed: int = 0) -> dict:
    key = jax.random.key(seed)
    ks = jax.random.split(key, 32)
    f32 = jnp.float32

    def nrm(k, shape, scale):
        return jax.random.normal(k, shape, f32) * scale

    n_pages = PAST_LEN // PAGE_SIZE
    n_used = DEC_BATCH * n_pages
    n_phys = n_used + max(1, n_used // 4)
    win_buf = min(WINDOW, PAST_LEN)
    perm = jax.random.permutation(ks[0], n_phys)
    page_table = perm[:n_used].reshape(DEC_BATCH, n_pages).astype(jnp.int32)
    return {
        'x_prompt': nrm(ks[1], (BATCH, SEQ, D_MODEL), 1.0),
        'x_sample': nrm(ks[2], (DEC_BATCH, DEC_SEQ, D_MODEL), 1.0),
        'cache_kv': nrm(ks[3], (DEPTH, n_phys, PAGE_SIZE, 4, N_KV, HEAD_DIM), 1.0),
        'page_table': page_table,
        'cache_win': nrm(ks[4], (DEPTH, DEC_BATCH, win_buf, 2, N_KV, HEAD_DIM), 1.0),
        'state_conv': nrm(ks[5], (DEPTH, DEC_BATCH, CONV_W - 1, D_CONV), 1.0),
        'w_in': nrm(ks[6], (DEPTH, D_MODEL, N_IN), D_MODEL ** -0.5),
        'conv_w': nrm(ks[7], (DEPTH, CONV_W, D_CONV), CONV_W ** -0.5),
        'pe_k': nrm(ks[8], (DEPTH, CMP_LEN, HEAD_DIM), 0.1),
        'pe_v': nrm(ks[9], (DEPTH, CMP_LEN, HEAD_DIM), 0.1),
        'w_ck1': nrm(ks[10], (DEPTH, CMP_LEN, HEAD_DIM, CMP_HIDDEN), (CMP_LEN * HEAD_DIM) ** -0.5),
        'w_ck2': nrm(ks[11], (DEPTH, CMP_HIDDEN, HEAD_DIM), CMP_HIDDEN ** -0.5),
        'w_cv1': nrm(ks[12], (DEPTH, CMP_LEN, HEAD_DIM, CMP_HIDDEN), (CMP_LEN * HEAD_DIM) ** -0.5),
        'w_cv2': nrm(ks[13], (DEPTH, CMP_HIDDEN, HEAD_DIM), CMP_HIDDEN ** -0.5),
        'g_nsa': 1.0 + nrm(ks[14], (DEPTH, D_NSA), 0.05),
        'g_conv': 1.0 + nrm(ks[15], (DEPTH, D_CONV), 0.05),
        'w_out': nrm(ks[16], (DEPTH, D_MIX, D_MODEL), BETA * D_MIX ** -0.5),
        'ln1_g': 1.0 + nrm(ks[17], (DEPTH, D_MODEL), 0.05),
        'ln1_b': nrm(ks[18], (DEPTH, D_MODEL), 0.02),
        'w_rg': nrm(ks[19], (DEPTH, D_MODEL, N_GROUPS), D_MODEL ** -0.5),
        'b_rg': nrm(ks[20], (DEPTH, N_GROUPS), 0.01),
        'w_re': nrm(ks[21], (DEPTH, D_MODEL, N_GROUPS * N_EXP), D_MODEL ** -0.5),
        'b_re': nrm(ks[22], (DEPTH, N_GROUPS * N_EXP), 0.01),
        'w_eg': nrm(ks[23], (DEPTH, N_GROUPS, N_EXP, D_MODEL, D_FF), D_MODEL ** -0.5),
        'w_eu': nrm(ks[24], (DEPTH, N_GROUPS, N_EXP, D_MODEL, D_FF), D_MODEL ** -0.5),
        'w_ed': nrm(ks[25], (DEPTH, N_GROUPS, N_EXP, D_FF, D_MODEL), BETA * D_FF ** -0.5),
        'ln2_g': 1.0 + nrm(ks[26], (DEPTH, D_MODEL), 0.05),
        'ln2_b': nrm(ks[27], (DEPTH, D_MODEL), 0.02),
        'rel_bias': nrm(ks[28], (N_BUCKETS, N_HEADS), 0.2),
    }

def _split_cols(proj):
    sizes = [D_NSA] + [N_KV * HEAD_DIM] * 6 + [3 * N_HEADS] + [D_CONV] * 3
    offs = np.cumsum(sizes)[:-1].tolist()
    return jnp.split(proj, offs, axis=-1)

def reference(x_prompt, x_sample, cache_kv, page_table, cache_win, state_conv, w_in, conv_w, pe_k, pe_v,
              w_ck1, w_ck2, w_cv1, w_cv2, g_nsa, g_conv, w_out, ln1_g, ln1_b, w_rg, b_rg, w_re, b_re,
              w_eg, w_eu, w_ed, ln2_g, ln2_b, rel_bias):
    B, S, D = x_prompt.shape
    DB, DS = x_sample.shape[0], x_sample.shape[1]
    n_p, n_s = B * S, DB * DS
    n_pages = page_table.shape[1]
    past = n_pages * PAGE_SIZE
    win_buf = cache_win.shape[2]
    pos_p = jnp.arange(S, dtype=jnp.int32)
    pos_s = past + jnp.arange(DS, dtype=jnp.int32)
    xp, xs = x_prompt, x_sample
    kv_p_l, kv_s_l, win_p_l, win_s_l, conv_p_l, conv_s_l = [], [], [], [], [], []
    for l in range(DEPTH):
        X = jnp.concatenate([xp.reshape(n_p, D), xs.reshape(n_s, D)], axis=0)
        q, kc, vc, ksl, vsl, kw, vw, gt, cb, cc, chh = _split_cols(X @ w_in[l])
        q = q.reshape(-1, N_KV, GQ, HEAD_DIM) * HEAD_DIM ** -0.5
        kv_rows = jnp.stack([kc, vc, ksl, vsl], axis=1).reshape(-1, 4, N_KV, HEAD_DIM)
        win_rows = jnp.stack([kw, vw], axis=1).reshape(-1, 2, N_KV, HEAD_DIM)
        gates = jax.nn.sigmoid(gt).reshape(-1, N_KV, GQ, 3)
        u = cc * chh
        cmp_w = (pe_k[l], pe_v[l], w_ck1[l], w_ck2[l], w_cv1[l], w_cv2[l])

        q_p = q[:n_p].reshape(B, S, N_KV, GQ, HEAD_DIM)
        kv_p = kv_rows[:n_p].reshape(B, S, 4, N_KV, HEAD_DIM)
        win_p = win_rows[:n_p].reshape(B, S, 2, N_KV, HEAD_DIM)
        o_cmp_p, o_slc_p = _nsa_global(q_p, kv_p, pos_p, *cmp_w, rel_bias)
        o_win_p = _window_prompt(q_p, win_p[:, :, 0], win_p[:, :, 1], rel_bias)
        g_p = gates[:n_p].reshape(B, S, N_KV, GQ, 3)
        o_p = (g_p[..., 0:1] * o_cmp_p + g_p[..., 1:2] * o_slc_p + g_p[..., 2:3] * o_win_p).reshape(n_p, D_NSA)
        u_p_ext = jnp.pad(u[:n_p].reshape(B, S, D_CONV), ((0, 0), (CONV_W - 1, 0), (0, 0)))
        z_p = cb[:n_p].reshape(B, S, D_CONV) * _short_conv(u_p_ext, conv_w[l])

        q_s = q[n_p:].reshape(DB, DS, N_KV, GQ, HEAD_DIM)
        kv_s = kv_rows[n_p:].reshape(DB, DS, 4, N_KV, HEAD_DIM)
        win_s = win_rows[n_p:].reshape(DB, DS, 2, N_KV, HEAD_DIM)
        past_kv = cache_kv[l][page_table].reshape(DB, past, 4, N_KV, HEAD_DIM)
        kv_all = jnp.concatenate([past_kv, kv_s], axis=1)
        o_cmp_s, o_slc_s = _nsa_global(q_s, kv_all, pos_s, *cmp_w, rel_bias)
        win_all = jnp.concatenate([cache_win[l], win_s], axis=1)
        kpos_w = past - win_buf + jnp.arange(win_buf + DS, dtype=jnp.int32)
        dist_w = pos_s[:, None] - kpos_w[None, :]
        o_win_s, _ = _attend(q_s, win_all[:, :, 0], win_all[:, :, 1], dist_w,
                             (dist_w >= 0) & (dist_w < WINDOW), rel_bias)
        g_s = gates[n_p:].reshape(DB, DS, N_KV, GQ, 3)
        o_s = (g_s[..., 0:1] * o_cmp_s + g_s[..., 1:2] * o_slc_s + g_s[..., 2:3] * o_win_s).reshape(n_s, D_NSA)
        u_s_ext = jnp.concatenate([state_conv[l], u[n_p:].reshape(DB, DS, D_CONV)], axis=1)
        z_s = cb[n_p:].reshape(DB, DS, D_CONV) * _short_conv(u_s_ext, conv_w[l])

        o_nsa = jnp.concatenate([o_p, o_s], axis=0)
        o_conv = jnp.concatenate([z_p.reshape(n_p, D_CONV), z_s.reshape(n_s, D_CONV)], axis=0)
        mix = jnp.concatenate([_rmsnorm(o_nsa, g_nsa[l]), _rmsnorm(o_conv, g_conv[l])], axis=-1) @ w_out[l]
        X1 = _layernorm(ALPHA * X + mix, ln1_g[l], ln1_b[l])
        X2 = _layernorm(ALPHA * X1 + _hmoe(X1, w_rg[l], b_rg[l], w_re[l], b_re[l], w_eg[l], w_eu[l], w_ed[l]),
                        ln2_g[l], ln2_b[l])
        xp = X2[:n_p].reshape(B, S, D)
        xs = X2[n_p:].reshape(DB, DS, D)

        kv_p_l.append(kv_p)
        kv_s_l.append(kv_s)
        win_p_l.append(win_p[:, S - min(WINDOW, S):])
        win_s_l.append(win_all[:, win_all.shape[1] - min(WINDOW, past + DS):])
        conv_p_l.append(u_p_ext[:, u_p_ext.shape[1] - (CONV_W - 1):])
        conv_s_l.append(u_s_ext[:, u_s_ext.shape[1] - (CONV_W - 1):])
    return (xp, xs, jnp.stack(kv_p_l), jnp.stack(kv_s_l), jnp.stack(win_p_l), jnp.stack(win_s_l),
            jnp.stack(conv_p_l), jnp.stack(conv_s_l))


_drawn_inputs = setup_inputs


def setup_inputs(seed=0):
    import zlib

    import numpy as np

    out = dict(_drawn_inputs(seed))
    spreads = {}
    factors = {'pe_k': 3.161, 'g_nsa': 2.827, 'g_conv': 2.746, 'b_rg': 23.763, 'b_re': 8.0, 'ln2_b': 3.12}
    for name, (base, spread) in spreads.items():
        noise = np.random.default_rng([zlib.crc32(name.encode()), seed]).standard_normal(out[name].shape)
        drawn = base * np.exp(spread * noise) if base else spread * noise
        out[name] = __import__('jax').numpy.asarray(drawn.astype(out[name].dtype))
    for name, factor in factors.items():
        out[name] = (out[name] * factor).astype(out[name].dtype)
    return out
```

```python
from contextlib import ExitStack
import math

import numpy as np
import concourse.bass as bass
from concourse import mybir

F32 = mybir.dt.float32
I32 = mybir.dt.int32
U32 = mybir.dt.uint32
ACT = mybir.ActivationFunctionType
ALU = mybir.AluOpType
AX = mybir.AxisListType.X
ds = bass.ds

P = 128
D = 1024
KT = D // P
SEQ, DB = 512, 8
TOK = SEQ + DB
HALF = TOK // 2
QT = SEQ // P
TT = QT + 1
HD, NKV, GQ = 64, 2, 4
NH = NKV * GQ
DG = NH * HD
KVW = NKV * HD
CT = DG // P
PAST, PAGE = 4096, 128
PAGES = PAST // PAGE
STRIDE, CLEN = 16, 32
NJ = CLEN // 2
JP = STRIDE // 2
CHUNKS = PAST // STRIDE
NCMP = CHUNKS - 1
PCH = SEQ // STRIDE
PCMP = PCH - 1
SLC = 64
WIN = 512
BUCKETS, MAXD = 32, 128
NG, NE = 4, 8
EX = NG * NE
FF = 256
NEG = -1e30
ALPHA = 2.0 ** 0.25
SCALE = HD ** -0.5
HCOLS = 1024
HW = 880
SEL = 15
SELK = 7 * P + SLC + 1
TOPB = SEL - 2
CAP = 96
PASSES = -(-TOK // CAP)
SLOTS = PASSES * EX
GATES = 3 * NH
O_KV = DG
O_GATE = O_KV + 6 * KVW
O_CONV = O_GATE + GATES


def bucket(dist):
    n = np.maximum(dist, 0)
    nf = np.maximum(n, 1).astype(np.float32)
    half = BUCKETS // 2
    large = half + (np.log(nf / np.float32(half)) / np.float32(math.log(MAXD / half))
                    * np.float32(BUCKETS - half)).astype(np.int32)
    return np.where(n < half, n, np.minimum(large, BUCKETS - 1))


def onehot(dist):
    out = np.zeros((BUCKETS + 1, len(dist)), np.float32)
    out[np.where(dist >= 0, bucket(dist), BUCKETS), np.arange(len(dist))] = 1.0
    return out


def constants():
    p = np.arange(P)
    c = {}
    c["ident"] = np.eye(P)
    c["tri"] = (p[:, None] < p[None, :])
    c["ones"] = np.ones((P, P))
    c["rep16"] = (p[:16, None] == p[None, :] // 8)
    c["rep_bg"] = (np.arange(DB)[:, None] == np.arange(16)[None, :] // 2)
    k, j, q = np.arange(16)[:, None, None], np.arange(8)[None, :, None], p[None, None, :]
    c["sel_pair"] = (k == 2 * j + (q >= SLC)).reshape(16, -1)
    k, b, g = np.arange(16)[:, None, None], np.arange(8)[None, :, None], np.arange(8)[None, None, :]
    c["sel_b"] = (k == 2 * b + g // GQ).reshape(16, -1)
    c0 = np.arange(2 * P)[:, None] * STRIDE
    s0 = np.arange(65)[None, :] * SLC
    shared = np.maximum(np.minimum(c0 + CLEN, s0 + SLC) - np.maximum(c0, s0), 0)
    c["shared"] = shared.reshape(2, P, 65).transpose(1, 0, 2).reshape(P, -1)
    dm = np.eye(BUCKETS)
    dm[BUCKETS - 1] -= 1
    c["dmat"] = dm
    c["hot_prompt"] = onehot(np.arange(HCOLS) - 511)
    c["hot_cmp"] = onehot(PAST - (np.arange(NCMP) * STRIDE + CLEN - 1))
    r = 4 * np.arange(P)[None, :] + np.arange(4)[:, None]
    c["hot_win"] = onehot(np.where(r == 0, 0, WIN - r).ravel())
    c["hot_sel"] = onehot(np.concatenate([SLC - np.arange(SLC), 2 * SLC - np.arange(SLC), [0]]))
    c["cidx"] = 2 * ((p[:, None] % 8) * STRIDE + np.arange(16)[None, :])
    c["iota"] = np.tile(np.arange(PAGES), (P, 1))
    c["slot_iota"] = np.tile(np.arange(SLOTS), (P, 1))
    c["choice"] = 2 * (p[:, None] + P * (np.arange(2 * TT)[None, :] // 2)) + np.arange(2 * TT)[None, :] % 2 + 1
    c["spare"] = (2 * TOK + 1 + p)[:, None]
    c["pos64"] = (2 * (p % SLC) + 1)[:, None]
    at, out = 0, {}
    for name, a in c.items():
        full = np.zeros((P, a.shape[1]), np.float32)
        full[:a.shape[0]] = a
        out[name] = (at, full)
        at += a.shape[1]
    return out


class Own:

    def __init__(self, engine, sem):
        self.engine, self.sem, self.n, self.turn = engine, sem, 0, None

    def did(self, instruction):
        instruction.then_inc(self.sem, 1)
        self.n += 1

    def settle(self):
        self.engine.wait_ge(self.sem, self.n if self.turn is None else self.turn + self.n)

    def enter(self, turn, per):
        self.turn, self.start, self.per = turn * per, self.n, per

    def leave(self, turns):
        assert self.n - self.start == self.per, (self.n - self.start, self.per)
        self.turn, self.n = None, self.start + turns * self.per


A_ONLY = ("rep16", "dmat", "hot_prompt", "hot_cmp", "hot_win", "hot_sel", "cidx")
C_ONLY = ("sel_pair",)
E_ONLY = ("slot_iota", "tri", "choice", "spare")


class Store:
    pass


def project(nc, ctx, io, psum, long, mid):
    def sb(name, shape, dt=F32):
        return ctx.enter_context(nc.sbuf_tensor(name, shape, dt))

    def sem(name):
        return ctx.enter_context(nc.semaphore(name))

    xin = sb("xin", [P, TT, D])
    xT = sb("xT", [P, KT, TOK])
    wring = sb("wring", [P, 2, KT, 3 * P])
    wgate = sb("wgate", [P, KT, GATES])
    kvT = sb("kvT", [P, 6, TOK])
    gateT = sb("gateT", [GATES, TOK])
    hA = sb("hA", [P, io.cA.shape[1]])
    rows_in = sb("rows_in", [16, DG])
    small_in = sb("small_in", [16, 3 * P + DG])
    conv = kvT[:, :, :].rearrange("p i n -> p (i n)")
    chT = conv[:, 0:TOK]
    u = conv[:, TOK:2 * TOK + 2]
    acc = conv[:, 2 * TOK + 2:3 * TOK + 2]
    ukeep = sb("ukeep", [P, CT, 10])
    urows = xin[0:10, 0, 0:DG]
    vh = xin[0:NH, 1, :]
    coef = sb("coef", [P, 116])
    tab = sb("tab", [BUCKETS + 1, NH])
    relb = sb("relb", [BUCKETS, NH])
    pg_i = sb("pg_i", [16, 16], I32)
    pg_f = sb("pg_f", [16, 16])

    def cA(name, rows=P):
        at, full = io.where[name]
        return hA[0:rows, at:at + full.shape[1]]

    def c0(name, rows=P):
        return long.c0(name, rows)

    ident = c0("ident")
    x_loaded = sem("x_loaded")
    consts_loaded = sem("consts_loaded")
    small_loaded = sem("small_loaded")
    w_loaded = [sem(f"w_loaded{s}") for s in range(2)]
    gate_w_loaded = sem("gate_w_loaded")
    xT_made = sem("xT_made")
    xT_act, xT_dve = sem("xT_act"), sem("xT_dve")
    mtile = sem("mtile")
    mt_act, mt_dve = sem("mt_act"), sem("mt_dve")
    mt_cc, mt_cb = sem("mt_cc"), sem("mt_cb")
    kvt_made = sem("kvt_made")
    kvt_act, kvt_dve = sem("kvt_act"), sem("kvt_dve")
    small_made, small_dve = sem("small_made"), sem("small_dve")
    misc_made, misc_dve = sem("misc_made"), sem("misc_dve")
    u_made, urows_done = sem("u_made"), sem("urows_done")
    idx_ready = sem("idx_ready")
    gathered = mid.gathered
    stores = sem("stores")
    table_stored = sem("table_stored")
    relaid = sem("relaid")
    own_dve = sem("own_dve_a")
    block = ctx.enter_context(nc.Block())

    w_in = io.w_in.rearrange("l (k p) n -> (l p) k n", p=P)

    @block.sync
    def _(sp):
        for t in range(QT):
            sp.dma_start(xin[:, t, :], io.x_prompt[0, t * P:(t + 1) * P, :]).then_inc(x_loaded, 16)
        sp.dma_start(xin[0:DB, QT, :], io.x_sample.rearrange("b s d -> (b s) d")).then_inc(x_loaded, 16)
        for c in range(2):
            for g in range(NKV):
                for i in range(2):
                    col = g * GQ * HD + (2 * c + i) * HD
                    sp.dma_start(wring[:, c, :, i * P + g * HD:i * P + (g + 1) * HD],
                                 w_in[:, :, col:col + HD]).then_inc(w_loaded[c], 16)
        sp.dma_start(wgate[:, :, :], w_in[:, :, O_GATE:O_GATE + GATES]).then_inc(gate_w_loaded, 16)
        for c in range(2):
            sp.wait_ge(mtile, 2 * c + 2)
            col = O_KV + 3 * c * P
            sp.dma_start(wring[:, c, :, :], w_in[:, :, col:col + 3 * P]).then_inc(w_loaded[c], 16)
        with sp.Fori(0, CT // 2) as pair:
            ct = pair * 2
            for s in range(2):
                sp.wait_ge(mtile, ct * 3 + 8 + 3 * s)
                for n, part in enumerate((2, 1, 0)):
                    sp.dma_start(wring[:, s, :, n * P:(n + 1) * P],
                                 w_in[:, :, ds(ct * P + O_CONV + part * DG + s * P, P)]
                                 ).then_inc(w_loaded[s], 16)
        sp.wait_ge(misc_dve, 4)
        sp.dma_start(io.vhan, vh).then_inc(stores, 16)
        sp.wait_ge(kvt_act, TT)
        sp.wait_ge(kvt_dve, TT)
        for t in range(QT):
            sp.dma_start(io.new_kv_prompt[t * P:(t + 1) * P, :], long.kvtok[:, t, 0:4 * KVW]).then_inc(stores, 16)
            sp.dma_start(io.new_win_prompt[t * P:(t + 1) * P, :], long.kvtok[:, t, 4 * KVW:]).then_inc(stores, 16)
        sp.dma_start(io.new_kv_sample, long.kvtok[0:DB, QT, 0:4 * KVW]).then_inc(stores, 16)
        sp.dma_start(io.fresh, long.kvtok[0:DB, QT, :]).then_inc(stores, 16)
        sp.dma_start(io.new_win_sample[:, WIN - 1, :], long.kvtok[0:DB, QT, 4 * KVW:]).then_inc(stores, 16)
        sp.wait_ge(urows_done, 1)
        sp.dma_start(io.new_conv_prompt, urows[0:2, :]).then_inc(stores, 16)
        sp.dma_start(io.new_conv_sample[:, 1, :], urows[2:10, :]).then_inc(stores, 16)
        sp.wait_ge(stores, 16 * (2 * QT + 6 + DB + 1))

    @block.scalar
    def _(act):
        act.dma_start(long.consts[:, :], io.c0).then_inc(consts_loaded, 16)
        act.dma_start(hA[:, :], io.cA).then_inc(consts_loaded, 16)
        act.dma_start(rows_in[:, :], io.state_conv.rearrange("b j c -> (b j) c")).then_inc(small_loaded, 16)
        act.dma_start(small_in[0:3, 0:DG], io.conv_w).then_inc(small_loaded, 16)
        act.dma_start(small_in[0:CT, DG:DG + P], io.g_nsa.rearrange("(c p) -> c p", p=P)).then_inc(small_loaded, 16)
        act.dma_start(small_in[0:CT, DG + P:DG + 2 * P], io.g_conv.rearrange("(c p) -> c p", p=P)).then_inc(small_loaded, 16)
        act.dma_start(mid.pe_in[:, 0, :], io.pe_k.rearrange("(l q) d -> l (q d)", q=2)).then_inc(small_loaded, 16)
        act.dma_start(mid.pe_in[:, 1, :], io.pe_v.rearrange("(l q) d -> l (q d)", q=2)).then_inc(small_loaded, 16)
        act.dma_start(relb[:, :], io.rel_bias).then_inc(small_loaded, 16)
        act.dma_start(pg_i[:, :].rearrange("p (b h) -> p b h", h=2),
                      io.page_table.rearrange("b (h p) -> p b h", p=16),
                      allow_slow_non_contiguous=True).then_inc(small_loaded, 16)
        for b in range(DB):
            src = io.cache_win[b, 1:WIN, :].rearrange("r c -> (r c)").rearrange("(a n) -> a n", a=16)
            dst = io.new_win_sample[b, 0:WIN - 1, :].rearrange("r c -> (r c)").rearrange("(a n) -> a n", a=16)
            act.dma_start(dst, src).then_inc(stores, 16)
        act.dma_start(io.new_conv_sample[:, 0, :], io.state_conv[:, 1, :]).then_inc(stores, 16)
        for t in range(TT):
            act.wait_ge(xT_made, t + 1)
            n = P if t < QT else DB
            act.copy(xT[:, 4:8, t * P:t * P + n],
                     psum[:, 7, 0:4 * n].rearrange("p (k n) -> p k n", n=n)).then_inc(xT_act, 1)
        for m in range(11):
            act.wait_ge(mtile, m + 1)
            src = psum[:, 2 * (m % 3), 0:HALF]
            if m < 4:
                act.mul(long.qT[:, m, 0:HALF], src, SCALE).then_inc(mt_act, 1)
            elif m < 10:
                act.copy(kvT[:, m - 4, 0:HALF], src).then_inc(mt_act, 1)
            else:
                act.activation(gateT[:, 0:HALF], src[0:GATES, :], ACT.Sigmoid).then_inc(mt_act, 1)
                act.activation(gateT[:, HALF:TOK], psum[0:GATES, 2 * (m % 3) + 1, 0:HALF],
                               ACT.Sigmoid).then_inc(mt_act, 1)
        for t in range(TT):
            n = P if t < QT else DB
            act.wait_ge(kvt_made, 2 * t + 1)
            act.copy(long.kvtok[0:n, t, 0:4 * P], psum[0:n, 6, :]).then_inc(kvt_act, 1)
        act.wait_ge(mt_dve, 10)
        for i in range(2):
            for g in range(NKV):
                for par in range(2):
                    src = kvT[g * HD:(g + 1) * HD, i, 0:SEQ].rearrange(
                        "p (c j q) -> p q j c", q=2, j=JP)[:, par]
                    act.copy(mid.xTp[par * HD:(par + 1) * HD, 2 * i + g, :, :], src).then_inc(relaid, 1)
        act.wait_ge(relaid, 8)
        with act.Fori(0, CT) as ct:
            for h in range(2):
                if h == 0:
                    act.wait_ge(mtile, ct * 3 + 12)
                    act.wait_ge(mt_cc, ct * 1 + 1)
                act.copy(chT[:, h * HALF:(h + 1) * HALF], psum[:, 4 + h, 0:HALF]).then_inc(mt_act, 1)

    @block.tensor
    def _(pe):
        pe.wait_ge(consts_loaded, 32)
        pe.wait_ge(x_loaded, 16 * TT)
        for t in range(TT):
            n = P if t < QT else DB
            if t:
                pe.wait_ge(xT_act, t)
                pe.wait_ge(xT_dve, t)
            for k in range(KT):
                last = pe.transpose(psum[:, 6 + k // 4, (k % 4) * n:(k % 4 + 1) * n],
                                    xin[0:n, t, k * P:(k + 1) * P], ident[0:n, 0:n])
            last.then_inc(xT_made, 1)
        pe.wait_ge(xT_act, TT)
        pe.wait_ge(xT_dve, TT)

        def tile(bank, w, width):
            for h in range(2):
                for k in range(KT):
                    last = pe.matmul(psum[0:width, bank + h, 0:HALF], w(k),
                                     xT[:, k, h * HALF:(h + 1) * HALF], start=k == 0, stop=k == KT - 1)
            last.then_inc(mtile, 1)

        def small_transposes():
            pe.wait_ge(small_loaded, 16 * 8)
            for ct in range(CT):
                pe.transpose(psum[:, 6, 16 * ct:16 * ct + 16], rows_in[0:16, ct * P:(ct + 1) * P], ident[0:16, 0:16])
                pe.transpose(psum[:, 6, 64 + 3 * ct:67 + 3 * ct], small_in[0:3, ct * P:(ct + 1) * P], ident[0:3, 0:3])
            for n in range(2):
                pe.transpose(psum[:, 6, 76 + CT * n:80 + CT * n], small_in[0:CT, DG + n * P:DG + (n + 1) * P],
                             ident[0:CT, 0:CT])
            for n in range(2):
                last = pe.transpose(psum[:, 6, 84 + 16 * n:100 + 16 * n], mid.pe_in[:, n, :], ident[0:16, 0:16])
            last.then_inc(small_made, 1)
            pe.matmul(psum[0:BUCKETS, 7, 0:NH], cA("dmat", BUCKETS), relb[:, :], start=True, stop=True)
            pe.wait_ge(idx_ready, 1)
            pe.matmul(psum[:, 7, 16:32], cA("rep16", 16), pg_f[:, :], start=True, stop=True).then_inc(misc_made, 1)

        def bias_tables():
            pe.wait_ge(small_dve, 1)
            pe.wait_ge(misc_dve, 3)
            for h in range(2):
                last = pe.matmul(psum[0:NH, 6 + h, :], tab[:, :], cA("hot_prompt", BUCKETS + 1)[:, h * 512:(h + 1) * 512],
                                 start=True, stop=True)
            last.then_inc(misc_made, 1)

        def sample_tables():
            pe.wait_ge(misc_dve, 4)
            pe.matmul(psum[0:NH, 6, :], tab[:, :], cA("hot_win", BUCKETS + 1), start=True, stop=True)
            pe.matmul(psum[0:NH, 7, 0:NCMP], tab[:, :], cA("hot_cmp", BUCKETS + 1), start=True, stop=True)
            pe.matmul(psum[0:NH, 7, NCMP:NCMP + 129], tab[:, :], cA("hot_sel", BUCKETS + 1),
                      start=True, stop=True).then_inc(misc_made, 1)

        for m in range(10):
            c, i = (m // 2, m % 2) if m < 4 else ((m - 4) // 3, (m - 4) % 3)
            if m in (0, 2):
                pe.wait_ge(w_loaded[c], 16 * 4)
            if m in (4, 7):
                pe.wait_ge(w_loaded[c], 16 * 5)
            if m >= 3:
                pe.wait_ge(mt_act, m - 2)
                pe.wait_ge(mt_dve, m - 2)
            tile(2 * (m % 3), lambda k: wring[:, c, k, i * P:(i + 1) * P], P)
            if m == 0:
                small_transposes()
            if m == 1:
                bias_tables()
            if m == 2:
                sample_tables()
        pe.wait_ge(gate_w_loaded, 16)
        pe.wait_ge(mt_act, 8)
        pe.wait_ge(mt_dve, 8)
        tile(2, lambda k: wgate[:, k, :], GATES)
        pe.wait_ge(misc_dve, 6)
        pe.wait_ge(mt_act, 12)
        pe.wait_ge(mt_dve, 10)
        for t in range(TT):
            n = P if t < QT else DB
            if t:
                pe.wait_ge(kvt_act, t)
            for i in range(4):
                last = pe.transpose(psum[0:n, 6, i * P:(i + 1) * P], kvT[:, i, t * P:t * P + n], ident)
            last.then_inc(kvt_made, 1)
            if t:
                pe.wait_ge(kvt_dve, t)
            for i in range(4, 6):
                pe.transpose(psum[0:n, 7, (i - 4) * P:(i - 3) * P], kvT[:, i, t * P:t * P + n], ident)
            pe.transpose(psum[0:n, 7, 2 * P:2 * P + GATES], gateT[:, t * P:t * P + n],
                         ident[0:GATES, 0:GATES]).then_inc(kvt_made, 1)
        with pe.Fori(0, CT // 2) as pair:
            ct = pair * 2
            for s in range(2):
                pe.wait_ge(w_loaded[s], ct * 24 + 16 * (5 + 3))
                for n, bank in enumerate((4, 0, 2)):
                    if n == 0:
                        pe.wait_ge(mt_act, ct * 2 + 12 + 2 * s)
                    elif n == 1:
                        pe.wait_ge(mt_cc, ct + s + 1)
                    else:
                        pe.wait_ge(mt_cb, ct + s + 1)
                    tile(bank, lambda k: wring[:, s, k, n * P:(n + 1) * P], P)
        pe.wait_ge(u_made, CT)
        pe.wait_ge(kvt_act, TT)
        for ct in range(CT):
            last = pe.transpose(psum[0:10, 6, ct * P:(ct + 1) * P], ukeep[:, ct, :], ident)
        last.then_inc(misc_made, 1)

    @block.vector
    def _(dve):
        own = Own(dve, own_dve)
        own.did(dve.memset(long.q8[:, :, :], 0.0))
        own.did(dve.memset(tab[:, :], NEG))
        dve.wait_ge(small_loaded, 16 * 8)
        dve.tensor_copy(pg_f[:, :], pg_i[:, :]).then_inc(idx_ready, 1)
        for t in range(TT):
            dve.wait_ge(xT_made, t + 1)
            n = P if t < QT else DB
            dve.tensor_copy(xT[:, 0:4, t * P:t * P + n],
                            psum[:, 6, 0:4 * n].rearrange("p (k n) -> p k n", n=n)).then_inc(xT_dve, 1)

        def small_tables():
            dve.wait_ge(small_made, 1)
            own.did(dve.tensor_copy(long.gains[:, :], psum[:, 6, 76:84]))
            own.did(dve.tensor_copy(mid.peT[:, :], psum[:, 6, 84:116]))
            dve.tensor_copy(coef[:, 0:76], psum[:, 6, 0:76]).then_inc(small_dve, 1)
            dve.wait_ge(misc_made, 1)
            own.settle()
            dve.tensor_copy(tab[0:BUCKETS, :], psum[0:BUCKETS, 7, 0:NH]).then_inc(misc_dve, 1)
            own.did(dve.tensor_copy(mid.pages[:, :], psum[:, 7, 16:32]))
            own.settle()
            dve.tensor_scalar(mid.pages[:, :], mid.pages[:, :], 2.0 * PAGE, None, ALU.mult).then_inc(misc_dve, 1)
            dve.wait_ge(misc_dve, 2)
            dve.tensor_tensor(mid.idx[:, :, :],
                              mid.pages[:, :].unsqueeze(2).to_broadcast([P, 16, 16]),
                              cA("cidx").unsqueeze(1).to_broadcast([P, 16, 16]), ALU.add).then_inc(misc_dve, 1)

        def tables():
            dve.wait_ge(misc_made, 2)
            own.did(dve.tensor_copy(vh[:, 0:512], psum[0:NH, 6, :]))
            dve.tensor_copy(vh[:, 512:1024], psum[0:NH, 7, :]).then_inc(misc_dve, 1)

        def tables2():
            dve.wait_ge(misc_made, 3)
            dve.tensor_copy(long.b_win[:, :], psum[0:NH, 6, :]).then_inc(misc_dve, 1)
            dve.tensor_copy(long.b_cs[:, :], psum[0:NH, 7, 0:NCMP + 129]).then_inc(misc_dve, 1)

        for m in range(10):
            dve.wait_ge(mtile, m + 1)
            src = psum[:, 2 * (m % 3) + 1, 0:HALF]
            if m < 4:
                dve.tensor_scalar(long.qT[:, m, HALF:TOK], src, SCALE, None, ALU.mult).then_inc(mt_dve, 1)
            else:
                dve.tensor_copy(kvT[:, m - 4, HALF:TOK], src).then_inc(mt_dve, 1)
            if m == 0:
                small_tables()
            if m == 1:
                tables()
            if m == 2:
                tables2()
        dve.wait_ge(mt_dve, 10)
        own.settle()
        for g in range(NKV):
            rows = slice(g * HD, (g + 1) * HD)
            own.did(dve.tensor_copy(long.q8[rows, :, g * GQ:(g + 1) * GQ],
                                    long.qT[rows, :, SEQ:TOK].rearrange("p r b -> p b r")))
        for t in range(TT):
            n = P if t < QT else DB
            dve.wait_ge(kvt_made, 2 * t + 2)
            own.did(dve.tensor_copy(long.kvtok[0:n, t, 4 * P:6 * P], psum[0:n, 7, 0:2 * P]))
            dve.tensor_copy(long.gates[0:n, t, :], psum[0:n, 7, 2 * P:2 * P + GATES]).then_inc(kvt_dve, 1)
        dve.wait_ge(mt_act, 12)
        own.did(dve.tensor_copy(long.kT[:, 0, :], kvT[:, 2, :]))
        own.did(dve.tensor_copy(long.kT[:, 1, :], kvT[:, 4, :]))
        dve.wait_ge(relaid, 8)
        dve.wait_ge(mtile, 12)
        own.settle()
        own.did(dve.memset(u[:, 0:2], 0.0))
        dve.sem_inc(mt_cc, 1)
        dve.sem_inc(mt_cb, 1)
        with dve.Fori(0, CT) as ct:
            own.enter(ct, 8)
            dve.wait_ge(mt_act, ct * 2 + 14)
            dve.wait_ge(mtile, ct * 3 + 13)
            own.settle()
            dve.wait_ge(mt_cb, ct + 1)
            own.did(dve.tensor_tensor(u[:, 2:2 + HALF], psum[:, 0, 0:HALF], chT[:, 0:HALF], ALU.mult))
            dve.tensor_tensor(u[:, 2 + HALF:], psum[:, 1, 0:HALF], chT[:, HALF:TOK], ALU.mult).then_inc(mt_cc, 1)
            own.settle()
            dve.wait_ge(mt_cc, ct + 2)
            taps = [coef[:, ds(ct * 3 + 64 + j, 1)] for j in range(3)]
            old = [coef[:, ds(ct * 16 + j, 16 - j)][:, ::2] for j in range(2)]
            own.did(dve.tensor_scalar(acc[:, 0:SEQ], u[:, 2:2 + SEQ], taps[2], None, ALU.mult))
            own.did(dve.tensor_scalar(acc[:, SEQ:TOK], u[:, 2 + SEQ:], taps[2], None, ALU.mult))
            own.settle()
            own.did(dve.scalar_tensor_tensor(acc[:, 0:SEQ], u[:, 1:1 + SEQ], taps[1], acc[:, 0:SEQ], ALU.mult, ALU.add))
            own.did(dve.scalar_tensor_tensor(acc[:, SEQ:TOK], old[1], taps[1], acc[:, SEQ:TOK], ALU.mult, ALU.add))
            own.settle()
            own.did(dve.scalar_tensor_tensor(acc[:, 0:SEQ], u[:, 0:SEQ], taps[0], acc[:, 0:SEQ], ALU.mult, ALU.add))
            own.did(dve.scalar_tensor_tensor(acc[:, SEQ:TOK], old[0], taps[0], acc[:, SEQ:TOK], ALU.mult, ALU.add))
            dve.tensor_copy(ukeep[:, ds(ct, 1), :], u[:, SEQ:SEQ + 10].unsqueeze(1)).then_inc(u_made, 1)
            dve.wait_ge(u_made, ct + 1)
            dve.wait_ge(mtile, ct * 3 + 14)
            own.settle()
            z = long.zT[:, ds(ct, 1), :].rearrange("p a n -> p (a n)")
            own.did(dve.tensor_tensor(z[:, 0:HALF], psum[:, 2, 0:HALF], acc[:, 0:HALF], ALU.mult))
            dve.tensor_tensor(z[:, HALF:TOK], psum[:, 3, 0:HALF], acc[:, HALF:TOK], ALU.mult).then_inc(mt_cb, 1)
        own.leave(CT)
        dve.wait_ge(misc_made, 4)
        dve.tensor_copy(urows, psum[0:10, 6, :]).then_inc(urows_done, 1)

    @block.gpsimd
    def _(pool):
        pool.wait_ge(misc_dve, 3)
        for s in range(4):
            mid.gather(pool, s, s, s)


def compress(nc, ctx, io, psum, long, mid):
    def sb(name, shape, dt=F32):
        return ctx.enter_context(nc.sbuf_tensor(name, shape, dt))

    def sem(name):
        return ctx.enter_context(nc.semaphore(name))

    w1 = sb("w1", [P, 2, NJ, P])
    w2 = sb("w2", [P, 2, HD])
    cT = sb("cT", [P, 2, NKV, JP, CHUNKS])
    cbias = sb("cbias", [P, 2])
    hid = sb("hid", [P, 2, CHUNKS])
    kc = sb("kc", [P, CHUNKS])
    vc = sb("vc", [P, 2, KVW])
    wraw = sb("wraw", [P, 2, 4, 2 * KVW])
    kwT = sb("kwT", [P, 4 * P])
    q8 = sb("q8s", [P, 2, NH])
    sc = sb("sc", [NH, 2, WIN])
    ex = sb("ex", [NH, 2, WIN])
    st = sb("st", [NH, 2, 4])
    pT = sb("pT", [P, 2, 4 * NH])
    ident = long.c0("ident")

    w_loaded = sem("cw_loaded")
    gathered = mid.gathered
    win_loaded = [sem(f"win_loaded{u}") for u in range(2)]
    win_new = [sem(f"win_new{u}") for u in range(2)]
    c_made, c_act, c_dve = sem("c_made"), sem("c_act"), sem("c_dve")
    h_made, h_act = sem("h_made"), sem("h_act")
    o_made, o_dve = sem("o_made"), sem("o_dve")
    b_made, b_dve = sem("b_made"), sem("b_dve")
    q_staged = sem("q_staged")
    neg_max = sem("neg_max")
    exp_made = sem("exp_made")
    prob_made = sem("prob_made")
    bias_made, bias_read = sem("cb_made"), sem("cb_read")
    own_dve, own_act = sem("own_dve_b"), sem("own_act_b")
    block = ctx.enter_context(nc.Block())

    STEPS = 4
    USES = 7

    def schedule():
        out = {s: [] for s in range(9)}
        for i in range(4):
            out[i].append(("w", 0, i))
            out[4 + i].append(("w", 1, i))
        for i in range(3):
            out[4 + i].append(("c", 0, i))
            out[8].append(("c", 1, i))
        return out

    PLAN = schedule()
    TICKET = {use: n for n, use in enumerate(use for s in range(9) for use in PLAN[s])}
    SOFT = {use[:2]: n for n, use in enumerate(sorted(
        (use for use in TICKET if use[2] == (0 if use[0] == "c" else 1)), key=TICKET.get))}

    @block.sync
    def _(sp):
        for n, w in enumerate((io.w_ck1, io.w_cv1)):
            sp.dma_start(w1[:, n, :, :], w.rearrange("l d e -> (l d) e").rearrange("(j q) e -> q j e", q=P)
                         ).then_inc(w_loaded, 16)
        sp.dma_start(w2[:, 0, :], io.w_ck2).then_inc(w_loaded, 16)
        sp.dma_start(w2[:, 1, :], io.w_cv2).then_inc(w_loaded, 16)

        def window(b, u, landed):
            sp.dma_start(wraw[:, u, :, :].rearrange("p t c -> p (t c)"),
                         io.cache_win[ds(b, 1)].rearrange("b (p t) c -> (b p) (t c)", t=4)
                         ).then_inc(win_loaded[u], 16)
            sp.wait_ge(win_loaded[u], landed)
            sp.dma_start(wraw[0:1, u, 0, :], io.fresh[ds(b, 1), 4 * KVW:]).then_inc(win_new[u], 16)

        for u in range(2):
            window(u, u, 16)
        with sp.Fori(0, DB // 2 - 1) as pair:
            b = pair * 2
            for u in range(2):
                sp.wait_ge(b_dve, b * USES + TICKET["w", u, 3] + 2)
                window(b + 2 + u, u, b * 8 + 32)

    @block.gpsimd
    def _(pool):
        with pool.Fori(0, DB // 2 - 1) as pair:
            b = pair * 2
            for u in range(2):
                pool.wait_ge(c_made, b * 16 + 16 * (u + 1))
                for h in range(2):
                    mid.gather(pool, 2 * u + h, b * 2 + 4 + 2 * u + h, b * 2 + 4 + 2 * u + h)

    @block.tensor
    def _(pe):
        pe.wait_ge(w_loaded, 16 * 4)
        for n in range(2):
            for j in range(NJ):
                last = pe.matmul(psum[:, 7, n:n + 1], w1[:, n, j, :], mid.peT[:, NJ * n + j:NJ * n + j + 1],
                                 start=j == 0, stop=j == NJ - 1)
        last.then_inc(bias_made, 1)
        pe.wait_ge(bias_read, 1)

        def transposes(b, unit, fills):
            u, n = unit // 2, unit % 2
            if n == 0 and 0 in fills:
                for h in range(2):
                    pe.wait_ge(gathered[2 * u + h], b * 128 + 256)
            for f in fills:
                done = b * 8 + 4 * unit + f // 2
                pe.wait_ge(c_act if f % 2 else c_dve, (done if unit == 0 and f < 2 else done - 1) + 1)
                for j in range(2):
                    for h in range(2):
                        last = pe.transpose(psum[:, f % 4, j * CHUNKS + h * P:j * CHUNKS + (h + 1) * P],
                                            mid.raw[:, 2 * u + h, 2 * f + j, n * KVW:(n + 1) * KVW], ident)
                last.then_inc(c_made, 1)

        def hidden(b, s):
            unit, n, g = s // 2, s % 4 // 2, s % 2
            pe.wait_ge(c_dve, b * 8 + 4 * unit + 5)
            pe.wait_ge(c_act, b * 8 + 4 * unit + 5)
            for r in range(2):
                for j in range(JP):
                    last = pe.matmul(psum[:, 4 + s % 2, 0:NCMP], w1[:, n, r * JP + j, :],
                                     cT[:, unit % 2, g, j, r:r + NCMP], start=r + j == 0, stop=r + j == JP)
            last.then_inc(h_made, 1)

        def output(b, s):
            u, n, g = s // 4, s % 4 // 2, s % 2
            pe.wait_ge(h_act, b * 4 + s + 1)
            if g == 0:
                pe.wait_ge(o_dve, b * 2 + 2 * u + n + 1)
            if n == 0:
                last = pe.matmul(psum[g * HD:(g + 1) * HD, 6, 0:NCMP], w2[:, 0, :], hid[:, s % 2, 0:NCMP],
                                 start=True, stop=True)
            else:
                for h in range(2):
                    m = P if h == 0 else NCMP - P
                    last = pe.matmul(psum[0:m, 6, h * KVW + g * HD:h * KVW + (g + 1) * HD],
                                     hid[:, s % 2, h * P:h * P + m], w2[:, 1, :], start=True, stop=True)
            if g == 1:
                last.then_inc(o_made, 1)

        def use(b, kind, u, i):
            t = b * USES + TICKET[kind, u, i]
            pe.wait_ge(b_dve, t + 1)
            x = 0 if kind == "c" else 1
            if kind == "w" and i == 0:
                pe.wait_ge(win_loaded[u], b * 8 + 16)
                pe.wait_ge(win_new[u], b * 8 + 16)
                for n in range(4):
                    last = pe.transpose(psum[:, 7, n * P:(n + 1) * P], wraw[:, u, n, 0:KVW], ident)
            elif (kind, i) == ("w", 1):
                pe.wait_ge(q_staged, b + u + 1)
                last = pe.matmul(psum[0:NH, 7, :], q8[:, u, :], kwT[:, :], start=True, stop=True)
            elif (kind, i) == ("c", 0):
                pe.wait_ge(o_dve, b * 2 + 2 * u + 2)
                last = pe.matmul(psum[0:NH, 7, 0:NCMP], q8[:, u, :], kc[:, 0:NCMP], start=True, stop=True)
            elif (kind, i) in (("w", 2), ("c", 1)):
                pe.wait_ge(prob_made, b * 2 + SOFT[kind, u] + 1)
                for n in range(4 if kind == "w" else 2):
                    m = NCMP - P if kind == "c" and n == 1 else P
                    last = pe.matmul(psum[0:m, 7, n * NH:(n + 1) * NH], sc[:, x, n * P:n * P + m],
                                     ident[0:NH, 0:NH], start=True, stop=True)
            elif kind == "w":
                for g in range(NKV):
                    for n in range(4):
                        last = pe.matmul(psum[0:HD, 7, g * GQ:(g + 1) * GQ],
                                         wraw[:, u, n, KVW + g * HD:KVW + (g + 1) * HD],
                                         pT[:, 1, n * NH + g * GQ:n * NH + (g + 1) * GQ], start=n == 0, stop=n == 3)
            else:
                pe.wait_ge(o_dve, b * 2 + 2 * u + 3)
                for g in range(NKV):
                    for n in range(2):
                        m = P if n == 0 else NCMP - P
                        last = pe.matmul(psum[0:HD, 7, g * GQ:(g + 1) * GQ], vc[0:m, n, g * HD:(g + 1) * HD],
                                         pT[0:m, 0, n * NH + g * GQ:n * NH + (g + 1) * GQ], start=n == 0, stop=n == 1)
            last.then_inc(b_made, 1)

        with pe.Fori(0, DB // 2) as pair:
            b = pair * 2
            transposes(b, 0, range(JP))
            for s in range(8):
                if s < 6:
                    transposes(b, s // 2 + 1, range(4 * (s % 2), 4 * (s % 2) + 4))
                if s:
                    output(b, s - 1)
                hidden(b, s)
                for kind, u, i in PLAN[s]:
                    use(b, kind, u, i)
            output(b, 7)
            for kind, u, i in PLAN[8]:
                use(b, kind, u, i)

        for n in range(4):
            for r in range(2):
                for j in range(JP):
                    last = pe.matmul(psum[:, 4, n * 32:n * 32 + PCMP], w1[:, n // 2, r * JP + j, :],
                                     mid.xTp[:, n, j, r:r + PCMP], start=r + j == 0, stop=r + j == JP)
        last.then_inc(h_made, 1)
        pe.wait_ge(h_act, 4 * DB + 1)
        for g in range(NKV):
            pe.matmul(psum[g * HD:(g + 1) * HD, 6, 0:PCMP], w2[:, 0, :], hid[:, 0, g * 32:g * 32 + PCMP],
                      start=True, stop=True)
            last = pe.matmul(psum[0:PCMP, 6, P + g * HD:P + (g + 1) * HD], hid[:, 0, 64 + g * 32:64 + g * 32 + PCMP],
                             w2[:, 1, :], start=True, stop=True)
        last.then_inc(o_made, 1)

    @block.scalar
    def _(act):
        act.wait_ge(bias_read, 1)

        def rows_in(b, unit, fills):
            for f in fills:
                act.wait_ge(c_made, b * 16 + 8 * unit + f + 1)
                for g in range(NKV):
                    for j in range(2):
                        last = act.copy(cT[j * HD:(j + 1) * HD, unit % 2, g, f, :],
                                        psum[g * HD:(g + 1) * HD, f % 4, j * CHUNKS:(j + 1) * CHUNKS])
                last.then_inc(c_act, 1)

        act.sem_inc(c_act, 1)
        with act.Fori(0, DB // 2) as pair:
            b = pair * 2
            rows_in(b, 0, range(1, JP, 2))
            for s in range(8):
                if s < 6:
                    rows_in(b, s // 2 + 1, range(4 * (s % 2) + 1, 4 * (s % 2) + 4, 2))
                act.wait_ge(h_made, b * 4 + s + 1)
                n = s % 4 // 2
                act.activation(hid[:, s % 2, 0:NCMP], psum[:, 4 + s % 2, 0:NCMP], ACT.Gelu_apprx_tanh,
                               bias=cbias[:, n:n + 1]).then_inc(h_act, 1)
                for kind, u, i in PLAN[s] + (PLAN[8] if s == 7 else []):
                    if (kind, i) in (("c", 0), ("w", 1)):
                        x = 0 if kind == "c" else 1
                        m = NCMP if kind == "c" else WIN
                        act.wait_ge(neg_max, b * 2 + SOFT[kind, u] + 1)
                        act.activation(ex[:, x, 0:m], sc[:, x, 0:m], ACT.Exp, bias=st[:, x, 0:1],
                                       accum_out=st[:, x, 1:2]).then_inc(exp_made, 1)
        act.wait_ge(h_made, 4 * DB + 1)
        own = Own(act, own_act)
        own.did(act.activation(hid[:, 0, 0:64].rearrange("p (g c) -> p g c", c=32)[:, :, 0:PCMP],
                               psum[:, 4, 0:64].rearrange("p (g c) -> p g c", c=32)[:, :, 0:PCMP],
                               ACT.Gelu_apprx_tanh, bias=cbias[:, 0:1]))
        act.activation(hid[:, 0, 64:128].rearrange("p (g c) -> p g c", c=32)[:, :, 0:PCMP],
                       psum[:, 4, 64:128].rearrange("p (g c) -> p g c", c=32)[:, :, 0:PCMP],
                       ACT.Gelu_apprx_tanh, bias=cbias[:, 1:2]).then_inc(h_act, 1)

    @block.vector
    def _(dve):
        own = Own(dve, own_dve)
        dve.wait_ge(bias_made, 1)
        dve.tensor_copy(cbias[:, :], psum[:, 7, 0:2]).then_inc(bias_read, 1)

        def rows_in(b, unit, fills):
            for f in fills:
                dve.wait_ge(c_made, b * 16 + 8 * unit + f + 1)
                for g in range(NKV):
                    for j in range(2):
                        last = dve.tensor_copy(cT[j * HD:(j + 1) * HD, unit % 2, g, f, :],
                                               psum[g * HD:(g + 1) * HD, f % 4, j * CHUNKS:(j + 1) * CHUNKS])
                last.then_inc(c_dve, 1)

        def output(b, s):
            u, n, g = s // 4, s % 4 // 2, s % 2
            if g == 1:
                dve.wait_ge(o_made, b * 2 + 2 * u + n + 1)
                if n == 0:
                    dve.tensor_copy(kc[:, 0:NCMP], psum[:, 6, 0:NCMP]).then_inc(o_dve, 1)
                else:
                    own.did(dve.tensor_copy(vc[:, 0, :], psum[:, 6, 0:KVW]))
                    dve.tensor_copy(vc[0:NCMP - P, 1, :], psum[0:NCMP - P, 6, KVW:2 * KVW]).then_inc(o_dve, 1)

        def use(b, kind, u, i):
            dve.wait_ge(b_made, b * USES + TICKET[kind, u, i] + 1)
            x = 0 if kind == "c" else 1
            if (kind, i) == ("w", 0):
                dve.tensor_copy(kwT[:, :], psum[:, 7, :]).then_inc(b_dve, 1)
            elif (kind, i) in (("c", 0), ("w", 1)):
                m = NCMP if kind == "c" else WIN
                bias = long.b_cs[:, 0:NCMP] if kind == "c" else long.b_win[:, :]
                n = b * 2 + SOFT[kind, u] + 1
                dve.tensor_tensor(sc[:, x, 0:m], psum[0:NH, 7, 0:m], bias, ALU.add).then_inc(b_dve, 1)
                dve.wait_ge(b_dve, b * USES + TICKET[kind, u, i] + 2)
                dve.tensor_reduce(st[:, x, 0:1], sc[:, x, 0:m], AX, ALU.max, negate=True).then_inc(neg_max, 1)
                dve.wait_ge(exp_made, n)
                own.did(dve.reciprocal(st[:, x, 2:3], st[:, x, 1:2]))
                own.settle()
                dve.tensor_scalar(sc[:, x, 0:m], ex[:, x, 0:m], st[:, x, 2:3], None, ALU.mult).then_inc(prob_made, 1)
            elif (kind, i) == ("w", 2):
                dve.tensor_copy(pT[:, 1, 0:4 * NH], psum[:, 7, 0:4 * NH]).then_inc(b_dve, 1)
            elif (kind, i) == ("c", 1):
                own.did(dve.tensor_copy(pT[:, 0, 0:NH], psum[:, 7, 0:NH]))
                dve.tensor_copy(pT[0:NCMP - P, 0, NH:2 * NH], psum[0:NCMP - P, 7, NH:2 * NH]).then_inc(b_dve, 1)
                dve.wait_ge(b_dve, b * USES + TICKET[kind, u, i] + 2)
                own.settle()
                for n in range(2):
                    m = P if n == 0 else NCMP - P
                    own.did(dve.tensor_reduce(long.pgT[0:m, n, ds(b * 2 + 2 * u, 2)],
                                              pT[0:m, 0, n * NH:(n + 1) * NH].rearrange("p (g r) -> p g r", g=NKV),
                                              AX, ALU.add))
            else:
                dve.tensor_copy(long.oT[:, x, ds(b * 8 + 8 * u, 8)], psum[0:HD, 7, 0:NH]).then_inc(b_dve, 1)

        dve.sem_inc(c_dve, 1)
        dve.sem_inc(o_dve, 1)
        dve.sem_inc(b_dve, 1)
        with dve.Fori(0, DB // 2) as pair:
            b = pair * 2
            own.enter(pair, 12)
            rows_in(b, 0, range(0, JP, 2))
            for u in range(2):
                dve.tensor_copy(q8[:, u, :], long.q8[:, ds(b + u, 1), :].rearrange("p a h -> p (a h)")
                                ).then_inc(q_staged, 1)
            for s in range(8):
                if s < 6:
                    rows_in(b, s // 2 + 1, range(4 * (s % 2), 4 * (s % 2) + 4, 2))
                if s:
                    output(b, s - 1)
                for kind, u, i in PLAN[s]:
                    use(b, kind, u, i)
            output(b, 7)
            for kind, u, i in PLAN[8]:
                use(b, kind, u, i)
        own.leave(DB // 2)
        dve.wait_ge(o_made, 2 * DB + 1)
        own.did(dve.tensor_copy(long.kcp[:, :], psum[:, 6, 0:PCMP]))
        own.did(dve.tensor_copy(long.vcp[:, :], psum[0:PCMP, 6, P:2 * P]))


def select(nc, ctx, io, psum, long):
    def sb(name, shape, dt=F32):
        return ctx.enter_context(nc.sbuf_tensor(name, shape, dt))

    def sem(name):
        return ctx.enter_context(nc.semaphore(name))

    R = DB * NKV
    imp = sb("imp", [R, 62])
    rest_ = sb("imp_rest", [R, 62])
    top = sb("top", [R, 2, 8])
    at = sb("at", [R, 2, 8], U32)
    blk_i = sb("blk_i", [R, 16], I32)
    page_i = sb("page_i", [R, 16], I32)
    blk = sb("blk", [R, 16])
    page = sb("page", [R, 16])
    is62 = sb("is62", [R, 16])
    hot = sb("hot", [R, 16, PAGES])
    row = sb("row", [R, 16])
    rowT = sb("rowT", [16, R])
    tab_i = sb("tab_i", [DB, PAGES], I32)
    tab_f = sb("tab_f", [DB, PAGES])
    tabs = sb("tabs", [R, PAGES])
    sel_pair = sb("sel_pair_c", [P, io.cC.shape[1]])
    spread = sb("spread", [P, 8 * R])
    table_loaded, pair_loaded = sem("table_loaded"), sem("pair_loaded")
    made, read = sem("s_made"), sem("s_read")
    own_dve = sem("own_dve_c")
    block = ctx.enter_context(nc.Block())
    c0 = long.c0

    @block.sync
    def _(sp):
        sp.dma_start(tab_i[:, :], io.page_table).then_inc(table_loaded, 16)
        sp.dma_start(sel_pair[:, :], io.cC).then_inc(pair_loaded, 16)

    @block.tensor
    def _(pe):
        for n in range(2):
            m = P if n == 0 else NCMP - P
            last = pe.matmul(psum[0:R, 0, 0:65], long.pgT[0:m, n, :], c0("shared")[0:m, n * 65:(n + 1) * 65],
                             start=n == 0, stop=n == 1)
        last.then_inc(made, 1)
        pe.wait_ge(read, 1)
        pe.matmul(psum[0:R, 1, 0:PAGES], c0("rep_bg", DB), tab_f[:, :], start=True, stop=True).then_inc(made, 1)
        pe.wait_ge(read, 2)
        pe.transpose(psum[0:16, 2, 0:R], row[:, :], c0("ident", R)[:, 0:R])
        for b in range(DB):
            last = pe.matmul(psum[0:NH, 3, b * 16:(b + 1) * 16], c0("sel_b", R)[:, b * NH:(b + 1) * NH],
                             is62[:, :], start=True, stop=True)
        last.then_inc(made, 1)
        pe.wait_ge(read, 3)
        pe.wait_ge(pair_loaded, 16)
        for j in range(8):
            last = pe.matmul(psum[:, 4, j * R:(j + 1) * R], sel_pair[0:16, j * P:(j + 1) * P], rowT[:, :],
                             start=True, stop=True)
        last.then_inc(made, 1)

    @block.vector
    def _(dve):
        own = Own(dve, own_dve)

        def then(instruction):
            own.did(instruction)
            own.settle()

        dve.wait_ge(table_loaded, 16)
        dve.tensor_copy(tab_f[:, :], tab_i[:, :]).then_inc(read, 1)
        dve.wait_ge(made, 1)
        then(dve.tensor_copy(imp[:, :], psum[0:R, 0, 1:63]))
        then(dve.max(top[:, 0, :], imp[:, :]))
        then(dve.max_index(at[:, 0, :], top[:, 0, :], imp[:, :]))
        then(dve.match_replace(rest_[:, :], top[:, 0, :], imp[:, :], NEG))
        then(dve.max(top[:, 1, :], rest_[:, :]))
        then(dve.max_index(at[:, 1, :], top[:, 1, :], rest_[:, :]))
        own.did(dve.tensor_copy(blk_i[:, 0:8], at[:, 0, :]))
        then(dve.tensor_copy(blk_i[:, 8:16], at[:, 1, :]))
        then(dve.tensor_copy(blk[:, :], blk_i[:, :]))
        then(dve.tensor_scalar(blk[:, :], blk[:, :], 1.0, None, ALU.add))
        own.did(dve.memset(blk[:, TOPB:TOPB + 1], 0.0))
        own.did(dve.memset(blk[:, TOPB + 1:TOPB + 2], 63.0))
        then(dve.memset(blk[:, TOPB + 2:TOPB + 3], 0.0))
        then(dve.tensor_copy(blk_i[:, :], blk[:, :]))
        then(dve.tensor_scalar(page_i[:, :], blk_i[:, :], 1, None, ALU.logical_shift_right))
        own.did(dve.tensor_scalar(is62[:, :], blk[:, :], 62.0, None, ALU.is_equal))
        then(dve.tensor_copy(page[:, :], page_i[:, :]))
        then(dve.tensor_tensor(hot[:, :, :], c0("iota", R)[:, 0:PAGES].unsqueeze(1).to_broadcast([R, 16, PAGES]),
                               page[:, :].unsqueeze(2).to_broadcast([R, 16, PAGES]), ALU.is_equal))
        dve.wait_ge(made, 2)
        then(dve.tensor_copy(tabs[:, :], psum[0:R, 1, 0:PAGES]))
        then(dve.tensor_tensor(hot[:, :, :], hot[:, :, :],
                               tabs[:, :].unsqueeze(1).to_broadcast([R, 16, PAGES]), ALU.mult))
        then(dve.tensor_reduce(row[:, :], hot[:, :, :], AX, ALU.add))
        then(dve.tensor_tensor(row[:, :], row[:, :], page[:, :], ALU.subtract))
        then(dve.tensor_scalar(row[:, :], row[:, :], 2.0, None, ALU.mult))
        then(dve.tensor_tensor(row[:, :], row[:, :], blk[:, :], ALU.add))
        dve.tensor_scalar(row[:, :], row[:, :], 2.0 * SLC, None, ALU.mult).then_inc(read, 1)
        dve.wait_ge(made, 3)
        own.did(dve.tensor_copy(long.flag62[:, :, :], psum[0:NH, 3, 0:DB * 16].rearrange("p (b s) -> p b s", s=16)))
        dve.tensor_copy(rowT[:, :], psum[0:16, 2, 0:R]).then_inc(read, 1)
        dve.wait_ge(made, 4)
        then(dve.tensor_copy(spread[:, :], psum[:, 4, 0:8 * R]))
        own.did(dve.tensor_scalar(long.sel_idx[:, :, :].rearrange("p r j -> p j r"),
                                  spread[:, :].rearrange("p (j r) -> p j r", r=R),
                                  c0("pos64"), None, ALU.add))


def attend(nc, ctx, io, psum, long):
    def sb(name, shape, dt=F32):
        return ctx.enter_context(nc.sbuf_tensor(name, shape, dt))

    def sem(name):
        return ctx.enter_context(nc.semaphore(name))

    ITEMS = NKV * QT
    RING = 4
    skew = sb("skew", [P, NH, HW])
    qs = sb("qs", [P, SEQ])
    bs = sb("bs", [P, NKV, 2 * P])
    bc = sb("bc", [P, NKV, QT, PCMP])
    pr = sb("pr", [P, 2, 2, SEQ])
    prT = sb("prT", [P, 2, 2, SEQ])
    pc = sb("pc", [P, ITEMS, 32])
    pcT = sb("pcT", [PCMP, ITEMS, P])
    cst = sb("st_c", [P, 4, ITEMS])
    st = sb("st_p", [P, 4, 2, 4])
    sel = sb("sel", [P, RING, NKV, 8, 2 * KVW])
    sel_stage = sb("sel_stage", [P, RING, NKV * 8], I32)
    apart = sb("apart_d", [P, 1])
    part = sb("part_d", [P, 2, HD])
    ksT = sb("ksT", [P, 2, 1024])
    q8 = sb("q8_d", [P, 2, NH])
    sc = sb("sc_d", [NH, 2, 1024])
    pT = sb("pT_d", [P, 2, 8 * NH])
    ss = sb("ss_d", [NH, 2, 4])
    ident = long.c0("ident")

    skew_loaded = sem("skew_loaded")
    staged_q, staged_b = sem("staged_q"), sem("staged_b")
    s_made, s_max, s_exp = sem("s_scores"), sem("s_max"), sem("s_exp")
    cs_made, cs_shifted, cs_exp, cs_prob = sem("cs_made"), sem("cs_shifted"), sem("cs_exp"), sem("cs_prob")
    ct_made, ct_act, ct_dve = sem("ct_made"), sem("ct_act"), sem("ct_dve")
    t_made, t_act, t_dve = sem("t_made"), sem("t_act"), sem("t_dve")
    o_made, o_read = sem("o_made_d"), sem("o_read_d")
    gathered = [sem(f"sel_gathered{s}") for s in range(RING)]
    fresh_in = [sem(f"sel_fresh{s}") for s in range(RING)]
    staged = sem("sel_staged")
    k_made, k_act, k_dve = sem("k_made"), sem("k_act"), sem("k_dve")
    q_staged = sem("sel_q")
    y_made, y_biased, y_max, y_exp, y_prob = sem("y_made"), sem("y_biased"), sem("y_max"), sem("y_exp"), sem("y_prob")
    p_made, p_read = sem("p_made"), sem("p_read")
    v_made, v_read = sem("v_made"), sem("v_read")
    g_made, g_read = sem("g_made"), sem("g_read")
    own_dve, own_act = sem("own_dve_d"), sem("own_act_d")
    block = ctx.enter_context(nc.Block())

    def item(n):
        return n // QT, n % QT, P * (n % QT + 1)

    @block.sync
    def _(sp):
        hankel = bass.AP(io.vhan.tensor, 0, [[1, P], [HCOLS, NH], [1, HW]])
        sp.dma_start(skew[:, :, :], hankel).then_inc(skew_loaded, 16)
        for b in range(RING):
            for g in range(NKV):
                sp.dma_start(sel[SLC:SLC + 1, b, g, 7, :], io.fresh[b:b + 1, 2 * KVW:4 * KVW]).then_inc(fresh_in[b], 16)
        for b in range(RING, DB):
            sp.wait_ge(v_made, b - RING + 2)
            for g in range(NKV):
                sp.dma_start(sel[SLC:SLC + 1, b - RING, g, 7, :], io.fresh[b:b + 1, 2 * KVW:4 * KVW]
                             ).then_inc(fresh_in[b - RING], 16)

    @block.gpsimd
    def _(pool):
        with pool.Fori(0, DB // RING) as four:
            for s in range(RING):
                pool.wait_ge(v_made, four * (s + 1) + 1)
                pool.tensor_copy(sel_stage[:, s, :], long.sel_idx[:, ds(four * 2 * RING + 2 * s, 2), :].rearrange(
                    "p r j -> p (r j)")).then_inc(staged, 1)
                pool.wait_ge(staged, four * RING + s + 1)
                pool.tensor_tensor(apart[:, 0:1], long.consts[:, 0:1], long.consts[:, 1:2], ALU.add)
                for g in range(NKV):
                    for j in range(8):
                        m = P if j < 7 else SLC
                        pool.indirect_dma_start(
                            sel[0:m, s, g, j, :], None, io.cache_rows,
                            bass.IndirectOffsetOnAxis(ap=sel_stage[0:m, s, g * 8 + j:g * 8 + j + 1], axis=0)
                        ).then_inc(gathered[s], 16)

    @block.tensor
    def _(pe):
        pe.sem_inc(v_made, 1)
        pe.sem_inc(o_made, 1)
        def scores(r, n):
            g, t, w = item(n)
            rows = slice(g * HD, (g + 1) * HD)
            for x in range(2):
                last = pe.matmul(psum[:, 2 * (n % 2) + x, 0:w], qs[rows, t * P:(t + 1) * P],
                                 long.kT[rows, x, 0:w], start=True, stop=True)
            last.then_inc(s_made, 1)

        def compressed_scores(r):
            for n in range(ITEMS):
                g, t, w = item(n)
                rows = slice(g * HD, (g + 1) * HD)
                last = pe.matmul(psum[:, 4 + g, t * 32:t * 32 + PCMP], qs[rows, t * P:(t + 1) * P], long.kcp[rows, :],
                                 start=True, stop=True)
            last.then_inc(cs_made, 1)

        def compressed_transposes(r):
            pe.wait_ge(cs_prob, r + 1)
            for n in range(ITEMS):
                last = pe.matmul(psum[0:PCMP, 4 + n // QT, (n % QT) * P:(n % QT + 1) * P], pc[:, n, 0:PCMP], ident,
                                 start=True, stop=True)
            last.then_inc(ct_made, 1)

        def transposes(r, n):
            g, t, w = item(n)
            if n == 0:
                pe.wait_ge(ct_act, r + 1)
            pe.wait_ge(s_exp, r * ITEMS + n + 1)
            for x in range(2):
                for k in range(t + 1):
                    out, p = psum[:, 5 + x, k * P:(k + 1) * P], pr[:, n % 2, x, k * P:(k + 1) * P]
                    if x == 0 and k == 0:
                        last = pe.matmul(out, p, ident, start=True, stop=True)
                    else:
                        last = pe.transpose(out, p, ident)
            last.then_inc(t_made, 1)

        def values(r, n):
            g, t, w = item(n)
            if n == 0:
                pe.wait_ge(ct_dve, r + 1)
            pe.wait_ge(t_act, r * ITEMS + n + 1)
            pe.wait_ge(t_dve, r * ITEMS + n + 1)
            if n:
                pe.wait_ge(o_read, r * ITEMS + n)
            bank = 4 if n % 2 else 7
            for x in range(2):
                col = (3 + 2 * x) * KVW + g * HD
                for k in range(t + 1):
                    pe.matmul(psum[:, bank, x * HD:(x + 1) * HD], prT[:, n % 2, x, k * P:(k + 1) * P],
                              long.kvtok[:, k, col:col + HD], start=k == 0, stop=k == t)
            pe.matmul(psum[:, bank, 2 * HD:3 * HD], pcT[:, n, :], long.vcp[:, g * HD:(g + 1) * HD],
                      start=True, stop=True).then_inc(o_made, 1)

        with pe.Fori(0, GQ) as r:
            pe.wait_ge(staged_q, r + 1)
            pe.wait_ge(o_read, r * ITEMS + 1)
            compressed_scores(r)
            scores(r, 0)
            scores(r, 1)
            compressed_transposes(r)
            for n in range(ITEMS):
                transposes(r, n)
                if n + 2 < ITEMS:
                    scores(r, n + 2)
                values(r, n)

        def keys(b, s):
            pe.wait_ge(gathered[s % RING], 256 * (b // RING + 1))
            pe.wait_ge(fresh_in[s % RING], 32 * (b // RING + 1))
            for g in range(NKV):
                for h in range(2):
                    k = 2 * b + g
                    if k >= 2:
                        pe.wait_ge(k_act if h else k_dve, k - 1)
                    for j in range(4):
                        m = P if 4 * h + j < 7 else SLC + 1
                        last = pe.transpose(psum[:, 2 * h + g, j * P:j * P + m],
                                            sel[0:m, s % RING, g, 4 * h + j, 0:KVW], ident[0:m, 0:m])
                    last.then_inc(k_made, 1)

        def sample_scores(b):
            pe.wait_ge(k_act, 2 * b + 2)
            pe.wait_ge(k_dve, 2 * b + 2)
            pe.wait_ge(q_staged, b + 1)
            if b:
                pe.wait_ge(y_biased, b)
            pe.matmul(psum[0:NH, 4, :], q8[:, b % 2, :], ksT[:, b % 2, 0:512], start=True, stop=True)
            pe.matmul(psum[0:NH, 5, 0:SELK - 512], q8[:, b % 2, :], ksT[:, b % 2, 512:SELK],
                      start=True, stop=True).then_inc(y_made, 1)

        def sample_values(b):
            pe.wait_ge(y_prob, b + 1)
            if b:
                pe.wait_ge(p_read, b)
            for j in range(8):
                m = P if j < 7 else SLC + 1
                last = pe.transpose(psum[0:m, 6, j * NH:(j + 1) * NH], sc[:, b % 2, j * P:j * P + m], ident[0:NH, 0:NH])
            last.then_inc(p_made, 1)
            pe.wait_ge(p_read, b + 1)
            if b:
                pe.wait_ge(v_read, b)
            for g in range(NKV):
                for j in range(8):
                    m = P if j < 7 else SLC + 1
                    last = pe.matmul(psum[0:HD, 7, g * GQ:(g + 1) * GQ],
                                     sel[0:m, b % RING, g, j, KVW + g * HD:KVW + (g + 1) * HD],
                                     pT[0:m, b % 2, j * NH + g * GQ:j * NH + (g + 1) * GQ], start=j == 0, stop=j == 7)
            last.then_inc(v_made, 1)

        pe.wait_ge(o_read, GQ * ITEMS + 1)
        for b in range(DB + 1):
            if b < DB:
                keys(b, b)
                sample_scores(b)
            if b:
                sample_values(b - 1)
        pe.wait_ge(v_read, DB)
        for x in range(3):
            for h in range(NH):
                last = pe.transpose(psum[0:DB, x, h * HD:(h + 1) * HD], long.oT[:, x, h::NH], ident[0:HD, 0:HD])
        last.then_inc(g_made, 1)

    @block.scalar
    def _(act):
        def exps(r, n):
            g, t, w = item(n)
            act.wait_ge(s_max, r * ITEMS + n + 1)
            for x in range(2):
                last = act.activation(pr[:, n % 2, x, 0:w], psum[:, 2 * (n % 2) + x, 0:w], ACT.Exp,
                                      bias=st[:, n % 4, x, 0:1], accum_out=st[:, n % 4, x, 1:2])
            last.then_inc(s_exp, 1)

        def rows_in(r, n):
            g, t, w = item(n)
            act.wait_ge(t_made, r * ITEMS + n + 1)
            act.copy(prT[:, n % 2, 0, 0:w], psum[:, 5, 0:w]).then_inc(t_act, 1)

        with act.Fori(0, GQ) as r:
            act.wait_ge(o_made, r * ITEMS + 1)
            act.copy(qs[:, :], long.qT[:, ds(r, 1), 0:SEQ].rearrange("p a n -> p (a n)")).then_inc(staged_q, 1)
            act.wait_ge(cs_shifted, r + 1)
            act.activation(pc[:, :, 0:PCMP], pc[:, :, 0:PCMP], ACT.Exp).then_inc(cs_exp, 1)
            exps(r, 0)
            act.wait_ge(ct_made, r + 1)
            act.copy(pcT[:, QT:ITEMS, :].rearrange("p n q -> p (n q)"), psum[0:PCMP, 5, :]).then_inc(ct_act, 1)
            for n in range(ITEMS):
                if n + 1 < ITEMS:
                    exps(r, n + 1)
                rows_in(r, n)

        for b in range(DB + 1):
            if b < DB:
                for g in range(NKV):
                    rows = slice(g * HD, (g + 1) * HD)
                    act.wait_ge(k_made, 4 * b + 2 * g + 2)
                    act.copy(ksT[rows, b % 2, 512:SELK], psum[rows, 2 + g, 0:SELK - 512]).then_inc(k_act, 1)
                act.wait_ge(y_max, b + 1)
                act.activation(sc[:, b % 2, 0:SELK], sc[:, b % 2, 0:SELK], ACT.Exp, bias=ss[:, b % 2, 0:1],
                               accum_out=ss[:, b % 2, 1:2]).then_inc(y_exp, 1)

    @block.vector
    def _(dve):
        own = Own(dve, own_dve)
        dve.sem_inc(o_read, 1)
        dve.wait_ge(skew_loaded, 16)

        def compressed_shift(r):
            dve.wait_ge(cs_made, r + 1)
            c = pc[:, :, 0:PCMP]
            then(dve.tensor_tensor(c.rearrange("p (g t) c -> p g t c", g=NKV),
                                   psum[:, 4:6, 0:QT * 32].rearrange("p g (t c) -> p g t c", c=32)[:, :, :, 0:PCMP],
                                   bc[:, :, :, :], ALU.add))
            then(dve.tensor_reduce(cst[:, 0, :], c, AX, ALU.max, negate=True))
            then(dve.tensor_scalar(cst[:, 0, :], cst[:, 0, :], -0.1 * NEG, None, ALU.min))
            dve.tensor_tensor(c, c, cst[:, 0, :].unsqueeze(2).to_broadcast([P, ITEMS, PCMP]), ALU.add
                              ).then_inc(cs_shifted, 1)

        def compressed_weights(r):
            c = pc[:, :, 0:PCMP]
            dve.wait_ge(cs_exp, r + 1)
            then(dve.tensor_reduce(cst[:, 1, :], c, AX, ALU.add))
            then(dve.tensor_scalar(cst[:, 1, :], cst[:, 1, :], 0.5, None, ALU.max))
            then(dve.reciprocal(cst[:, 2, :], cst[:, 1, :]))
            for g in range(NKV):
                own.did(dve.tensor_tensor(cst[:, 3, g * QT:(g + 1) * QT].unsqueeze(2),
                                          cst[:, 2, g * QT:(g + 1) * QT].unsqueeze(2),
                                          long.gates[:, 0:QT, ds(r * 3 + g * GQ * 3, 1)], ALU.mult))
            own.settle()
            dve.tensor_tensor(c, c, cst[:, 3, :].unsqueeze(2).to_broadcast([P, ITEMS, PCMP]), ALU.mult
                              ).then_inc(cs_prob, 1)

        def compressed_in(r):
            dve.wait_ge(ct_made, r + 1)
            dve.tensor_copy(pcT[:, 0:QT, :].rearrange("p n q -> p (n q)"), psum[0:PCMP, 4, :]).then_inc(ct_dve, 1)

        def biases(r, n):
            g, t, w = item(n)
            banks = psum[:, 2 * (n % 2):2 * (n % 2) + 2, :]
            dve.wait_ge(s_made, r * ITEMS + n + 1)
            v = min(w, 2 * P)
            then(dve.tensor_tensor(banks[:, :, w - v:w], banks[:, :, w - v:w],
                                   bs[:, g, 2 * P - v:2 * P].unsqueeze(1).to_broadcast([P, 2, v]), ALU.add))
            dve.tensor_reduce(st[:, n % 4, :, 0:1], banks[:, :, 0:w], AX, ALU.max, negate=True).then_inc(s_max, 1)

        def rows_in(r, n):
            g, t, w = item(n)
            dve.wait_ge(t_made, r * ITEMS + n + 1)
            dve.tensor_copy(prT[:, n % 2, 1, 0:w], psum[:, 6, 0:w]).then_inc(t_dve, 1)

        def merge(r, n):
            g, t, w = item(n)
            s, k = r * ITEMS + n, n % 4
            dve.wait_ge(s_exp, s + 1)
            then(dve.reciprocal(st[:, k, :, 3:4], st[:, k, :, 1:2]))
            then(dve.tensor_tensor(st[:, k, :, 2:3], st[:, k, :, 3:4],
                                   long.gates[:, t, ds(r * 3 + g * GQ * 3 + 1, 2)].unsqueeze(2), ALU.mult))
            dve.wait_ge(o_made, s + 2)
            out = long.otok[:, t, ds(r * HD + g * GQ * HD, HD)]
            bank = psum[:, 4 if n % 2 else 7, :]
            then(dve.tensor_scalar(part[:, 0, :], bank[:, 0:HD], st[:, k, 0, 2:3], None, ALU.mult))
            then(dve.scalar_tensor_tensor(part[:, 1, :], bank[:, HD:2 * HD], st[:, k, 1, 2:3], part[:, 0, :],
                                          ALU.mult, ALU.add))
            dve.tensor_tensor(out, bank[:, 2 * HD:3 * HD], part[:, 1, :], ALU.add).then_inc(o_read, 1)

        def then(instruction):
            own.did(instruction)
            own.settle()

        with dve.Fori(0, GQ) as r:
            own.enter(r, NKV * (1 + QT) + 3 + 5 + ITEMS * (1 + 4))
            dve.wait_ge(o_read, r * ITEMS + 1)
            for g in range(NKV):
                head = skew[:, ds(r + g * GQ, 1), :].rearrange("p a y -> p (a y)")
                own.did(dve.tensor_copy(bs[:, g, ::-1], head[:, 384:640]))
                for t in range(QT):
                    first = 480 + P * t
                    own.did(dve.tensor_copy(bc[:, g, t, ::-1], head[:, first - 16 * (PCMP - 1):first + 1:16]))
            own.settle()
            compressed_shift(r)
            biases(r, 0)
            compressed_weights(r)
            biases(r, 1)
            compressed_in(r)
            for n in range(ITEMS):
                rows_in(r, n)
                if n + 2 < ITEMS:
                    biases(r, n + 2)
                merge(r, n)
        own.leave(GQ)

        for b in range(DB + 1):
            if b < DB:
                dve.tensor_copy(q8[:, b % 2, :], long.q8[:, b, :]).then_inc(q_staged, 1)
                for g in range(NKV):
                    rows = slice(g * HD, (g + 1) * HD)
                    dve.wait_ge(k_made, 4 * b + 2 * g + 1)
                    dve.tensor_copy(ksT[rows, b % 2, 0:512], psum[rows, g, :]).then_inc(k_dve, 1)
                dve.wait_ge(y_made, b + 1)
                s = sc[:, b % 2, :]
                own.did(dve.tensor_tensor(
                    s[:, 0:1024].rearrange("p (k n) -> p k n", n=SLC),
                    long.flag62[:, b, :].unsqueeze(2).to_broadcast([NH, 16, SLC]),
                    long.b_cs[:, NCMP + SLC:NCMP + 2 * SLC].unsqueeze(1).to_broadcast([NH, 16, SLC]), ALU.mult))
                own.settle()
                own.did(dve.tensor_copy(s[:, 14 * SLC:15 * SLC], long.b_cs[:, NCMP:NCMP + SLC]))
                own.did(dve.tensor_copy(s[:, SELK - 1:SELK], long.b_cs[:, NCMP + 2 * SLC:NCMP + 2 * SLC + 1]))
                own.settle()
                own.did(dve.tensor_tensor(s[:, 0:512], psum[0:NH, 4, :], s[:, 0:512], ALU.add))
                dve.tensor_tensor(s[:, 512:SELK], psum[0:NH, 5, 0:SELK - 512], s[:, 512:SELK], ALU.add
                                  ).then_inc(y_biased, 1)
                own.settle()
                dve.wait_ge(y_biased, b + 1)
                dve.tensor_reduce(ss[:, b % 2, 0:1], s[:, 0:SELK], AX, ALU.max, negate=True).then_inc(y_max, 1)
                dve.wait_ge(y_exp, b + 1)
                own.did(dve.reciprocal(ss[:, b % 2, 2:3], ss[:, b % 2, 1:2]))
                own.settle()
                dve.tensor_scalar(s[:, 0:SELK], s[:, 0:SELK], ss[:, b % 2, 2:3], None, ALU.mult).then_inc(y_prob, 1)
            if b:
                dve.wait_ge(p_made, b)
                c = b - 1
                own.did(dve.tensor_copy(pT[:, c % 2, 0:7 * NH], psum[:, 6, 0:7 * NH]))
                dve.tensor_copy(pT[0:SLC + 1, c % 2, 7 * NH:], psum[0:SLC + 1, 6, 7 * NH:8 * NH]).then_inc(p_read, 1)
                dve.wait_ge(v_made, b + 1)
                dve.tensor_copy(long.oT[:, 2, c * NH:(c + 1) * NH], psum[0:HD, 7, 0:NH]).then_inc(v_read, 1)
        dve.wait_ge(g_made, 1)
        out = long.otok[0:DB, QT, :].rearrange("p (h d) -> p h d", d=HD)
        gates = long.gates[0:DB, QT, :].rearrange("p (h x) -> p h x", x=3)
        tmp = qs[0:DB, :].rearrange("p (h d) -> p h d", d=HD)
        for x, gate in enumerate((0, 2, 1)):
            own.did(dve.tensor_tensor(out if x == 0 else tmp, psum[0:DB, x, :].rearrange("p (h d) -> p h d", d=HD),
                                      gates[:, :, gate:gate + 1].to_broadcast([DB, NH, HD]), ALU.mult))
            own.settle()
            if x:
                own.did(dve.tensor_tensor(out, out, tmp, ALU.add))
                own.settle()


def mix(nc, ctx, io, psum, long):
    def sb(name, shape, dt=F32):
        return ctx.enter_context(nc.sbuf_tensor(name + "_mix", shape, dt))

    def sem(name):
        return ctx.enter_context(nc.semaphore(name + "_mix"))

    LOG = NG + EX
    w_out = sb("w_out", [P, KT, D])
    xa = sb("xa", [P, TT, D])
    zg = sb("zg", [P, CT, TOK])
    zsq = sb("zsq", [P, CT, TOK])
    oT = sb("oT_e", [P, 2, CT, P])
    xT = sb("xT_e", [P, KT, P])
    ln = sb("ln1", [P, 2, D])
    w_r = sb("w_r", [P, KT, LOG])
    w_rg = sb("w_rg_in", [P, KT, NG])
    w_re = sb("w_re_in", [P, KT, EX])
    b_r = sb("b_r", [P, LOG])
    rms = sb("rms", [P, TT, 2])
    stats = sb("stats", [P, 2, 6])
    mv = sb("mv", [P, TT, 4])
    log = sb("log", [P, TT, LOG])
    lg8 = sb("lg8", [P, TT, 8])
    le = sb("le", [P, TT, NE])
    mul_le = sb("mul_le", [P, NE, NG])
    top_g = sb("top_g", [P, TT, 8])
    at_g = sb("at_g", [P, TT, 8], U32)
    top_e = sb("top", [P, TT, 8])
    at_e = sb("at", [P, TT, 8], U32)
    pick = sb("pick", [P, TT, 3])
    hot_g = sb("hot_g", [P, NG])
    hot = sb("hot", [P, TT, 2, EX])
    both = sb("both", [P, TT, EX])
    acc = sb("acc", [P, TT, EX])
    ranks = sb("ranks", [P, TT, 2, EX])
    place = sb("place", [P, 4, TT, 2])
    steps = sb("steps", [P, PASSES - 1])
    over = sb("over", [P, TT * 2, PASSES - 1])
    hot_pos = sb("hot_pos", [P, TT * 2, CAP])
    hot_slot = sb("hot_slot", [P, TT * 2, SLOTS])
    ex = sb("ex", [P, TT, NG + 1])
    share = sb("share", [P, TT, 2])
    junk = sb("junk", [P, TT, DG])
    rms_done = sb("rms_done", [P, 1])
    found = sb("found", [CAP, SLOTS])
    empty = sb("empty", [CAP, SLOTS])
    first = sb("first", [CAP, SLOTS])
    choice = sb("choice", [CAP, SLOTS], I32)
    count = sb("count", [1, EX + PASSES + 2])
    ident = long.c0("ident")
    consts = sb("consts", [P, io.cE.shape[1]])

    def c_e(name):
        at, full = io.where[name]
        return consts[:, at:at + full.shape[1]]

    iota = c_e("slot_iota")

    x_in = [sem(f"x_in{t}") for t in range(TT)]
    wo_z_in, wo_o_in, small_in = sem("wo_z_in"), sem("wo_o_in"), sem("small_in")
    x1_out = sem("x1_out")
    rms_clear, o_squared, z_squared = sem("rms_clear"), sem("o_squared"), sem("z_squared")
    msq, root = sem("msq"), sem("root")
    zg_made, xa_ready = sem("zg_made"), sem("xa_ready")
    ssq_made, ssq_read = sem("ssq_made"), sem("ssq_read")
    ot_made, ot_read = sem("ot_made"), sem("ot_read")
    pz_made, pz_read, po_made, po_read = sem("pz_made"), sem("pz_read"), sem("po_made"), sem("po_read")
    var_made, dev_made, norm_scale, normed = sem("var_made"), sem("dev_made"), sem("norm_scale"), sem("normed")
    x1_made = sem("x1_made")
    xt_made, xt_act, xt_dve = sem("xt_made"), sem("xt_act"), sem("xt_dve")
    log_made, log_read = sem("log_made"), sem("log_read")
    w_r_made = sem("w_r_made")
    hot_made, rank_made, rank_read = sem("hot_made"), sem("rank_made"), sem("rank_read")
    exp_asked, exp_made = sem("exp_asked"), sem("exp_made")
    slot_hot, table_made = sem("slot_hot"), sem("table_made")
    own_dve = sem("own_dve")
    block = ctx.enter_context(nc.Block())

    def rows(t):
        return P if t < QT else DB

    @block.sync
    def _(sp):
        for t in range(TT):
            src = io.x_prompt[0, t * P:(t + 1) * P, :] if t < QT else io.x_sample[:, 0, :]
            sp.dma_start(xa[0:rows(t), t, :], src).then_inc(x_in[t], 16)
        for t in range(TT):
            sp.wait_ge(x1_made, t + 1)
            sp.dma_start(io.x1[t * P:t * P + rows(t), :], xa[0:rows(t), t, :]).then_inc(x1_out, 16)
        sp.wait_ge(x1_out, 16 * TT)

    @block.gpsimd
    def _(pool):
        def everywhere(row):
            return bass.AP(row.tensor, row.offset, [[0, P], [1, row.shape[1]]])

        pool.dma_start(consts[:, :], io.cE).then_inc(small_in, 16)
        w = io.w_out.rearrange("(k p) n -> p k n", p=P)
        for h in range(4):
            k = (2 * h + CT) % KT
            pool.dma_start(w_out[:, k:k + 2, :], w[:, k:k + 2, :]).then_inc(wo_z_in if h < 2 else wo_o_in, 16)
        pool.dma_start(w_rg[:, :, :], io.w_rg.rearrange("(p k) n -> p k n", k=KT)).then_inc(small_in, 16)
        pool.dma_start(w_re[:, :, :], io.w_re.rearrange("(p k) n -> p k n", k=KT)).then_inc(small_in, 16)
        pool.dma_start(b_r[:, 0:NG], everywhere(io.b_rg)).then_inc(small_in, 16)
        pool.dma_start(b_r[:, NG:LOG], everywhere(io.b_re)).then_inc(small_in, 16)
        pool.dma_start(ln[:, 0, :], everywhere(io.ln1_g)).then_inc(small_in, 16)
        pool.dma_start(ln[:, 1, :], everywhere(io.ln1_b)).then_inc(small_in, 16)

    @block.tensor
    def _(pe):
        def turn(t):
            m = rows(t)
            if t:
                pe.wait_ge(ot_read, t)
            for k in range(CT):
                last = pe.transpose(psum[:, 4, k * P:k * P + m], long.otok[0:m, t, k * P:(k + 1) * P], ident[0:m, 0:m])
            last.then_inc(ot_made, 1)

        def product(t, half, x, first, made, read):
            if t:
                pe.wait_ge(read, t)
            for n in range(2):
                for k in range(CT):
                    last = pe.matmul(psum[0:rows(t), 2 * half + n, :], x(k), w_out[:, first + k, n * 512:(n + 1) * 512],
                                     start=k == 0, stop=k == CT - 1)
            last.then_inc(made, 1)

        def transpose_x1(t):
            m = rows(t)
            pe.wait_ge(x1_made, t + 1)
            if t:
                pe.wait_ge(xt_act, t)
                pe.wait_ge(xt_dve, t)
            for k in range(KT):
                last = pe.transpose(psum[:, 6 + k // 4, (k % 4) * P:(k % 4) * P + m], xa[0:m, t, k::KT],
                                    ident[0:m, 0:m])
            last.then_inc(xt_made, 1)

        def logits(t):
            pe.wait_ge(xt_act, t + 1)
            pe.wait_ge(xt_dve, t + 1)
            if t == 0:
                pe.wait_ge(w_r_made, 1)
                pe.wait_ge(ssq_read, 1)
            else:
                pe.wait_ge(log_read, t)
                if t > 1:
                    pe.wait_ge(rank_read, t - 1)
            for k in range(KT):
                last = pe.matmul(psum[0:rows(t), 5, 0:LOG], xT[:, k, 0:rows(t)], w_r[:, k, :],
                                 start=k == 0, stop=k == KT - 1)
            last.then_inc(log_made, 1)

        def rank(t):
            m = rows(t)
            pe.wait_ge(hot_made, t + 1)
            here = psum[0:m, 5, LOG:LOG + EX]
            last = pe.matmul(here, c_e("tri")[0:m, 0:m], both[0:m, t, :], start=True, stop=t == 0)
            if t:
                last = pe.matmul(here, long.c0("ones")[:, 0:m], acc[:, t - 1, :], start=False, stop=True)
            if t == QT:
                last = pe.matmul(psum[0:1, 5, 2 * LOG:2 * LOG + EX], long.c0("ones")[:, 0:1], acc[:, t, :],
                                 start=True, stop=True)
            last.then_inc(rank_made, 1)

        def product_z(t):
            product(t, 1, lambda k: zg[:, k, t * P:t * P + rows(t)], CT, pz_made, pz_read)

        def product_o(t):
            pe.wait_ge(ot_read, t + 1)
            product(t, 0, lambda k: oT[:, t % 2, k, 0:rows(t)], 0, po_made, po_read)

        turn(0)
        pe.wait_ge(zg_made, 1)
        pe.wait_ge(small_in, 112)
        pe.wait_ge(wo_z_in, 32)
        product_z(0)
        pe.wait_ge(z_squared, 1)
        for t in range(TT):
            for k in range(CT):
                last = pe.matmul(psum[0:rows(t), 5, t:t + 1], zsq[:, k, t * P:t * P + rows(t)],
                                 long.c0("ones")[:, 0:1], start=k == 0, stop=k == CT - 1)
        last.then_inc(ssq_made, 1)
        pe.wait_ge(wo_o_in, 32)
        product_o(0)
        for t in range(1, TT):
            turn(t)
            product_z(t)
            if t > 1:
                rank(t - 2)
            transpose_x1(t - 1)
            product_o(t)
            logits(t - 1)
        rank(TT - 2)
        transpose_x1(TT - 1)
        logits(TT - 1)
        rank(TT - 1)
        pe.wait_ge(slot_hot, 1)
        for t in range(TT):
            for k in range(2):
                n = 2 * t + k
                last = pe.matmul(psum[0:CAP, 5, 0:SLOTS], hot_pos[0:rows(t), n, :], hot_slot[0:rows(t), n, :],
                                 start=n == 0, stop=n == 2 * TT - 1)
        last.then_inc(table_made, 1)

    @block.scalar
    def _(act):
        def squares(t):
            m = rows(t)
            return act.activation(junk[0:m, t, :], long.otok[0:m, t, :], ACT.Square, accum_out=rms[0:m, t, 0:1])

        act.activation(zsq[:, :, :], long.zT[:, :, :], ACT.Square).then_inc(z_squared, 1)
        for t in range(TT):
            act.wait_ge(x_in[t], 16)
            act.mul(xa[0:rows(t), t, :], xa[0:rows(t), t, :], ALPHA).then_inc(xa_ready, 1)
            if t == 0:
                act.wait_ge(rms_clear, 1)
                for u in range(TT):
                    last = squares(u)
                last.then_inc(o_squared, 1)
        act.wait_ge(msq, 1)
        act.sqrt(rms[:, :, :], rms[:, :, :]).then_inc(root, 1)
        for t in range(TT):
            m = rows(t)
            act.wait_ge(var_made, t + 1)
            act.sqrt(mv[0:m, t, 2:3], mv[0:m, t, 2:3]).then_inc(dev_made, 1)
            act.wait_ge(norm_scale, t + 1)
            act.activation(xa[0:m, t, :], xa[0:m, t, :], ACT.Identity, bias=mv[0:m, t, 3:4],
                           scale=mv[0:m, t, 2:3]).then_inc(normed, 1)
            act.wait_ge(xt_made, t + 1)
            if t:
                act.wait_ge(log_made, t)
            act.copy(xT[:, 0:4, 0:m], psum[:, 6, :].rearrange("p (k n) -> p k n", n=P)[:, :, 0:m]).then_inc(xt_act, 1)
        act.wait_ge(exp_asked, 1)
        act.activation(ex[:, :, :], ex[:, :, :], ACT.Exp).then_inc(exp_made, 1)

    @block.vector
    def _(dve):
        own = Own(dve, own_dve)

        def then(instruction):
            own.did(instruction)
            own.settle()

        def gains(half, n):
            return long.gains[:, half * CT:(half + 1) * CT].unsqueeze(2).to_broadcast([P, CT, n])

        def scale_o(t):
            m = rows(t)
            dve.wait_ge(ot_made, t + 1)
            if t > 1:
                dve.wait_ge(po_made, t - 1)
            dve.tensor_tensor(oT[:, t % 2, :, 0:m], psum[:, 4, :].rearrange("p (k n) -> p k n", n=P)[:, :, 0:m],
                              gains(0, m), ALU.mult).then_inc(ot_read, 1)

        def transposed(t):
            dve.wait_ge(xt_made, t + 1)
            if t:
                dve.wait_ge(log_made, t)
            dve.tensor_copy(xT[:, 4:8, 0:rows(t)], psum[:, 7, :].rearrange("p (k n) -> p k n", n=P)[:, :, 0:rows(t)]
                            ).then_inc(xt_dve, 1)

        def route(t):
            m = rows(t)
            dve.wait_ge(log_made, t + 1)
            dve.tensor_tensor(log[0:m, t, :], psum[0:m, 5, 0:LOG], b_r[0:m, :], ALU.add).then_inc(log_read, 1)
            dve.wait_ge(log_read, t + 1)
            then(dve.tensor_copy(lg8[0:m, t, 0:NG], log[0:m, t, 0:NG]))
            then(dve.max(top_g[0:m, t, :], lg8[0:m, t, :]))
            then(dve.max_index(at_g[0:m, t, :], top_g[0:m, t, :], lg8[0:m, t, :]))
            then(dve.tensor_copy(pick[0:m, t, 0:1], at_g[0:m, t, 0:1]))
            then(dve.tensor_scalar(hot_g[0:m, :], iota[0:m, 0:NG], pick[0:m, t, 0:1], None, ALU.is_equal))
            then(dve.tensor_tensor(mul_le[0:m, :, :],
                                   log[0:m, t, NG:LOG].rearrange("p (g e) -> p e g", e=NE),
                                   hot_g[0:m, :].unsqueeze(1).to_broadcast([m, NE, NG]), ALU.mult))
            then(dve.tensor_reduce(le[0:m, t, :], mul_le[0:m, :, :], AX, ALU.add))
            then(dve.max(top_e[0:m, t, :], le[0:m, t, :]))
            then(dve.max_index(at_e[0:m, t, :], top_e[0:m, t, :], le[0:m, t, :]))
            then(dve.tensor_copy(pick[0:m, t, 1:3], at_e[0:m, t, 0:2]))
            then(dve.scalar_tensor_tensor(pick[0:m, t, 1:3], pick[0:m, t, 0:1].to_broadcast([m, 2]), float(NE),
                                          pick[0:m, t, 1:3], ALU.mult, ALU.add))
            then(dve.tensor_tensor(hot[0:m, t, :, :], iota[0:m, 0:EX].unsqueeze(1).to_broadcast([m, 2, EX]),
                                   pick[0:m, t, 1:3].unsqueeze(2).to_broadcast([m, 2, EX]), ALU.is_equal))
            then(dve.tensor_tensor(both[0:m, t, :], hot[0:m, t, 0, :], hot[0:m, t, 1, :], ALU.add))
            if t == 0:
                dve.tensor_copy(acc[:, t, :], both[:, t, :]).then_inc(hot_made, 1)
            else:
                dve.tensor_tensor(acc[:, t, :], acc[:, t - 1, :], both[:, t, :], ALU.add).then_inc(hot_made, 1)

        def ranked(t):
            m = rows(t)
            dve.wait_ge(rank_made, t + 1)
            if t == QT:
                own.did(dve.tensor_copy(count[:, 0:EX], psum[0:1, 5, 2 * LOG:2 * LOG + EX]))
            dve.tensor_tensor(ranks[0:m, t, :, :], hot[0:m, t, :, :],
                              psum[0:m, 5, LOG:LOG + EX].unsqueeze(1).to_broadcast([m, 2, EX]),
                              ALU.mult).then_inc(rank_read, 1)

        own.did(dve.memset(rms[:, :, :], 1.0 * DG))
        for part in (log, top_g, top_e, pick, hot, both, ranks):
            last = dve.memset(part[:, QT:TT], 0.0)
            own.did(last)
        then(dve.memset(lg8[:, :, :], NEG))
        dve.tensor_copy(rms_done[:, :], rms[:, 0, 0:1]).then_inc(rms_clear, 1)
        dve.tensor_tensor(zg[:, :, :], long.zT[:, :, :], gains(1, TOK), ALU.mult).then_inc(zg_made, 1)
        scale_o(0)
        dve.wait_ge(small_in, 112)
        own.did(dve.tensor_copy(w_r[:, :, 0:NG], w_rg[:, :, :]))
        dve.tensor_copy(w_r[:, :, NG:LOG], w_re[:, :, :]).then_inc(w_r_made, 1)
        dve.wait_ge(ssq_made, 1)
        own.did(dve.tensor_copy(rms[:, 0:QT, 1:2], psum[:, 5, 0:QT].unsqueeze(2)))
        dve.tensor_copy(rms[0:DB, QT, 1:2], psum[0:DB, 5, QT:TT]).then_inc(ssq_read, 1)
        dve.wait_ge(ssq_read, 1)
        dve.wait_ge(o_squared, 1)
        dve.tensor_scalar(rms[:, :, :], rms[:, :, :], 1.0 / DG, 1e-6, ALU.mult, ALU.add).then_inc(msq, 1)
        dve.wait_ge(root, 1)
        then(dve.reciprocal(rms[:, :, :], rms[:, :, :]))
        for t in range(TT):
            m = rows(t)
            x = xa[0:m, t, :].rearrange("p (h n) -> p h n", h=2)
            dve.wait_ge(xa_ready, t + 1)
            dve.wait_ge(pz_made, t + 1)
            dve.scalar_tensor_tensor(x, psum[0:m, 2:4, :], rms[0:m, t, 1:2], x, ALU.mult, ALU.add).then_inc(pz_read, 1)
            if t > 1:
                ranked(t - 2)
            if t:
                transposed(t - 1)
            dve.wait_ge(pz_read, t + 1)
            dve.wait_ge(po_made, t + 1)
            dve.scalar_tensor_tensor(x, psum[0:m, 0:2, :], rms[0:m, t, 0:1], x, ALU.mult, ALU.add).then_inc(po_read, 1)
            dve.wait_ge(po_read, t + 1)
            for h in range(2):
                own.did(dve.bn_stats(stats[0:m, h, :], xa[0:m, t, h * 512:(h + 1) * 512]))
            own.settle()
            then(dve.bn_aggr(mv[0:m, t, 0:2], stats[0:m, :, :]))
            dve.tensor_scalar(mv[0:m, t, 2:3], mv[0:m, t, 1:2], 1e-5, None, ALU.add).then_inc(var_made, 1)
            if t + 1 < TT:
                scale_o(t + 1)
            dve.wait_ge(dev_made, t + 1)
            then(dve.reciprocal(mv[0:m, t, 2:3], mv[0:m, t, 2:3]))
            dve.scalar_tensor_tensor(mv[0:m, t, 3:4], mv[0:m, t, 0:1], -1.0, mv[0:m, t, 2:3],
                                     ALU.mult, ALU.mult).then_inc(norm_scale, 1)
            if t:
                route(t - 1)
            dve.wait_ge(normed, t + 1)
            then(dve.tensor_tensor(xa[0:m, t, :], xa[0:m, t, :], ln[0:m, 0, :], ALU.mult))
            dve.tensor_tensor(xa[0:m, t, :], xa[0:m, t, :], ln[0:m, 1, :], ALU.add).then_inc(x1_made, 1)
        ranked(TT - 2)
        transposed(TT - 1)
        route(TT - 1)
        ranked(TT - 1)
        dve.wait_ge(rank_read, TT)
        rank_, pass_, pos = (place[:, i, :, :].rearrange("p t k -> p (t k)") for i in range(3))
        expert = pick[:, :, 1:3]
        own.did(dve.tensor_scalar(steps[:, :], iota[:, 1:PASSES], float(CAP), None, ALU.mult))
        own.did(dve.tensor_reduce(place[:, 0, :, :], ranks[:, :, :, :], AX, ALU.add))
        own.settle()
        then(dve.tensor_tensor(over[:, :, :], rank_.unsqueeze(2).to_broadcast([P, 2 * TT, PASSES - 1]),
                               steps[:, :].unsqueeze(1).to_broadcast([P, 2 * TT, PASSES - 1]), ALU.is_ge))
        then(dve.tensor_reduce(pass_, over[:, :, :], AX, ALU.add))
        own.did(dve.scalar_tensor_tensor(pos, pass_, -float(CAP), rank_, ALU.mult, ALU.add))
        own.did(dve.scalar_tensor_tensor(place[:, 3, :, :], place[:, 1, :, :], float(EX), expert, ALU.mult, ALU.add))
        own.settle()
        for t in range(TT):
            for k in range(2):
                own.did(dve.tensor_scalar(hot_slot[:, 2 * t + k, :], iota, place[:, 3, t, k:k + 1],
                                          c_e("choice")[:, 2 * t + k:2 * t + k + 1],
                                          ALU.is_equal, ALU.mult))
        own.settle()
        dve.tensor_tensor(hot_pos[:, :, :], iota[:, 0:CAP].unsqueeze(1).to_broadcast([P, 2 * TT, CAP]),
                          pos.unsqueeze(2).to_broadcast([P, 2 * TT, CAP]), ALU.is_equal).then_inc(slot_hot, 1)
        then(dve.tensor_reduce(count[:, EX:EX + 1], count[:, 0:EX], AX, ALU.max))
        then(dve.tensor_scalar(count[:, EX + 2:EX + 1 + PASSES], steps[0:1, :], count[:, EX:EX + 1], None, ALU.is_lt))
        then(dve.tensor_reduce(count[:, EX + 1:EX + 2], count[:, EX + 2:EX + 1 + PASSES], AX, ALU.add))
        own.did(dve.tensor_scalar(long.passes[:, 0:1], count[:, EX + 1:EX + 2], 1.0, None, ALU.add))
        own.did(dve.tensor_scalar(long.passes[:, 1:2], count[:, EX + 1:EX + 2], 1.0, float(EX // 4), ALU.add, ALU.mult))
        own.did(dve.tensor_tensor(ex[:, :, 0:NG], log[:, :, 0:NG], top_g[:, :, 0:1].to_broadcast([P, TT, NG]),
                                  ALU.subtract))
        dve.tensor_tensor(ex[:, :, NG:NG + 1], top_e[:, :, 1:2], top_e[:, :, 0:1], ALU.subtract).then_inc(exp_asked, 1)
        dve.wait_ge(table_made, 1)
        then(dve.tensor_copy(found[:, :], psum[0:CAP, 5, 0:SLOTS]))
        own.did(dve.tensor_scalar(empty[:, :], found[:, :], 0.0, c_e("spare")[0:CAP, :], ALU.is_equal, ALU.mult))
        own.did(dve.tensor_scalar(first[:, :], found[:, :], 1.0, 1.0, ALU.max, ALU.subtract))
        own.settle()
        own.did(dve.scalar_tensor_tensor(long.dest[:, :], found[:, :], 1.0, empty[:, :], ALU.subtract, ALU.add))
        then(dve.tensor_copy(choice[:, :], first[:, :]))
        own.did(dve.tensor_scalar(long.table[:, 0:SLOTS], choice[:, :], 1, None, ALU.logical_shift_right))
        own.did(dve.memset(long.table[:, SLOTS:], 0))
        dve.wait_ge(exp_made, 1)
        own.did(dve.tensor_reduce(share[:, :, 0:1], ex[:, :, 0:NG], AX, ALU.add))
        own.did(dve.tensor_scalar(share[:, :, 1:2], ex[:, :, NG:NG + 1], 1.0, None, ALU.add))
        own.settle()
        then(dve.tensor_tensor(share[:, :, 0:1], share[:, :, 0:1], share[:, :, 1:2], ALU.mult))
        then(dve.reciprocal(long.weights[:, :, 0:1], share[:, :, 0:1]))
        then(dve.tensor_tensor(long.weights[:, :, 1:2], long.weights[:, :, 0:1], ex[:, :, NG:NG + 1], ALU.mult))


def experts(nc, io, psum, long):
    with ExitStack() as ctx:
        def sb(name, shape, dt=F32):
            return ctx.enter_context(nc.sbuf_tensor(name + "_exp", shape, dt))

        def sem(name):
            return ctx.enter_context(nc.semaphore(name + "_exp"))

        RING = 4
        TURNS = EX // RING
        FT = FF // P
        wg = sb("wg", [P, RING, KT, FF])
        wu = sb("wu", [P, RING, KT, FF])
        wd = sb("wd", [P, RING, FT, D])
        x = sb("x", [CAP, RING, D])
        stage = sb("stage", [CAP, RING], I32)
        to = sb("to", [CAP, RING], I32)
        apart = sb("apart", [P, 2 + RING])
        xT = sb("xT", [P, KT, CAP])
        sg = sb("sg", [P, FT * CAP])
        gs = sb("gs", [P, FT * CAP])
        hT = sb("hT", [P, FT, CAP])
        y = sb("y", [CAP, RING, D])
        ident = long.c0("ident")[0:CAP, 0:CAP]
        half = KT // 2 * CAP

        w_in = [sem(f"w_in{s}") for s in range(RING)]
        x_in = [sem(f"x_in{s}") for s in range(RING)]
        staged, to_staged = sem("staged"), sem("to_staged")
        t_made = [sem(f"t_made{s}") for s in range(RING)]
        xt_act, xt_dve = sem("xt_act"), sem("xt_dve")
        gu_made, sg_made, gs_made, h_made = sem("gu_made"), sem("sg_made"), sem("gs_made"), sem("h_made")
        y_made = [sem(f"y_made{s}") for s in range(RING)]
        y_act, y_dve = sem("y_act"), sem("y_dve")
        y_free = sem("y_free")
        y_out = [sem(f"y_out{s}") for s in range(RING)]
        block = ctx.enter_context(nc.Block())

        @block.sync
        def _(sp):
            passes = sp.value_load(long.passes[0:1, 0:1], min_val=1, max_val=PASSES)
            with sp.Fori(0, passes) as p:
                with sp.Fori(0, TURNS) as turn:
                    for s in range(RING):
                        sp.wait_ge(y_made[s], p * TURNS + turn + 1)
                        e = turn * RING + s
                        sp.dma_start(wg[:, s, :, :], io.w_eg[ds(e, 1), :, :].rearrange("a (p k) f -> p (a k) f", k=KT)
                                     ).then_inc(w_in[s], 16)
                        sp.dma_start(wu[:, s, :, :], io.w_eu[ds(e, 1), :, :].rearrange("a (p k) f -> p (a k) f", k=KT)
                                     ).then_inc(w_in[s], 16)
                        sp.dma_start(wd[:, s, :, :], io.w_ed[ds(e, 1), :, :].rearrange("a (p j) n -> p (a j) n", j=FT)
                                     ).then_inc(w_in[s], 16)

        @block.gpsimd
        def _(pool):
            turns = pool.value_load(long.passes[0:1, 1:2], min_val=TURNS, max_val=PASSES * TURNS)

            def fetch(s):
                pool.indirect_dma_start(x[:, s, :], None, io.x1,
                                        bass.IndirectOffsetOnAxis(ap=stage[:, s:s + 1], axis=0)).then_inc(x_in[s], 16)

            pool.tensor_copy(stage[:, 0:1], long.table[:, 0:1]).then_inc(staged, 1)
            pool.tensor_copy(stage[:, 1:2], long.table[:, 1:2]).then_inc(staged, 1)
            pool.tensor_copy(stage[:, 2:3], long.table[:, 2:3]).then_inc(staged, 1)
            pool.sem_inc(y_free, 1)
            pool.wait_ge(staged, 3)
            fetch(0)
            fetch(1)
            fetch(2)
            with pool.Fori(0, turns) as turn:
                for u in range(RING):
                    s = (u + 3) % RING
                    pool.wait_ge(t_made[s], turn + (u + 3) // RING + 1)
                    pool.tensor_copy(stage[:, s:s + 1], long.table[:, ds(turn * RING + u + 3, 1)]).then_inc(staged, 1)
                    pool.wait_ge(staged, turn * RING + u + 4)
                    pool.tensor_tensor(apart[:, 0:1], long.consts[:, 0:1], long.consts[:, 1:2], ALU.add)
                    fetch(s)
                    n = turn * RING + u
                    pool.tensor_copy(to[:, u:u + 1], long.dest[:, ds(n, 1)]).then_inc(to_staged, 1)
                    pool.wait_ge(to_staged, n + 1)
                    if u:
                        pool.wait_ge(y_out[u - 1], turn * 16 + 16)
                    pool.wait_ge(y_act, n + 2)
                    pool.wait_ge(y_dve, n + 2)
                    pool.tensor_tensor(apart[:, 1:2], long.consts[:, 0:1], long.consts[:, 1:2], ALU.add)
                    pool.indirect_dma_start(io.yrows, bass.IndirectOffsetOnAxis(ap=to[:, u:u + 1], axis=0),
                                            y[:, u, :], None).then_inc(y_out[u], 16)
                pool.wait_ge(y_out[RING - 1], turn * 16 + 16)
                pool.tensor_tensor(apart[:, 2:3], long.consts[:, 0:1], long.consts[:, 1:2], ALU.add).then_inc(y_free, 1)

        @block.tensor
        def _(pe):
            turns = pe.value_load(long.passes[0:1, 1:2], min_val=TURNS, max_val=PASSES * TURNS)

            def turned(s, fills, before):
                pe.wait_ge(x_in[s], fills * 16)
                pe.wait_ge(xt_act, before)
                pe.wait_ge(xt_dve, before)
                for k in range(KT):
                    bank, col = k // 4, (k % 4) * CAP
                    last = pe.matmul(psum[:, bank, col:col + CAP], x[:, s, k::KT], ident, start=True, stop=True)
                last.then_inc(t_made[s], 1)

            for s in range(RING):
                pe.sem_inc(y_made[s], 1)
                pe.sem_inc(t_made[s], 1)
            pe.wait_ge(x_in[0], 16)
            for k in range(KT):
                last = pe.matmul(psum[:, k // 4, (k % 4) * CAP:(k % 4 + 1) * CAP], x[:, 0, k::KT], ident,
                                 start=True, stop=True)
            last.then_inc(t_made[0], 1)
            with pe.Fori(0, turns) as turn:
                for s in range(RING):
                    n = turn * RING + s
                    pe.wait_ge(xt_act, n + 1)
                    pe.wait_ge(xt_dve, n + 1)
                    pe.wait_ge(w_in[s], (turn + 1) * 48)
                    for bank, w in ((2, wg), (3, wu)):
                        for j in range(FT):
                            for k in range(KT):
                                last = pe.matmul(psum[:, bank, j * CAP:(j + 1) * CAP], w[:, s, k, j::FT], xT[:, k, :],
                                                 start=k == 0, stop=k == KT - 1)
                    last.then_inc(gu_made, 1)
                    turned((s + 1) % RING, turn + 1 + (s + 1) // RING, n + 1)
                    pe.wait_ge(h_made, n + 1)
                    pe.wait_ge(y_act, n + 1)
                    pe.wait_ge(y_dve, n + 1)
                    for i in range(2):
                        for j in range(FT):
                            last = pe.matmul(psum[0:CAP, 6 + i, :], hT[:, j, :], wd[:, s, j, i * 512:(i + 1) * 512],
                                             start=j == 0, stop=j == FT - 1)
                    last.then_inc(y_made[s], 1)

        @block.scalar
        def _(act):
            turns = act.value_load(long.passes[0:1, 1:2], min_val=TURNS, max_val=PASSES * TURNS)

            def rows_in():
                act.copy(xT[:, 0:KT // 2, :].rearrange("p k n -> p (k n)"), psum[:, 0, 0:half]).then_inc(xt_act, 1)

            act.sem_inc(y_act, 1)
            act.wait_ge(t_made[0], 2)
            rows_in()
            with act.Fori(0, turns) as turn:
                for s in range(RING):
                    n = turn * RING + s
                    act.wait_ge(gu_made, n + 1)
                    act.activation(sg[:, :], psum[:, 2, 0:FT * CAP], ACT.Sigmoid).then_inc(sg_made, 1)
                    act.wait_ge(t_made[(s + 1) % RING], turn + 1 + (s + 1) // RING + 1)
                    rows_in()
                    act.wait_ge(y_made[s], turn + 2)
                    act.wait_ge(y_free, turn + 1)
                    act.copy(y[:, s, 0:512], psum[0:CAP, 6, :]).then_inc(y_act, 1)
        @block.vector
        def _(dve):
            turns = dve.value_load(long.passes[0:1, 1:2], min_val=TURNS, max_val=PASSES * TURNS)

            def rows_in():
                dve.tensor_copy(xT[:, KT // 2:KT, :].rearrange("p k n -> p (k n)"), psum[:, 1, 0:half]
                                ).then_inc(xt_dve, 1)

            dve.sem_inc(y_dve, 1)
            dve.wait_ge(t_made[0], 2)
            rows_in()
            with dve.Fori(0, turns) as turn:
                for s in range(RING):
                    n = turn * RING + s
                    dve.wait_ge(sg_made, n + 1)
                    dve.tensor_tensor(gs[:, :], psum[:, 2, 0:FT * CAP], sg[:, :], ALU.mult).then_inc(gs_made, 1)
                    dve.wait_ge(gs_made, n + 1)
                    dve.tensor_tensor(hT[:, :, :].rearrange("p j n -> p (j n)"), gs[:, :], psum[:, 3, 0:FT * CAP],
                                      ALU.mult).then_inc(h_made, 1)
                    dve.wait_ge(t_made[(s + 1) % RING], turn + 1 + (s + 1) // RING + 1)
                    rows_in()
                    dve.wait_ge(y_made[s], turn + 2)
                    dve.wait_ge(y_free, turn + 1)
                    dve.tensor_copy(y[:, s, 512:1024], psum[0:CAP, 7, :]).then_inc(y_dve, 1)


def finish(nc, io, psum, long):
    with ExitStack() as ctx:
        def sb(name, shape, dt=F32):
            return ctx.enter_context(nc.sbuf_tensor(name + "_fin", shape, dt))

        def sem(name):
            return ctx.enter_context(nc.semaphore(name + "_fin"))

        x = sb("x", [P, TT, D])
        y = sb("y", [P, TT, 2, D])
        ln = sb("ln2", [P, 2, D])
        stats = sb("stats", [P, 2, 6])
        mv = sb("mv", [P, TT, 4])
        ln_in = sem("ln_in")
        x_in = [sem(f"x_in{t}") for t in range(TT)]
        y_in = [sem(f"y_in{t}") for t in range(TT)]
        xa_ready, var_made, dev_made = sem("xa_ready"), sem("var_made"), sem("dev_made")
        norm_scale, normed, out_made, out_done = sem("norm_scale"), sem("normed"), sem("out_made"), sem("out_done")
        own_dve = sem("own_dve")
        block = ctx.enter_context(nc.Block())

        def rows(t):
            return P if t < QT else DB

        @block.sync
        def _(sp):
            def everywhere(row):
                return bass.AP(row.tensor, row.offset, [[0, P], [1, row.shape[1]]])

            rows_of = io.yrows[0:2 * TOK, :].rearrange("(t k) n -> t k n", k=2)
            for t in range(TT):
                sp.dma_start(x[0:rows(t), t, :], io.x1[t * P:t * P + rows(t), :]).then_inc(x_in[t], 16)
                sp.dma_start(y[0:rows(t), t, :, :], rows_of[t * P:t * P + rows(t), :, :]).then_inc(y_in[t], 16)
            sp.dma_start(ln[:, 0, :], everywhere(io.ln2_g)).then_inc(ln_in, 16)
            sp.dma_start(ln[:, 1, :], everywhere(io.ln2_b)).then_inc(ln_in, 16)
            for t in range(TT):
                sp.wait_ge(out_made, t + 1)
                out = io.y_prompt[t * P:(t + 1) * P, :] if t < QT else io.y_sample
                sp.dma_start(out, x[0:rows(t), t, :]).then_inc(out_done, 16)
            sp.wait_ge(out_done, 16 * TT)

        @block.scalar
        def _(act):
            for t in range(TT):
                act.wait_ge(x_in[t], 16)
                act.mul(x[0:rows(t), t, :], x[0:rows(t), t, :], ALPHA).then_inc(xa_ready, 1)
            for t in range(TT):
                m = rows(t)
                act.wait_ge(var_made, t + 1)
                act.sqrt(mv[0:m, t, 2:3], mv[0:m, t, 2:3]).then_inc(dev_made, 1)
                act.wait_ge(norm_scale, t + 1)
                act.activation(x[0:m, t, :], x[0:m, t, :], ACT.Identity, bias=mv[0:m, t, 3:4],
                               scale=mv[0:m, t, 2:3]).then_inc(normed, 1)

        @block.vector
        def _(dve):
            own = Own(dve, own_dve)

            def then(instruction):
                own.did(instruction)
                own.settle()

            def gains(t):
                m = rows(t)
                dve.wait_ge(normed, t + 1)
                then(dve.tensor_tensor(x[0:m, t, :], x[0:m, t, :], ln[0:m, 0, :], ALU.mult))
                dve.tensor_tensor(x[0:m, t, :], x[0:m, t, :], ln[0:m, 1, :], ALU.add).then_inc(out_made, 1)

            dve.wait_ge(ln_in, 32)
            for t in range(TT):
                m = rows(t)
                dve.wait_ge(xa_ready, t + 1)
                dve.wait_ge(y_in[t], 16)
                for k in range(2):
                    then(dve.scalar_tensor_tensor(x[0:m, t, :], y[0:m, t, k, :], long.weights[0:m, t, k:k + 1],
                                                  x[0:m, t, :], ALU.mult, ALU.add))
                for h in range(2):
                    own.did(dve.bn_stats(stats[0:m, h, :], x[0:m, t, h * 512:(h + 1) * 512]))
                own.settle()
                then(dve.bn_aggr(mv[0:m, t, 0:2], stats[0:m, :, :]))
                dve.tensor_scalar(mv[0:m, t, 2:3], mv[0:m, t, 1:2], 1e-5, None, ALU.add).then_inc(var_made, 1)
                if t:
                    gains(t - 1)
                dve.wait_ge(dev_made, t + 1)
                then(dve.reciprocal(mv[0:m, t, 2:3], mv[0:m, t, 2:3]))
                dve.scalar_tensor_tensor(mv[0:m, t, 3:4], mv[0:m, t, 0:1], -1.0, mv[0:m, t, 2:3],
                                         ALU.mult, ALU.mult).then_inc(norm_scale, 1)
            gains(TT - 1)


def rest(nc, whole, attention, io, psum, long, upto):
    def sb(stack, name, shape, dt=F32):
        return stack.enter_context(nc.sbuf_tensor(name, shape, dt))

    with attention:
        long.otok = sb(attention, "otok", [P, TT, DG])
        long.sel_idx = sb(attention, "sel_idx", [P, DB * NKV, 8], I32)
        long.flag62 = sb(attention, "flag62", [NH, DB, 16])
        with ExitStack() as stage:
            select(nc, stage, io, psum, long)
        if upto > 3:
            with ExitStack() as stage:
                attend(nc, stage, io, psum, long)
        if upto > 4:
            with ExitStack() as stage:
                mix(nc, stage, io, psum, long)
    used = sorted(nc.released_uncleared_semaphores)
    assert used == list(range(used[0], used[-1] + 1))
    with nc.Block() as block:
        @block.gpsimd
        def _(pool):
            pool.sem_clear(range(used[0], used[-1] + 1))
    if upto > 5:
        experts(nc, io, psum, long)
    if upto > 6:
        finish(nc, io, psum, long)


def hybrid_layer(nc, io, upto):
    with ExitStack() as whole:
        def sb(stack, name, shape, dt=F32):
            return stack.enter_context(nc.sbuf_tensor(name, shape, dt))

        psum = whole.enter_context(nc.psum_tensor("psum", [P, 8, 512], F32))
        long, mid = Store(), Store()
        long.consts = sb(whole, "consts", [P, io.c0.shape[1]])
        long.zT = sb(whole, "zT", [P, CT, TOK])
        long.gains = sb(whole, "gains", [P, 2 * CT])
        long.gates = sb(whole, "gates", [P, TT, GATES])

        long.table = sb(whole, "table", [CAP, SLOTS + 3], I32)
        long.dest = sb(whole, "dest", [CAP, SLOTS], I32)
        long.weights = sb(whole, "weights", [P, TT, 2])
        long.passes = sb(whole, "passes", [1, 2], I32)

        def c0(name, rows=P):
            at, full = io.where[name]
            return long.consts[0:rows, at:at + full.shape[1]]

        long.c0 = c0
        with ExitStack() as attention:
            long.qT = sb(attention, "qT", [P, GQ, TOK])
            long.kT = sb(attention, "kT", [P, 2, TOK])
            long.kvtok = sb(attention, "kvtok", [P, TT, 6 * KVW])
            long.q8 = sb(attention, "q8", [P, DB, NH])
            long.b_win = sb(attention, "b_win", [NH, WIN])
            long.b_cs = sb(attention, "b_cs", [NH, NCMP + 129])
            long.pgT = sb(attention, "pgT", [P, 2, 16])
            long.oT = sb(attention, "oT", [HD, 3, DB * NH])
            long.kcp = sb(attention, "kcp", [P, PCMP])
            long.vcp = sb(attention, "vcp", [PCMP, KVW])
            with ExitStack() as cache:
                mid.raw = sb(cache, "raw", [P, 4, STRIDE, 2 * KVW])
                mid.stage = sb(cache, "stage", [P, 4, STRIDE], I32)
                mid.idx = sb(cache, "idx", [P, 16, STRIDE], I32)
                mid.apart = sb(cache, "apart", [P, 1])
                mid.pages = sb(cache, "pages", [P, 16])
                mid.xTp = sb(cache, "xTp", [P, 4, JP, PCH])
                mid.peT = sb(cache, "peT", [P, 2 * NJ])
                mid.pe_in = sb(cache, "pe_in", [16, 2, P])
                mid.gathered = [cache.enter_context(nc.semaphore(f"gathered{s}")) for s in range(4)]
                mid.staged = cache.enter_context(nc.semaphore("staged"))

                def gather(pool, slot, half, fill):
                    pool.tensor_copy(mid.stage[:, slot, :], mid.idx[:, ds(half, 1), :].rearrange(
                        "p a j -> p (a j)")).then_inc(mid.staged, 1)
                    pool.wait_ge(mid.staged, fill + 1)
                    pool.tensor_tensor(mid.apart[:, 0:1], long.consts[:, 0:1], long.consts[:, 1:2], ALU.add)
                    for j in range(STRIDE):
                        pool.indirect_dma_start(mid.raw[:, slot, j, :], None, io.cache_rows,
                                                bass.IndirectOffsetOnAxis(ap=mid.stage[:, slot, j:j + 1], axis=0)
                                                ).then_inc(mid.gathered[slot], 16)

                mid.gather = gather
                with ExitStack() as stage:
                    project(nc, stage, io, psum, long, mid)
                if upto > 1:
                    with ExitStack() as stage:
                        compress(nc, stage, io, psum, long, mid)
            if upto > 2:
                rest(nc, whole, attention, io, psum, long, upto)


_OUTS = [((1, SEQ, D), "y_prompt"), ((DB, 1, D), "y_sample"),
         ((1, 1, SEQ, 4, NKV, HD), "new_kv_prompt"), ((1, DB, 1, 4, NKV, HD), "new_kv_sample"),
         ((1, 1, WIN, 2, NKV, HD), "new_win_prompt"), ((1, DB, WIN, 2, NKV, HD), "new_win_sample"),
         ((1, 1, 2, DG), "new_conv_prompt"), ((1, DB, 2, DG), "new_conv_sample")]


def declare(nc, inputs, upto=99):
    io = Store()
    arrays = {}

    def give(name, a):
        arrays[f"in_{name}_dram"] = a
        return nc.dram_tensor(f"in_{name}_dram", a.shape, mybir.dt.from_np(a.dtype), kind="ExternalInput").ap()

    table = constants()

    def together(group, names):
        at = 0
        for n in names:
            table[n] = (at, table[n][1])
            at += table[n][1].shape[1]
        return give(group, np.concatenate([table[n][1] for n in names], axis=1))

    io.c0 = together("c0", [n for n in table if n not in A_ONLY + C_ONLY + E_ONLY])
    io.cA = together("cA", A_ONLY)
    io.cC = together("cC", C_ONLY)
    io.cE = together("cE", E_ONLY)
    io.where = table
    ap = {name: give(name, np.ascontiguousarray(a)) for name, a in inputs.items()}
    io.x_prompt, io.x_sample = ap["x_prompt"], ap["x_sample"]
    io.cache_rows = ap["cache_kv"].rearrange("l n s (a c) g d -> (l n s a) (c g d)", a=2)
    io.page_table = ap["page_table"]
    io.cache_win = ap["cache_win"].rearrange("l b w c g d -> (l b) w (c g d)")
    io.state_conv = ap["state_conv"].rearrange("l b j c -> (l b) j c")
    io.w_in = ap["w_in"]
    io.conv_w = ap["conv_w"].rearrange("l j c -> (l j) c")
    io.pe_k = ap["pe_k"].rearrange("o l d -> (o l) d")
    io.pe_v = ap["pe_v"].rearrange("o l d -> (o l) d")
    io.w_ck1 = ap["w_ck1"].rearrange("o l d e -> (o l) d e")
    io.w_cv1 = ap["w_cv1"].rearrange("o l d e -> (o l) d e")
    io.w_ck2 = ap["w_ck2"].rearrange("o e d -> (o e) d")
    io.w_cv2 = ap["w_cv2"].rearrange("o e d -> (o e) d")
    io.g_nsa = ap["g_nsa"].rearrange("l c -> (l c)")
    io.g_conv = ap["g_conv"].rearrange("l c -> (l c)")
    io.rel_bias = ap["rel_bias"]
    io.w_out = ap["w_out"].rearrange("l k n -> (l k) n")
    io.w_rg = ap["w_rg"].rearrange("l k n -> (l k) n")
    io.w_re = ap["w_re"].rearrange("l k n -> (l k) n")
    io.b_rg, io.b_re = ap["b_rg"], ap["b_re"]
    io.ln1_g, io.ln1_b, io.ln2_g, io.ln2_b = ap["ln1_g"], ap["ln1_b"], ap["ln2_g"], ap["ln2_b"]
    io.w_eg = ap["w_eg"].rearrange("l g e k f -> (l g e) k f")
    io.w_eu = ap["w_eu"].rearrange("l g e k f -> (l g e) k f")
    io.w_ed = ap["w_ed"].rearrange("l g e f n -> (l g e) f n")
    out = {name: nc.dram_tensor(f"out_{name}_dram", shape, F32, kind="ExternalOutput").ap() for shape, name in _OUTS}
    io.y_prompt = out["y_prompt"].rearrange("b s d -> (b s) d")
    io.y_sample = out["y_sample"].rearrange("b s d -> (b s) d")
    io.new_kv_prompt = out["new_kv_prompt"].rearrange("l b s c g d -> (l b s) (c g d)")
    io.new_kv_sample = out["new_kv_sample"].rearrange("l b s c g d -> (l b s) (c g d)")
    io.new_win_prompt = out["new_win_prompt"].rearrange("l b s c g d -> (l b s) (c g d)")
    io.new_win_sample = out["new_win_sample"].rearrange("l b s c g d -> (l b) s (c g d)")
    io.new_conv_prompt = out["new_conv_prompt"].rearrange("l b j c -> (l b j) c")
    io.new_conv_sample = out["new_conv_sample"].rearrange("l b j c -> (l b) j c")

    def scratch(name, shape, dt=F32):
        return nc.dram_tensor(name, shape, dt, kind="Internal").ap()

    io.fresh = scratch("fresh_rows", (DB, 6 * KVW))
    io.vhan = scratch("bias_by_distance", (NH, HCOLS))
    io.x1 = scratch("x1_rows", (TOK, D))
    io.yrows = scratch("expert_rows", (2 * TOK + CAP, D))
    hybrid_layer(nc, io, upto)
    return arrays


def kernel(**inputs):
    import concourse.bacc as bacc
    from concourse.bass_utils import run_bass_kernel_spmd

    nc = bacc.Bacc("TRN2", target_bir_lowering=False, num_devices=1)
    arrays = declare(nc, {name: np.asarray(a) for name, a in inputs.items()})
    r = run_bass_kernel_spmd(nc, [arrays], core_ids=[0])
    return tuple(r.results[0][f"out_{name}_dram"] for _, name in _OUTS)
```

```python
from contextlib import ExitStack
import math

import numpy as np
import concourse.bass as bass
from concourse import mybir

F32 = mybir.dt.float32
I32 = mybir.dt.int32
U32 = mybir.dt.uint32
ACT = mybir.ActivationFunctionType
ALU = mybir.AluOpType
AX = mybir.AxisListType.X
ds = bass.ds

P = 128
D = 1024
KT = D // P
SEQ, DB = 512, 8
TOK = SEQ + DB
HALF = TOK // 2
QT = SEQ // P
TT = QT + 1
HD, NKV, GQ = 64, 2, 4
NH = NKV * GQ
DG = NH * HD
KVW = NKV * HD
CT = DG // P
PAST, PAGE = 4096, 128
PAGES = PAST // PAGE
STRIDE, CLEN = 16, 32
NJ = CLEN // 2
JP = STRIDE // 2
CHUNKS = PAST // STRIDE
NCMP = CHUNKS - 1
PCH = SEQ // STRIDE
PCMP = PCH - 1
SLC = 64
WIN = 512
BUCKETS, MAXD = 32, 128
NG, NE = 4, 8
EX = NG * NE
FF = 256
NEG = -1e30
ALPHA = 2.0 ** 0.25
SCALE = HD ** -0.5
HCOLS = 1024
HW = 880
SEL = 15
SELK = 7 * P + SLC + 1
TOPB = SEL - 2
CAP = 96
PASSES = -(-TOK // CAP)
RING_EX = 4
SLOTS = PASSES * EX
GATES = 3 * NH
O_KV = DG
O_GATE = O_KV + 6 * KVW
O_CONV = O_GATE + GATES


def bucket(dist):
    n = np.maximum(dist, 0)
    nf = np.maximum(n, 1).astype(np.float32)
    half = BUCKETS // 2
    large = half + (np.log(nf / np.float32(half)) / np.float32(math.log(MAXD / half))
                    * np.float32(BUCKETS - half)).astype(np.int32)
    return np.where(n < half, n, np.minimum(large, BUCKETS - 1))


def onehot(dist):
    out = np.zeros((BUCKETS + 1, len(dist)), np.float32)
    out[np.where(dist >= 0, bucket(dist), BUCKETS), np.arange(len(dist))] = 1.0
    return out


def constants():
    p = np.arange(P)
    c = {}
    c["ident"] = np.eye(P)
    c["tri"] = (p[:, None] < p[None, :])
    c["ones"] = np.ones((P, P))
    c["rep16"] = (p[:16, None] == p[None, :] // 8)
    c["rep_bg"] = (np.arange(DB)[:, None] == np.arange(16)[None, :] // 2)
    k, j, q = np.arange(16)[:, None, None], np.arange(8)[None, :, None], p[None, None, :]
    c["sel_pair"] = (k == 2 * j + (q >= SLC)).reshape(16, -1)
    k, b, g = np.arange(16)[:, None, None], np.arange(8)[None, :, None], np.arange(8)[None, None, :]
    c["sel_b"] = (k == 2 * b + g // GQ).reshape(16, -1)
    c0 = np.arange(2 * P)[:, None] * STRIDE
    s0 = np.arange(65)[None, :] * SLC
    shared = np.maximum(np.minimum(c0 + CLEN, s0 + SLC) - np.maximum(c0, s0), 0)
    c["shared"] = shared.reshape(2, P, 65).transpose(1, 0, 2).reshape(P, -1)
    dm = np.eye(BUCKETS)
    dm[BUCKETS - 1] -= 1
    c["dmat"] = dm
    c["hot_prompt"] = onehot(np.arange(HCOLS) - 511)
    c["hot_cmp"] = onehot(PAST - (np.arange(NCMP) * STRIDE + CLEN - 1))
    r = 4 * np.arange(P)[None, :] + np.arange(4)[:, None]
    c["hot_win"] = onehot(np.where(r == 0, 0, WIN - r).ravel())
    c["hot_sel"] = onehot(np.concatenate([SLC - np.arange(SLC), 2 * SLC - np.arange(SLC), [0]]))
    c["cidx"] = 2 * ((p[:, None] % 8) * STRIDE + np.arange(16)[None, :])
    c["iota"] = np.tile(np.arange(PAGES), (P, 1))
    c["slot_iota"] = np.tile(np.arange(SLOTS), (P, 1))
    c["choice"] = 2 * (p[:, None] + P * (np.arange(2 * TT)[None, :] // 2)) + np.arange(2 * TT)[None, :] % 2 + 1
    c["spare"] = 2 * TOK + 1 + p[:, None] + CAP * (np.arange(SLOTS) % RING_EX)[None, :]
    c["pos64"] = (2 * (p % SLC) + 1)[:, None]
    at, out = 0, {}
    for name, a in c.items():
        full = np.zeros((P, a.shape[1]), np.float32)
        full[:a.shape[0]] = a
        out[name] = (at, full)
        at += a.shape[1]
    return out


class Own:

    def __init__(self, engine, sem):
        self.engine, self.sem, self.n, self.turn = engine, sem, 0, None

    def did(self, instruction):
        instruction.then_inc(self.sem, 1)
        self.n += 1

    def settle(self):
        self.engine.wait_ge(self.sem, self.n if self.turn is None else self.turn + self.n)

    def enter(self, turn, per):
        self.turn, self.start, self.per = turn * per, self.n, per

    def leave(self, turns):
        assert self.n - self.start == self.per, (self.n - self.start, self.per)
        self.turn, self.n = None, self.start + turns * self.per


A_ONLY = ("rep16", "dmat", "hot_prompt", "hot_cmp", "hot_win", "hot_sel", "cidx")
C_ONLY = ("sel_pair",)
E_ONLY = ("slot_iota", "tri", "choice", "spare")


class Store:
    pass


def project(nc, ctx, io, psum, long, mid):
    def sb(name, shape, dt=F32):
        return ctx.enter_context(nc.sbuf_tensor(name, shape, dt))

    def sem(name):
        return ctx.enter_context(nc.semaphore(name))

    xin = mid.early
    xT = sb("xT", [P, KT, TOK])
    wring = sb("wring", [P, 2, KT, 3 * P])
    wgate = sb("wgate", [P, KT, GATES])
    kvT = sb("kvT", [P, 6, TOK])
    gateT = sb("gateT", [GATES, TOK])
    hA = sb("hA", [P, io.cA.shape[1]])
    rows_in = sb("rows_in", [16, DG])
    small_in = sb("small_in", [16, 3 * P + DG])
    conv = kvT[:, :, :].rearrange("p i n -> p (i n)")
    chT = conv[:, 0:TOK]
    u = conv[:, TOK:2 * TOK + 2]
    acc = conv[:, 2 * TOK + 2:3 * TOK + 2]
    ukeep = sb("ukeep", [P, CT, 10])
    urows = small_in[0:10, 0:DG]
    vh = xin[0:NH, QT, :]
    coef = sb("coef", [P, 116])
    tab = sb("tab", [BUCKETS + 1, NH])
    relb = sb("relb", [BUCKETS, NH])
    pg_i = sb("pg_i", [16, 16], I32)
    pg_f = sb("pg_f", [16, 16])

    def cA(name, rows=P):
        at, full = io.where[name]
        return hA[0:rows, at:at + full.shape[1]]

    def c0(name, rows=P):
        return long.c0(name, rows)

    ident = c0("ident")
    x_loaded = [sem(f"x_loaded{t}") for t in range(TT)]
    consts_loaded, hots_loaded = sem("consts_loaded"), sem("hots_loaded")
    small_loaded = sem("small_loaded")
    w_loaded = [sem(f"w_loaded{s}") for s in range(2)]
    gate_w_loaded = sem("gate_w_loaded")
    xT_made = sem("xT_made")
    xT_act, xT_dve = sem("xT_act"), sem("xT_dve")
    mtile = sem("mtile")
    mt_act, mt_dve = sem("mt_act"), sem("mt_dve")
    mt_cc, mt_cb = sem("mt_cc"), sem("mt_cb")
    kvt_made = sem("kvt_made")
    kvt_act, kvt_dve = sem("kvt_act"), sem("kvt_dve")
    small_made, small_dve = sem("small_made"), sem("small_dve")
    misc_made, misc_dve = sem("misc_made"), sem("misc_dve")
    u_made, urows_done = sem("u_made"), sem("urows_done")
    idx_ready = sem("idx_ready")
    gathered = mid.gathered
    stores = sem("stores")
    table_stored = sem("table_stored")
    relaid = sem("relaid")
    own_dve = sem("own_dve_a")
    block = ctx.enter_context(nc.Block())

    w_in = io.w_in.rearrange("l (k p) n -> (l p) k n", p=P)

    @block.sync
    def _(sp):
        for t in range(QT):
            sp.dma_start(xin[:, t, :], io.x_prompt[0, t * P:(t + 1) * P, :]).then_inc(x_loaded[t], 16)
        sp.dma_start(xin[0:DB, QT, :], io.x_sample.rearrange("b s d -> (b s) d")).then_inc(x_loaded[QT], 16)
        for c in range(2):
            for g in range(NKV):
                for i in range(2):
                    col = g * GQ * HD + (2 * c + i) * HD
                    sp.dma_start(wring[:, c, :, i * P + g * HD:i * P + (g + 1) * HD],
                                 w_in[:, :, col:col + HD]).then_inc(w_loaded[c], 16)
        sp.dma_start(wgate[:, :, :], w_in[:, :, O_GATE:O_GATE + GATES]).then_inc(gate_w_loaded, 16)
        sp.wait_ge(xT_made, TT)
        for n, w in enumerate((io.w_ck1, io.w_cv1)):
            sp.dma_start(mid.w1[:, n, :, :], w.rearrange("l d e -> (l d) e").rearrange("(j q) e -> q j e", q=P)
                         ).then_inc(mid.w_loaded, 16)
        sp.dma_start(mid.w2[:, 0, :], io.w_ck2).then_inc(mid.w_loaded, 16)
        sp.dma_start(mid.w2[:, 1, :], io.w_cv2).then_inc(mid.w_loaded, 16)
        for c in range(2):
            sp.wait_ge(mtile, 2 * c + 2)
            col = O_KV + 3 * c * P
            sp.dma_start(wring[:, c, :, :], w_in[:, :, col:col + 3 * P]).then_inc(w_loaded[c], 16)
        with sp.Fori(0, CT // 2) as pair:
            ct = pair * 2
            for s in range(2):
                sp.wait_ge(mtile, ct * 3 + 8 + 3 * s)
                for n, part in enumerate((2, 1, 0)):
                    sp.dma_start(wring[:, s, :, n * P:(n + 1) * P],
                                 w_in[:, :, ds(ct * P + O_CONV + part * DG + s * P, P)]
                                 ).then_inc(w_loaded[s], 16)
        for b in range(DB):
            src = io.cache_win[b, 1:WIN, :].rearrange("r c -> (r c)").rearrange("(a n) -> a n", a=16)
            dst = io.new_win_sample[b, 0:WIN - 1, :].rearrange("r c -> (r c)").rearrange("(a n) -> a n", a=16)
            sp.dma_start(dst, src).then_inc(stores, 16)
        sp.dma_start(io.new_conv_sample[:, 0, :], io.state_conv[:, 1, :]).then_inc(stores, 16)
        sp.wait_ge(misc_dve, 4)
        sp.dma_start(io.vhan, vh).then_inc(stores, 16)
        sp.wait_ge(kvt_act, TT)
        sp.wait_ge(kvt_dve, TT)
        for t in range(QT):
            sp.dma_start(io.new_kv_prompt[t * P:(t + 1) * P, :], long.kvtok[:, t, 0:4 * KVW]).then_inc(stores, 16)
            sp.dma_start(io.new_win_prompt[t * P:(t + 1) * P, :], long.kvtok[:, t, 4 * KVW:]).then_inc(stores, 16)
        sp.dma_start(io.new_kv_sample, long.kvtok[0:DB, QT, 0:4 * KVW]).then_inc(stores, 16)
        sp.dma_start(io.fresh, long.kvtok[0:DB, QT, :]).then_inc(stores, 16)
        sp.dma_start(io.new_win_sample[:, WIN - 1, :], long.kvtok[0:DB, QT, 4 * KVW:]).then_inc(stores, 16)
        sp.wait_ge(urows_done, 1)
        sp.dma_start(io.new_conv_prompt, urows[0:2, :]).then_inc(stores, 16)
        sp.dma_start(io.new_conv_sample[:, 1, :], urows[2:10, :]).then_inc(stores, 16)
        sp.wait_ge(stores, 16 * (2 * QT + 6 + DB + 1))

    @block.scalar
    def _(act):
        act.dma_start(long.consts[:, :], io.c0).then_inc(consts_loaded, 16)
        act.dma_start(rows_in[:, :], io.state_conv.rearrange("b j c -> (b j) c")).then_inc(small_loaded, 16)
        act.dma_start(small_in[0:3, 0:DG], io.conv_w).then_inc(small_loaded, 16)
        act.dma_start(small_in[0:CT, DG:DG + P], io.g_nsa.rearrange("(c p) -> c p", p=P)).then_inc(small_loaded, 16)
        act.dma_start(small_in[0:CT, DG + P:DG + 2 * P], io.g_conv.rearrange("(c p) -> c p", p=P)).then_inc(small_loaded, 16)
        act.dma_start(mid.pe_in[:, 0, :], io.pe_k.rearrange("(l q) d -> l (q d)", q=2)).then_inc(small_loaded, 16)
        act.dma_start(mid.pe_in[:, 1, :], io.pe_v.rearrange("(l q) d -> l (q d)", q=2)).then_inc(small_loaded, 16)
        act.dma_start(relb[:, :], io.rel_bias).then_inc(small_loaded, 16)
        act.dma_start(pg_i[:, :].rearrange("p (b h) -> p b h", h=2),
                      io.page_table.rearrange("b (h p) -> p b h", p=16),
                      allow_slow_non_contiguous=True).then_inc(small_loaded, 16)
        act.dma_start(hA[:, :], io.cA).then_inc(hots_loaded, 16)
        for t in range(TT):
            act.wait_ge(xT_made, t + 1)
            n = P if t < QT else DB
            act.copy(xT[:, 4:8, t * P:t * P + n],
                     psum[:, 7 - 2 * (t % 4), 0:4 * n].rearrange("p (k n) -> p k n", n=n)).then_inc(xT_act, 1)
        for m in range(11):
            act.wait_ge(mtile, m + 1)
            src = psum[:, 2 * (m % 3), 0:HALF]
            if m < 4:
                act.mul(long.qT[:, m, 0:HALF], src, SCALE).then_inc(mt_act, 1)
            elif m < 10:
                act.copy(kvT[:, m - 4, 0:HALF], src).then_inc(mt_act, 1)
            else:
                act.activation(gateT[:, 0:HALF], src[0:GATES, :], ACT.Sigmoid).then_inc(mt_act, 1)
                act.activation(gateT[:, HALF:TOK], psum[0:GATES, 2 * (m % 3) + 1, 0:HALF],
                               ACT.Sigmoid).then_inc(mt_act, 1)
        for t in range(TT):
            n = P if t < QT else DB
            act.wait_ge(kvt_made, 2 * t + 1)
            act.copy(long.kvtok[0:n, t, 0:4 * P], psum[0:n, 6, :]).then_inc(kvt_act, 1)
        act.wait_ge(mt_dve, 10)
        for i in range(2):
            for g in range(NKV):
                for par in range(2):
                    src = kvT[g * HD:(g + 1) * HD, i, 0:SEQ].rearrange(
                        "p (c j q) -> p q j c", q=2, j=JP)[:, par]
                    act.copy(mid.xTp[par * HD:(par + 1) * HD, 2 * i + g, :, :], src).then_inc(relaid, 1)
        act.wait_ge(relaid, 8)
        with act.Fori(0, CT) as ct:
            for h in range(2):
                if h == 0:
                    act.wait_ge(mtile, ct * 3 + 12)
                    act.wait_ge(mt_cc, ct * 1 + 1)
                act.copy(chT[:, h * HALF:(h + 1) * HALF], psum[:, 4 + h, 0:HALF]).then_inc(mt_act, 1)

    @block.tensor
    def _(pe):
        pe.wait_ge(consts_loaded, 16)
        for t in range(TT):
            n = P if t < QT else DB
            pe.wait_ge(x_loaded[t], 16)
            if t > 3:
                pe.wait_ge(xT_act, t - 3)
                pe.wait_ge(xT_dve, t - 3)
            for k in range(KT):
                last = pe.transpose(psum[:, 6 - 2 * (t % 4) + k // 4, (k % 4) * n:(k % 4 + 1) * n],
                                    xin[0:n, t, k * P:(k + 1) * P], ident[0:n, 0:n])
            last.then_inc(xT_made, 1)
        pe.wait_ge(xT_act, TT)
        pe.wait_ge(xT_dve, TT)

        def tile(bank, w, width):
            for h in range(2):
                for k in range(KT):
                    last = pe.matmul(psum[0:width, bank + h, 0:HALF], w(k),
                                     xT[:, k, h * HALF:(h + 1) * HALF], start=k == 0, stop=k == KT - 1)
            last.then_inc(mtile, 1)

        def small_transposes():
            pe.wait_ge(small_loaded, 16 * 8)
            pe.wait_ge(hots_loaded, 16)
            for ct in range(CT):
                pe.transpose(psum[:, 6, 16 * ct:16 * ct + 16], rows_in[0:16, ct * P:(ct + 1) * P], ident[0:16, 0:16])
                pe.transpose(psum[:, 6, 64 + 3 * ct:67 + 3 * ct], small_in[0:3, ct * P:(ct + 1) * P], ident[0:3, 0:3])
            for n in range(2):
                pe.transpose(psum[:, 6, 76 + CT * n:80 + CT * n], small_in[0:CT, DG + n * P:DG + (n + 1) * P],
                             ident[0:CT, 0:CT])
            for n in range(2):
                last = pe.transpose(psum[:, 6, 84 + 16 * n:100 + 16 * n], mid.pe_in[:, n, :], ident[0:16, 0:16])
            last.then_inc(small_made, 1)
            pe.matmul(psum[0:BUCKETS, 7, 0:NH], cA("dmat", BUCKETS), relb[:, :], start=True, stop=True)
            pe.wait_ge(idx_ready, 1)
            pe.matmul(psum[:, 7, 16:32], cA("rep16", 16), pg_f[:, :], start=True, stop=True).then_inc(misc_made, 1)

        def bias_tables():
            pe.wait_ge(small_dve, 1)
            pe.wait_ge(misc_dve, 3)
            for h in range(2):
                last = pe.matmul(psum[0:NH, 6 + h, :], tab[:, :], cA("hot_prompt", BUCKETS + 1)[:, h * 512:(h + 1) * 512],
                                 start=True, stop=True)
            last.then_inc(misc_made, 1)

        def sample_tables():
            pe.wait_ge(misc_dve, 4)
            pe.matmul(psum[0:NH, 6, :], tab[:, :], cA("hot_win", BUCKETS + 1), start=True, stop=True)
            pe.matmul(psum[0:NH, 7, 0:NCMP], tab[:, :], cA("hot_cmp", BUCKETS + 1), start=True, stop=True)
            pe.matmul(psum[0:NH, 7, NCMP:NCMP + 129], tab[:, :], cA("hot_sel", BUCKETS + 1),
                      start=True, stop=True).then_inc(misc_made, 1)

        for m in range(10):
            c, i = (m // 2, m % 2) if m < 4 else ((m - 4) // 3, (m - 4) % 3)
            if m in (0, 2):
                pe.wait_ge(w_loaded[c], 16 * 4)
            if m in (4, 7):
                pe.wait_ge(w_loaded[c], 16 * 5)
            if m >= 3:
                pe.wait_ge(mt_act, m - 2)
                pe.wait_ge(mt_dve, m - 2)
            tile(2 * (m % 3), lambda k: wring[:, c, k, i * P:(i + 1) * P], P)
            if m == 0:
                small_transposes()
            if m == 1:
                bias_tables()
            if m == 2:
                sample_tables()
        pe.wait_ge(gate_w_loaded, 16)
        pe.wait_ge(mt_act, 8)
        pe.wait_ge(mt_dve, 8)
        tile(2, lambda k: wgate[:, k, :], GATES)
        pe.wait_ge(misc_dve, 6)
        pe.wait_ge(mt_act, 12)
        pe.wait_ge(mt_dve, 10)
        for t in range(TT):
            n = P if t < QT else DB
            if t:
                pe.wait_ge(kvt_act, t)
            for i in range(4):
                last = pe.transpose(psum[0:n, 6, i * P:(i + 1) * P], kvT[:, i, t * P:t * P + n], ident)
            last.then_inc(kvt_made, 1)
            if t:
                pe.wait_ge(kvt_dve, t)
            for i in range(4, 6):
                pe.transpose(psum[0:n, 7, (i - 4) * P:(i - 3) * P], kvT[:, i, t * P:t * P + n], ident)
            pe.transpose(psum[0:n, 7, 2 * P:2 * P + GATES], gateT[:, t * P:t * P + n],
                         ident[0:GATES, 0:GATES]).then_inc(kvt_made, 1)
        with pe.Fori(0, CT // 2) as pair:
            ct = pair * 2
            for s in range(2):
                pe.wait_ge(w_loaded[s], ct * 24 + 16 * (5 + 3))
                for n, bank in enumerate((4, 0, 2)):
                    if n == 0:
                        pe.wait_ge(mt_act, ct * 2 + 12 + 2 * s)
                    elif n == 1:
                        pe.wait_ge(mt_cc, ct + s + 1)
                    else:
                        pe.wait_ge(mt_cb, ct + s + 1)
                    tile(bank, lambda k: wring[:, s, k, n * P:(n + 1) * P], P)
        pe.wait_ge(u_made, CT)
        pe.wait_ge(kvt_act, TT)
        for ct in range(CT):
            last = pe.transpose(psum[0:10, 6, ct * P:(ct + 1) * P], ukeep[:, ct, :], ident)
        last.then_inc(misc_made, 1)

    @block.vector
    def _(dve):
        own = Own(dve, own_dve)
        own.did(dve.memset(long.q8[:, :, :], 0.0))
        own.did(dve.memset(tab[:, :], NEG))
        for t in range(TT):
            dve.wait_ge(xT_made, t + 1)
            n = P if t < QT else DB
            dve.tensor_copy(xT[:, 0:4, t * P:t * P + n],
                            psum[:, 6 - 2 * (t % 4), 0:4 * n].rearrange("p (k n) -> p k n", n=n)).then_inc(xT_dve, 1)
        dve.wait_ge(small_loaded, 16 * 8)
        dve.wait_ge(hots_loaded, 16)
        dve.tensor_copy(pg_f[:, :], pg_i[:, :]).then_inc(idx_ready, 1)

        def small_tables():
            dve.wait_ge(small_made, 1)
            own.did(dve.tensor_copy(long.gains[:, :], psum[:, 6, 76:84]))
            own.did(dve.tensor_copy(mid.peT[:, :], psum[:, 6, 84:116]))
            dve.tensor_copy(coef[:, 0:76], psum[:, 6, 0:76]).then_inc(small_dve, 1)
            dve.wait_ge(misc_made, 1)
            own.settle()
            dve.tensor_copy(tab[0:BUCKETS, :], psum[0:BUCKETS, 7, 0:NH]).then_inc(misc_dve, 1)
            own.did(dve.tensor_copy(mid.pages[:, :], psum[:, 7, 16:32]))
            own.settle()
            dve.tensor_scalar(mid.pages[:, :], mid.pages[:, :], 2.0 * PAGE, None, ALU.mult).then_inc(misc_dve, 1)
            dve.wait_ge(misc_dve, 2)
            dve.tensor_tensor(mid.idx[:, :, :],
                              mid.pages[:, :].unsqueeze(2).to_broadcast([P, 16, 16]),
                              cA("cidx").unsqueeze(1).to_broadcast([P, 16, 16]), ALU.add).then_inc(misc_dve, 1)

        def tables():
            dve.wait_ge(misc_made, 2)
            own.did(dve.tensor_copy(vh[:, 0:512], psum[0:NH, 6, :]))
            dve.tensor_copy(vh[:, 512:1024], psum[0:NH, 7, :]).then_inc(misc_dve, 1)

        def tables2():
            dve.wait_ge(misc_made, 3)
            dve.tensor_copy(long.b_win[:, :], psum[0:NH, 6, :]).then_inc(misc_dve, 1)
            dve.tensor_copy(long.b_cs[:, :], psum[0:NH, 7, 0:NCMP + 129]).then_inc(misc_dve, 1)

        for m in range(10):
            dve.wait_ge(mtile, m + 1)
            src = psum[:, 2 * (m % 3) + 1, 0:HALF]
            if m < 4:
                dve.tensor_scalar(long.qT[:, m, HALF:TOK], src, SCALE, None, ALU.mult).then_inc(mt_dve, 1)
            else:
                dve.tensor_copy(kvT[:, m - 4, HALF:TOK], src).then_inc(mt_dve, 1)
            if m == 0:
                small_tables()
            if m == 1:
                tables()
            if m == 2:
                tables2()
        dve.wait_ge(mt_dve, 10)
        own.settle()
        for g in range(NKV):
            rows = slice(g * HD, (g + 1) * HD)
            own.did(dve.tensor_copy(long.q8[rows, :, g * GQ:(g + 1) * GQ],
                                    long.qT[rows, :, SEQ:TOK].rearrange("p r b -> p b r")))
        for t in range(TT):
            n = P if t < QT else DB
            dve.wait_ge(kvt_made, 2 * t + 2)
            own.did(dve.tensor_copy(long.kvtok[0:n, t, 4 * P:6 * P], psum[0:n, 7, 0:2 * P]))
            dve.tensor_copy(long.gates[0:n, t, :], psum[0:n, 7, 2 * P:2 * P + GATES]).then_inc(kvt_dve, 1)
        dve.wait_ge(mt_act, 12)
        own.did(dve.tensor_copy(long.kT[:, 0, :], kvT[:, 2, :]))
        own.did(dve.tensor_copy(long.kT[:, 1, :], kvT[:, 4, :]))
        dve.wait_ge(relaid, 8)
        dve.wait_ge(mtile, 12)
        own.settle()
        own.did(dve.memset(u[:, 0:2], 0.0))
        dve.sem_inc(mt_cc, 1)
        dve.sem_inc(mt_cb, 1)
        with dve.Fori(0, CT) as ct:
            own.enter(ct, 8)
            dve.wait_ge(mt_act, ct * 2 + 14)
            dve.wait_ge(mtile, ct * 3 + 13)
            own.settle()
            dve.wait_ge(mt_cb, ct + 1)
            own.did(dve.tensor_tensor(u[:, 2:2 + HALF], psum[:, 0, 0:HALF], chT[:, 0:HALF], ALU.mult))
            dve.tensor_tensor(u[:, 2 + HALF:], psum[:, 1, 0:HALF], chT[:, HALF:TOK], ALU.mult).then_inc(mt_cc, 1)
            own.settle()
            dve.wait_ge(mt_cc, ct + 2)
            taps = [coef[:, ds(ct * 3 + 64 + j, 1)] for j in range(3)]
            old = [coef[:, ds(ct * 16 + j, 16 - j)][:, ::2] for j in range(2)]
            own.did(dve.tensor_scalar(acc[:, 0:SEQ], u[:, 2:2 + SEQ], taps[2], None, ALU.mult))
            own.did(dve.tensor_scalar(acc[:, SEQ:TOK], u[:, 2 + SEQ:], taps[2], None, ALU.mult))
            own.settle()
            own.did(dve.scalar_tensor_tensor(acc[:, 0:SEQ], u[:, 1:1 + SEQ], taps[1], acc[:, 0:SEQ], ALU.mult, ALU.add))
            own.did(dve.scalar_tensor_tensor(acc[:, SEQ:TOK], old[1], taps[1], acc[:, SEQ:TOK], ALU.mult, ALU.add))
            own.settle()
            own.did(dve.scalar_tensor_tensor(acc[:, 0:SEQ], u[:, 0:SEQ], taps[0], acc[:, 0:SEQ], ALU.mult, ALU.add))
            own.did(dve.scalar_tensor_tensor(acc[:, SEQ:TOK], old[0], taps[0], acc[:, SEQ:TOK], ALU.mult, ALU.add))
            dve.tensor_copy(ukeep[:, ds(ct, 1), :], u[:, SEQ:SEQ + 10].unsqueeze(1)).then_inc(u_made, 1)
            dve.wait_ge(u_made, ct + 1)
            dve.wait_ge(mtile, ct * 3 + 14)
            own.settle()
            z = long.zT[:, ds(ct, 1), :].rearrange("p a n -> p (a n)")
            own.did(dve.tensor_tensor(z[:, 0:HALF], psum[:, 2, 0:HALF], acc[:, 0:HALF], ALU.mult))
            dve.tensor_tensor(z[:, HALF:TOK], psum[:, 3, 0:HALF], acc[:, HALF:TOK], ALU.mult).then_inc(mt_cb, 1)
        own.leave(CT)
        dve.wait_ge(misc_made, 4)
        dve.tensor_copy(urows, psum[0:10, 6, :]).then_inc(urows_done, 1)

    @block.gpsimd
    def _(pool):
        pool.wait_ge(misc_dve, 3)
        for s in range(4):
            mid.gather(pool, s, s, s)


def compress(nc, ctx, io, psum, long, mid):
    def sb(name, shape, dt=F32):
        return ctx.enter_context(nc.sbuf_tensor(name, shape, dt))

    def sem(name):
        return ctx.enter_context(nc.semaphore(name))

    w1 = mid.w1
    w2 = mid.w2
    cT = sb("cT", [P, 2, NKV, JP, CHUNKS])
    cbias = sb("cbias", [P, 2])
    hid = sb("hid", [P, 2, CHUNKS])
    kc = sb("kc", [P, CHUNKS])
    vc = sb("vc", [P, 2, KVW])
    wraw = sb("wraw", [P, 2, 4, 2 * KVW])
    kwT = sb("kwT", [P, 4 * P])
    q8 = sb("q8s", [P, 2, NH])
    sc = sb("sc", [NH, 2, WIN])
    ex = sb("ex", [NH, 2, WIN])
    st = sb("st", [NH, 2, 4])
    pT = sb("pT", [P, 2, 4 * NH])
    ident = long.c0("ident")

    w_loaded = mid.w_loaded
    gathered = mid.gathered
    win_loaded = [sem(f"win_loaded{u}") for u in range(2)]
    win_new = [sem(f"win_new{u}") for u in range(2)]
    c_made, c_act, c_dve = sem("c_made"), sem("c_act"), sem("c_dve")
    h_made, h_act = sem("h_made"), sem("h_act")
    o_made, o_dve = sem("o_made"), sem("o_dve")
    b_made, b_dve = sem("b_made"), sem("b_dve")
    q_staged = sem("q_staged")
    neg_max = sem("neg_max")
    exp_made = sem("exp_made")
    prob_made = sem("prob_made")
    bias_made, bias_read = sem("cb_made"), sem("cb_read")
    own_dve, own_act = sem("own_dve_b"), sem("own_act_b")
    block = ctx.enter_context(nc.Block())

    STEPS = 4
    USES = 7

    def schedule():
        out = {s: [] for s in range(9)}
        for i in range(4):
            out[i].append(("w", 0, i))
            out[4 + i].append(("w", 1, i))
        for i in range(3):
            out[4 + i].append(("c", 0, i))
            out[8].append(("c", 1, i))
        return out

    PLAN = schedule()
    TICKET = {use: n for n, use in enumerate(use for s in range(9) for use in PLAN[s])}
    SOFT = {use[:2]: n for n, use in enumerate(sorted(
        (use for use in TICKET if use[2] == (0 if use[0] == "c" else 1)), key=TICKET.get))}

    @block.sync
    def _(sp):
        def window(b, u, landed):
            sp.dma_start(wraw[:, u, :, :].rearrange("p t c -> p (t c)"),
                         io.cache_win[ds(b, 1)].rearrange("b (p t) c -> (b p) (t c)", t=4)
                         ).then_inc(win_loaded[u], 16)
            sp.wait_ge(win_loaded[u], landed)
            sp.dma_start(wraw[0:1, u, 0, :], io.fresh[ds(b, 1), 4 * KVW:]).then_inc(win_new[u], 16)

        for u in range(2):
            window(u, u, 16)
        with sp.Fori(0, DB // 2 - 1) as pair:
            b = pair * 2
            for u in range(2):
                sp.wait_ge(b_dve, b * USES + TICKET["w", u, 3] + 2)
                window(b + 2 + u, u, b * 8 + 32)

    @block.gpsimd
    def _(pool):
        with pool.Fori(0, DB // 2 - 1) as pair:
            b = pair * 2
            for u in range(2):
                pool.wait_ge(c_made, b * 16 + 16 * (u + 1))
                for h in range(2):
                    mid.gather(pool, 2 * u + h, b * 2 + 4 + 2 * u + h, b * 2 + 4 + 2 * u + h)

    @block.tensor
    def _(pe):
        pe.wait_ge(w_loaded, 16 * 4)
        for n in range(2):
            for j in range(NJ):
                last = pe.matmul(psum[:, 7, n:n + 1], w1[:, n, j, :], mid.peT[:, NJ * n + j:NJ * n + j + 1],
                                 start=j == 0, stop=j == NJ - 1)
        last.then_inc(bias_made, 1)
        pe.wait_ge(bias_read, 1)

        def transposes(b, unit, fills):
            u, n = unit // 2, unit % 2
            if n == 0 and 0 in fills:
                for h in range(2):
                    pe.wait_ge(gathered[2 * u + h], b * 128 + 256)
            for f in fills:
                done = b * 8 + 4 * unit + f // 2
                pe.wait_ge(c_act if f % 2 else c_dve, (done if unit == 0 and f < 2 else done - 1) + 1)
                for j in range(2):
                    for h in range(2):
                        last = pe.transpose(psum[:, f % 4, j * CHUNKS + h * P:j * CHUNKS + (h + 1) * P],
                                            mid.raw[:, 2 * u + h, 2 * f + j, n * KVW:(n + 1) * KVW], ident)
                last.then_inc(c_made, 1)

        def hidden(b, s):
            unit, n, g = s // 2, s % 4 // 2, s % 2
            pe.wait_ge(c_dve, b * 8 + 4 * unit + 5)
            pe.wait_ge(c_act, b * 8 + 4 * unit + 5)
            for r in range(2):
                for j in range(JP):
                    last = pe.matmul(psum[:, 4 + s % 2, 0:NCMP], w1[:, n, r * JP + j, :],
                                     cT[:, unit % 2, g, j, r:r + NCMP], start=r + j == 0, stop=r + j == JP)
            last.then_inc(h_made, 1)

        def output(b, s):
            u, n, g = s // 4, s % 4 // 2, s % 2
            pe.wait_ge(h_act, b * 4 + s + 1)
            if g == 0:
                pe.wait_ge(o_dve, b * 2 + 2 * u + n + 1)
            if n == 0:
                last = pe.matmul(psum[g * HD:(g + 1) * HD, 6, 0:NCMP], w2[:, 0, :], hid[:, s % 2, 0:NCMP],
                                 start=True, stop=True)
            else:
                for h in range(2):
                    m = P if h == 0 else NCMP - P
                    last = pe.matmul(psum[0:m, 6, h * KVW + g * HD:h * KVW + (g + 1) * HD],
                                     hid[:, s % 2, h * P:h * P + m], w2[:, 1, :], start=True, stop=True)
            if g == 1:
                last.then_inc(o_made, 1)

        def use(b, kind, u, i):
            t = b * USES + TICKET[kind, u, i]
            pe.wait_ge(b_dve, t + 1)
            x = 0 if kind == "c" else 1
            if kind == "w" and i == 0:
                pe.wait_ge(win_loaded[u], b * 8 + 16)
                pe.wait_ge(win_new[u], b * 8 + 16)
                for n in range(4):
                    last = pe.transpose(psum[:, 7, n * P:(n + 1) * P], wraw[:, u, n, 0:KVW], ident)
            elif (kind, i) == ("w", 1):
                pe.wait_ge(q_staged, b + u + 1)
                last = pe.matmul(psum[0:NH, 7, :], q8[:, u, :], kwT[:, :], start=True, stop=True)
            elif (kind, i) == ("c", 0):
                pe.wait_ge(o_dve, b * 2 + 2 * u + 2)
                last = pe.matmul(psum[0:NH, 7, 0:NCMP], q8[:, u, :], kc[:, 0:NCMP], start=True, stop=True)
            elif (kind, i) in (("w", 2), ("c", 1)):
                pe.wait_ge(prob_made, b * 2 + SOFT[kind, u] + 1)
                for n in range(4 if kind == "w" else 2):
                    m = NCMP - P if kind == "c" and n == 1 else P
                    last = pe.matmul(psum[0:m, 7, n * NH:(n + 1) * NH], sc[:, x, n * P:n * P + m],
                                     ident[0:NH, 0:NH], start=True, stop=True)
            elif kind == "w":
                for g in range(NKV):
                    for n in range(4):
                        last = pe.matmul(psum[0:HD, 7, g * GQ:(g + 1) * GQ],
                                         wraw[:, u, n, KVW + g * HD:KVW + (g + 1) * HD],
                                         pT[:, 1, n * NH + g * GQ:n * NH + (g + 1) * GQ], start=n == 0, stop=n == 3)
            else:
                pe.wait_ge(o_dve, b * 2 + 2 * u + 3)
                for g in range(NKV):
                    for n in range(2):
                        m = P if n == 0 else NCMP - P
                        last = pe.matmul(psum[0:HD, 7, g * GQ:(g + 1) * GQ], vc[0:m, n, g * HD:(g + 1) * HD],
                                         pT[0:m, 0, n * NH + g * GQ:n * NH + (g + 1) * GQ], start=n == 0, stop=n == 1)
            last.then_inc(b_made, 1)

        with pe.Fori(0, DB // 2) as pair:
            b = pair * 2
            transposes(b, 0, range(JP))
            for s in range(8):
                if s < 6:
                    transposes(b, s // 2 + 1, range(4 * (s % 2), 4 * (s % 2) + 4))
                if s:
                    output(b, s - 1)
                hidden(b, s)
                for kind, u, i in PLAN[s]:
                    use(b, kind, u, i)
            output(b, 7)
            for kind, u, i in PLAN[8]:
                use(b, kind, u, i)

        for n in range(4):
            for r in range(2):
                for j in range(JP):
                    last = pe.matmul(psum[:, 4, n * 32:n * 32 + PCMP], w1[:, n // 2, r * JP + j, :],
                                     mid.xTp[:, n, j, r:r + PCMP], start=r + j == 0, stop=r + j == JP)
        last.then_inc(h_made, 1)
        pe.wait_ge(h_act, 4 * DB + 1)
        for g in range(NKV):
            pe.matmul(psum[g * HD:(g + 1) * HD, 6, 0:PCMP], w2[:, 0, :], hid[:, 0, g * 32:g * 32 + PCMP],
                      start=True, stop=True)
            last = pe.matmul(psum[0:PCMP, 6, P + g * HD:P + (g + 1) * HD], hid[:, 0, 64 + g * 32:64 + g * 32 + PCMP],
                             w2[:, 1, :], start=True, stop=True)
        last.then_inc(o_made, 1)

    @block.scalar
    def _(act):
        act.wait_ge(bias_read, 1)

        def rows_in(b, unit, fills):
            for f in fills:
                act.wait_ge(c_made, b * 16 + 8 * unit + f + 1)
                for g in range(NKV):
                    for j in range(2):
                        last = act.copy(cT[j * HD:(j + 1) * HD, unit % 2, g, f, :],
                                        psum[g * HD:(g + 1) * HD, f % 4, j * CHUNKS:(j + 1) * CHUNKS])
                last.then_inc(c_act, 1)

        act.sem_inc(c_act, 1)
        with act.Fori(0, DB // 2) as pair:
            b = pair * 2
            rows_in(b, 0, range(1, JP, 2))
            for s in range(8):
                if s < 6:
                    rows_in(b, s // 2 + 1, range(4 * (s % 2) + 1, 4 * (s % 2) + 4, 2))
                act.wait_ge(h_made, b * 4 + s + 1)
                n = s % 4 // 2
                act.activation(hid[:, s % 2, 0:NCMP], psum[:, 4 + s % 2, 0:NCMP], ACT.Gelu_apprx_tanh,
                               bias=cbias[:, n:n + 1]).then_inc(h_act, 1)
                for kind, u, i in PLAN[s] + (PLAN[8] if s == 7 else []):
                    if (kind, i) in (("c", 0), ("w", 1)):
                        x = 0 if kind == "c" else 1
                        m = NCMP if kind == "c" else WIN
                        act.wait_ge(neg_max, b * 2 + SOFT[kind, u] + 1)
                        act.activation(ex[:, x, 0:m], sc[:, x, 0:m], ACT.Exp, bias=st[:, x, 0:1],
                                       accum_out=st[:, x, 1:2]).then_inc(exp_made, 1)
        act.wait_ge(h_made, 4 * DB + 1)
        own = Own(act, own_act)
        own.did(act.activation(hid[:, 0, 0:64].rearrange("p (g c) -> p g c", c=32)[:, :, 0:PCMP],
                               psum[:, 4, 0:64].rearrange("p (g c) -> p g c", c=32)[:, :, 0:PCMP],
                               ACT.Gelu_apprx_tanh, bias=cbias[:, 0:1]))
        act.activation(hid[:, 0, 64:128].rearrange("p (g c) -> p g c", c=32)[:, :, 0:PCMP],
                       psum[:, 4, 64:128].rearrange("p (g c) -> p g c", c=32)[:, :, 0:PCMP],
                       ACT.Gelu_apprx_tanh, bias=cbias[:, 1:2]).then_inc(h_act, 1)

    @block.vector
    def _(dve):
        own = Own(dve, own_dve)
        dve.wait_ge(bias_made, 1)
        dve.tensor_copy(cbias[:, :], psum[:, 7, 0:2]).then_inc(bias_read, 1)

        def rows_in(b, unit, fills):
            for f in fills:
                dve.wait_ge(c_made, b * 16 + 8 * unit + f + 1)
                for g in range(NKV):
                    for j in range(2):
                        last = dve.tensor_copy(cT[j * HD:(j + 1) * HD, unit % 2, g, f, :],
                                               psum[g * HD:(g + 1) * HD, f % 4, j * CHUNKS:(j + 1) * CHUNKS])
                last.then_inc(c_dve, 1)

        def output(b, s):
            u, n, g = s // 4, s % 4 // 2, s % 2
            if g == 1:
                dve.wait_ge(o_made, b * 2 + 2 * u + n + 1)
                if n == 0:
                    dve.tensor_copy(kc[:, 0:NCMP], psum[:, 6, 0:NCMP]).then_inc(o_dve, 1)
                else:
                    own.did(dve.tensor_copy(vc[:, 0, :], psum[:, 6, 0:KVW]))
                    dve.tensor_copy(vc[0:NCMP - P, 1, :], psum[0:NCMP - P, 6, KVW:2 * KVW]).then_inc(o_dve, 1)

        def use(b, kind, u, i):
            dve.wait_ge(b_made, b * USES + TICKET[kind, u, i] + 1)
            x = 0 if kind == "c" else 1
            if (kind, i) == ("w", 0):
                dve.tensor_copy(kwT[:, :], psum[:, 7, :]).then_inc(b_dve, 1)
            elif (kind, i) in (("c", 0), ("w", 1)):
                m = NCMP if kind == "c" else WIN
                bias = long.b_cs[:, 0:NCMP] if kind == "c" else long.b_win[:, :]
                n = b * 2 + SOFT[kind, u] + 1
                dve.tensor_tensor(sc[:, x, 0:m], psum[0:NH, 7, 0:m], bias, ALU.add).then_inc(b_dve, 1)
                dve.wait_ge(b_dve, b * USES + TICKET[kind, u, i] + 2)
                dve.tensor_reduce(st[:, x, 0:1], sc[:, x, 0:m], AX, ALU.max, negate=True).then_inc(neg_max, 1)
                dve.wait_ge(exp_made, n)
                own.did(dve.reciprocal(st[:, x, 2:3], st[:, x, 1:2]))
                own.settle()
                dve.tensor_scalar(sc[:, x, 0:m], ex[:, x, 0:m], st[:, x, 2:3], None, ALU.mult).then_inc(prob_made, 1)
            elif (kind, i) == ("w", 2):
                dve.tensor_copy(pT[:, 1, 0:4 * NH], psum[:, 7, 0:4 * NH]).then_inc(b_dve, 1)
            elif (kind, i) == ("c", 1):
                own.did(dve.tensor_copy(pT[:, 0, 0:NH], psum[:, 7, 0:NH]))
                dve.tensor_copy(pT[0:NCMP - P, 0, NH:2 * NH], psum[0:NCMP - P, 7, NH:2 * NH]).then_inc(b_dve, 1)
                dve.wait_ge(b_dve, b * USES + TICKET[kind, u, i] + 2)
                own.settle()
                for n in range(2):
                    m = P if n == 0 else NCMP - P
                    own.did(dve.tensor_reduce(long.pgT[0:m, n, ds(b * 2 + 2 * u, 2)],
                                              pT[0:m, 0, n * NH:(n + 1) * NH].rearrange("p (g r) -> p g r", g=NKV),
                                              AX, ALU.add))
            else:
                dve.tensor_copy(long.oT[:, x, ds(b * 8 + 8 * u, 8)], psum[0:HD, 7, 0:NH]).then_inc(b_dve, 1)

        dve.sem_inc(c_dve, 1)
        dve.sem_inc(o_dve, 1)
        dve.sem_inc(b_dve, 1)
        with dve.Fori(0, DB // 2) as pair:
            b = pair * 2
            own.enter(pair, 12)
            rows_in(b, 0, range(0, JP, 2))
            for u in range(2):
                dve.tensor_copy(q8[:, u, :], long.q8[:, ds(b + u, 1), :].rearrange("p a h -> p (a h)")
                                ).then_inc(q_staged, 1)
            for s in range(8):
                if s < 6:
                    rows_in(b, s // 2 + 1, range(4 * (s % 2), 4 * (s % 2) + 4, 2))
                if s:
                    output(b, s - 1)
                for kind, u, i in PLAN[s]:
                    use(b, kind, u, i)
            output(b, 7)
            for kind, u, i in PLAN[8]:
                use(b, kind, u, i)
        own.leave(DB // 2)
        dve.wait_ge(o_made, 2 * DB + 1)
        own.did(dve.tensor_copy(long.kcp[:, :], psum[:, 6, 0:PCMP]))
        own.did(dve.tensor_copy(long.vcp[:, :], psum[0:PCMP, 6, P:2 * P]))


def select(nc, ctx, io, psum, long, ahead):
    def sb(name, shape, dt=F32):
        return ctx.enter_context(nc.sbuf_tensor(name, shape, dt))

    def sem(name):
        return ctx.enter_context(nc.semaphore(name))

    R = DB * NKV
    imp = sb("imp", [R, 62])
    rest_ = sb("imp_rest", [R, 62])
    top = sb("top", [R, 2, 8])
    at = sb("at", [R, 2, 8], U32)
    blk_i = sb("blk_i", [R, 16], I32)
    page_i = sb("page_i", [R, 16], I32)
    blk = sb("blk", [R, 16])
    page = sb("page", [R, 16])
    is62 = sb("is62", [R, 16])
    hot = sb("hot", [R, 16, PAGES])
    row = sb("row", [R, 16])
    rowT = sb("rowT", [16, R])
    tab_i = sb("tab_i", [DB, PAGES], I32)
    tab_f = sb("tab_f", [DB, PAGES])
    tabs = sb("tabs", [R, PAGES])
    sel_pair = sb("sel_pair_c", [P, io.cC.shape[1]])
    spread = sb("spread", [P, 8 * R])
    table_loaded, pair_loaded = sem("table_loaded"), sem("pair_loaded")
    made, read = sem("s_made"), sem("s_read")
    own_dve = sem("own_dve_c")
    block = ctx.enter_context(nc.Block())
    c0 = long.c0

    @block.sync
    def _(sp):
        sp.dma_start(tab_i[:, :], io.page_table).then_inc(table_loaded, 16)
        sp.dma_start(sel_pair[:, :], io.cC).then_inc(pair_loaded, 16)
        hankel = bass.AP(io.vhan.tensor, 0, [[1, P], [HCOLS, NH], [1, HW]])
        sp.dma_start(ahead.skew, hankel).then_inc(ahead.skew_loaded, 16)

    @block.tensor
    def _(pe):
        for n in range(2):
            m = P if n == 0 else NCMP - P
            last = pe.matmul(psum[0:R, 0, 0:65], long.pgT[0:m, n, :], c0("shared")[0:m, n * 65:(n + 1) * 65],
                             start=n == 0, stop=n == 1)
        last.then_inc(made, 1)
        pe.wait_ge(read, 1)
        pe.matmul(psum[0:R, 1, 0:PAGES], c0("rep_bg", DB), tab_f[:, :], start=True, stop=True).then_inc(made, 1)
        pe.wait_ge(read, 2)
        pe.transpose(psum[0:16, 2, 0:R], row[:, :], c0("ident", R)[:, 0:R])
        for b in range(DB):
            last = pe.matmul(psum[0:NH, 3, b * 16:(b + 1) * 16], c0("sel_b", R)[:, b * NH:(b + 1) * NH],
                             is62[:, :], start=True, stop=True)
        last.then_inc(made, 1)
        pe.wait_ge(read, 3)
        pe.wait_ge(pair_loaded, 16)
        for j in range(8):
            last = pe.matmul(psum[:, 4, j * R:(j + 1) * R], sel_pair[0:16, j * P:(j + 1) * P], rowT[:, :],
                             start=True, stop=True)
        last.then_inc(made, 1)

    @block.vector
    def _(dve):
        own = Own(dve, own_dve)

        def then(instruction):
            own.did(instruction)
            own.settle()

        dve.wait_ge(table_loaded, 16)
        dve.tensor_copy(tab_f[:, :], tab_i[:, :]).then_inc(read, 1)
        dve.wait_ge(made, 1)
        then(dve.tensor_copy(imp[:, :], psum[0:R, 0, 1:63]))
        then(dve.max(top[:, 0, :], imp[:, :]))
        then(dve.max_index(at[:, 0, :], top[:, 0, :], imp[:, :]))
        then(dve.match_replace(rest_[:, :], top[:, 0, :], imp[:, :], NEG))
        then(dve.max(top[:, 1, :], rest_[:, :]))
        then(dve.max_index(at[:, 1, :], top[:, 1, :], rest_[:, :]))
        own.did(dve.tensor_copy(blk_i[:, 0:8], at[:, 0, :]))
        then(dve.tensor_copy(blk_i[:, 8:16], at[:, 1, :]))
        then(dve.tensor_copy(blk[:, :], blk_i[:, :]))
        then(dve.tensor_scalar(blk[:, :], blk[:, :], 1.0, None, ALU.add))
        own.did(dve.memset(blk[:, TOPB:TOPB + 1], 0.0))
        own.did(dve.memset(blk[:, TOPB + 1:TOPB + 2], 63.0))
        then(dve.memset(blk[:, TOPB + 2:TOPB + 3], 0.0))
        then(dve.tensor_copy(blk_i[:, :], blk[:, :]))
        then(dve.tensor_scalar(page_i[:, :], blk_i[:, :], 1, None, ALU.logical_shift_right))
        own.did(dve.tensor_scalar(is62[:, :], blk[:, :], 62.0, None, ALU.is_equal))
        then(dve.tensor_copy(page[:, :], page_i[:, :]))
        then(dve.tensor_tensor(hot[:, :, :], c0("iota", R)[:, 0:PAGES].unsqueeze(1).to_broadcast([R, 16, PAGES]),
                               page[:, :].unsqueeze(2).to_broadcast([R, 16, PAGES]), ALU.is_equal))
        dve.wait_ge(made, 2)
        then(dve.tensor_copy(tabs[:, :], psum[0:R, 1, 0:PAGES]))
        then(dve.tensor_tensor(hot[:, :, :], hot[:, :, :],
                               tabs[:, :].unsqueeze(1).to_broadcast([R, 16, PAGES]), ALU.mult))
        then(dve.tensor_reduce(row[:, :], hot[:, :, :], AX, ALU.add))
        then(dve.tensor_tensor(row[:, :], row[:, :], page[:, :], ALU.subtract))
        then(dve.tensor_scalar(row[:, :], row[:, :], 2.0, None, ALU.mult))
        then(dve.tensor_tensor(row[:, :], row[:, :], blk[:, :], ALU.add))
        dve.tensor_scalar(row[:, :], row[:, :], 2.0 * SLC, None, ALU.mult).then_inc(read, 1)
        dve.wait_ge(made, 3)
        own.did(dve.tensor_copy(long.flag62[:, :, :], psum[0:NH, 3, 0:DB * 16].rearrange("p (b s) -> p b s", s=16)))
        dve.tensor_copy(rowT[:, :], psum[0:16, 2, 0:R]).then_inc(read, 1)
        dve.wait_ge(made, 4)
        then(dve.tensor_copy(spread[:, :], psum[:, 4, 0:8 * R]))
        own.did(dve.tensor_scalar(long.sel_idx[:, :, :].rearrange("p r j -> p j r"),
                                  spread[:, :].rearrange("p (j r) -> p j r", r=R),
                                  c0("pos64"), None, ALU.add))


def attend(nc, ctx, io, psum, long, ahead):
    def sb(name, shape, dt=F32):
        return ctx.enter_context(nc.sbuf_tensor(name, shape, dt))

    def sem(name):
        return ctx.enter_context(nc.semaphore(name))

    ITEMS = NKV * QT
    RING = 4
    HALVES = DB // RING
    HEADS = GQ // HALVES
    skew = ahead.skew
    qs = sb("qs", [P, SEQ])
    bs = sb("bs", [P, NKV, 2 * P])
    bc = sb("bc", [P, NKV, QT, PCMP])
    pr = ahead.xa[:, 0:2, :].rearrange("p i (x k) -> p i x k", x=2)
    prT = ahead.xa[:, 2:4, :].rearrange("p i (x k) -> p i x k", x=2)
    pc = sb("pc", [P, ITEMS, 32])
    pcT = sb("pcT", [PCMP, ITEMS, P])
    cst = sb("st_c", [P, 4, ITEMS])
    st = sb("st_p", [P, 4, 2, 4])
    sel = sb("sel", [P, RING, NKV, 8, 2 * KVW])
    sel_stage = sb("sel_stage", [P, RING, NKV * 8], I32)
    apart = sb("apart_d", [P, 1])
    part = sb("part_d", [P, 2, HD])
    ksT = sb("ksT", [P, 2, 1024])
    q8 = sb("q8_d", [P, 2, NH])
    sc = sb("sc_d", [NH, 2, 1024])
    pT = sb("pT_d", [P, 2, 8 * NH])
    ss = sb("ss_d", [NH, 2, 4])
    ident = long.c0("ident")

    staged_q = sem("staged_q")
    s_made, s_max, s_exp = sem("s_scores"), sem("s_max"), sem("s_exp")
    cs_made, cs_shifted, cs_exp, cs_prob = sem("cs_made"), sem("cs_shifted"), sem("cs_exp"), sem("cs_prob")
    ct_made, ct_act, ct_dve = sem("ct_made"), sem("ct_act"), sem("ct_dve")
    t_made, t_act, t_dve = sem("t_made"), sem("t_act"), sem("t_dve")
    o_made, o_read = sem("o_made_d"), sem("o_read_d")
    gathered = [sem(f"sel_gathered{s}") for s in range(RING)]
    fresh_in = [sem(f"sel_fresh{s}") for s in range(RING)]
    staged = sem("sel_staged")
    k_made, k_act, k_dve = sem("k_made"), sem("k_act"), sem("k_dve")
    q_staged = sem("sel_q")
    y_made, y_biased, y_max, y_exp, y_prob = sem("y_made"), sem("y_biased"), sem("y_max"), sem("y_exp"), sem("y_prob")
    p_made, p_read = sem("p_made"), sem("p_read")
    v_made, v_read = sem("v_made"), sem("v_read")
    g_made = sem("g_made")
    own_dve = sem("own_dve_d")
    block = ctx.enter_context(nc.Block())

    def item(n):
        return n // QT, n % QT, P * (n % QT + 1)

    @block.sync
    def _(sp):
        for b in range(RING):
            for g in range(NKV):
                sp.dma_start(sel[SLC:SLC + 1, b, g, 7, :], io.fresh[b:b + 1, 2 * KVW:4 * KVW]).then_inc(fresh_in[b], 16)
        for b in range(RING, DB):
            sp.wait_ge(v_made, b - RING + 2)
            for g in range(NKV):
                sp.dma_start(sel[SLC:SLC + 1, b - RING, g, 7, :], io.fresh[b:b + 1, 2 * KVW:4 * KVW]
                             ).then_inc(fresh_in[b - RING], 16)
        sp.wait_ge(o_read, GQ * ITEMS + 1)
        for t in range(TT):
            src = io.x_prompt[0, t * P:(t + 1) * P, :] if t < QT else io.x_sample[:, 0, :]
            sp.dma_start(ahead.xa[0:(P if t < QT else DB), t, :], src).then_inc(ahead.x_in[t], 16)
        w = io.w_out.rearrange("(k p) n -> p k n", p=P)
        for h in range(4):
            k = (2 * h + CT) % KT
            sp.dma_start(ahead.w_out[:, k:k + 2, :], w[:, k:k + 2, :]).then_inc(
                ahead.wo_z_in if h < 2 else ahead.wo_o_in, 16)

    @block.gpsimd
    def _(pool):
        with pool.Fori(0, DB // RING) as four:
            for s in range(RING):
                pool.wait_ge(v_made, four * (s + 1) + 1)
                pool.tensor_copy(sel_stage[:, s, :], long.sel_idx[:, ds(four * 2 * RING + 2 * s, 2), :].rearrange(
                    "p r j -> p (r j)")).then_inc(staged, 1)
                pool.wait_ge(staged, four * RING + s + 1)
                pool.tensor_tensor(apart[:, 0:1], long.consts[:, 0:1], long.consts[:, 1:2], ALU.add)
                for g in range(NKV):
                    for j in range(8):
                        m = P if j < 7 else SLC
                        pool.indirect_dma_start(
                            sel[0:m, s, g, j, :], None, io.cache_rows,
                            bass.IndirectOffsetOnAxis(ap=sel_stage[0:m, s, g * 8 + j:g * 8 + j + 1], axis=0)
                        ).then_inc(gathered[s], 16)

    @block.tensor
    def _(pe):
        pe.sem_inc(v_made, 1)
        pe.sem_inc(o_made, 1)
        def scores(r, n):
            g, t, w = item(n)
            rows = slice(g * HD, (g + 1) * HD)
            for x in range(2):
                last = pe.matmul(psum[:, 2 * (n % 2) + x, 0:w], qs[rows, t * P:(t + 1) * P],
                                 long.kT[rows, x, 0:w], start=True, stop=True)
            last.then_inc(s_made, 1)

        def compressed_scores(r):
            for n in range(ITEMS):
                g, t, w = item(n)
                rows = slice(g * HD, (g + 1) * HD)
                last = pe.matmul(psum[:, 4 + g, t * 32:t * 32 + PCMP], qs[rows, t * P:(t + 1) * P], long.kcp[rows, :],
                                 start=True, stop=True)
            last.then_inc(cs_made, 1)

        def compressed_transposes(r):
            pe.wait_ge(cs_prob, r + 1)
            for n in range(ITEMS):
                out, p = psum[0:PCMP, 4 + n // QT, (n % QT) * P:(n % QT + 1) * P], pc[:, n, 0:PCMP]
                if n == 0:
                    last = pe.matmul(out, p, ident, start=True, stop=True)
                else:
                    last = pe.transpose(out, p, ident)
            last.then_inc(ct_made, 1)

        def transposes(r, n):
            g, t, w = item(n)
            if n == 0:
                pe.wait_ge(ct_act, r + 1)
            pe.wait_ge(s_exp, r * ITEMS + n + 1)
            for x in range(2):
                for k in range(t + 1):
                    out, p = psum[:, 5 + x, k * P:(k + 1) * P], pr[:, n % 2, x, k * P:(k + 1) * P]
                    if x == 0 and k == 0:
                        last = pe.matmul(out, p, ident, start=True, stop=True)
                    else:
                        last = pe.transpose(out, p, ident)
            last.then_inc(t_made, 1)

        def values(r, n):
            g, t, w = item(n)
            if n == 0:
                pe.wait_ge(ct_dve, r + 1)
            pe.wait_ge(t_act, r * ITEMS + n + 1)
            pe.wait_ge(t_dve, r * ITEMS + n + 1)
            if n:
                pe.wait_ge(o_read, r * ITEMS + n)
            bank = 4 if n % 2 else 7
            for x in range(2):
                col = (3 + 2 * x) * KVW + g * HD
                for k in range(t + 1):
                    pe.matmul(psum[:, bank, x * HD:(x + 1) * HD], prT[:, n % 2, x, k * P:(k + 1) * P],
                              long.kvtok[:, k, col:col + HD], start=k == 0, stop=k == t)
            pe.matmul(psum[:, bank, 2 * HD:3 * HD], pcT[:, n, :], long.vcp[:, g * HD:(g + 1) * HD],
                      start=True, stop=True).then_inc(o_made, 1)

        def keys(half, s):
            pe.wait_ge(gathered[s], half * 256 + 256)
            pe.wait_ge(fresh_in[s], half * 32 + 32)
            for g in range(NKV):
                for h in range(2):
                    if s:
                        pe.wait_ge(k_act if h else k_dve, half * 2 * RING + 2 * s + g - 1)
                    for j in range(4):
                        m = P if 4 * h + j < 7 else SLC + 1
                        last = pe.transpose(psum[:, 2 * h + g, j * P:j * P + m],
                                            sel[0:m, s, g, 4 * h + j, 0:KVW], ident[0:m, 0:m])
                    last.then_inc(k_made, 1)

        def sample_scores(half, s):
            pe.wait_ge(k_act, half * 2 * RING + 2 * s + 2)
            pe.wait_ge(k_dve, half * 2 * RING + 2 * s + 2)
            pe.wait_ge(q_staged, half * RING + s + 1)
            if s:
                pe.wait_ge(y_biased, half * RING + s)
            pe.matmul(psum[0:NH, 4, :], q8[:, s % 2, :], ksT[:, s % 2, 0:512], start=True, stop=True)
            pe.matmul(psum[0:NH, 5, 0:SELK - 512], q8[:, s % 2, :], ksT[:, s % 2, 512:SELK],
                      start=True, stop=True).then_inc(y_made, 1)

        def sample_values(half, s):
            pe.wait_ge(y_prob, half * RING + s + 1)
            if s:
                pe.wait_ge(p_read, half * RING + s)
            for j in range(8):
                m = P if j < 7 else SLC + 1
                out, p = psum[0:m, 6, j * NH:(j + 1) * NH], sc[:, s % 2, j * P:j * P + m]
                if j == 0:
                    last = pe.matmul(out, p, ident[0:NH, 0:NH], start=True, stop=True)
                else:
                    last = pe.transpose(out, p, ident[0:NH, 0:NH])
            last.then_inc(p_made, 1)
            pe.wait_ge(p_read, half * RING + s + 1)
            if s:
                pe.wait_ge(v_read, half * RING + s)
            for g in range(NKV):
                for j in range(8):
                    m = P if j < 7 else SLC + 1
                    last = pe.matmul(psum[0:HD, 7, g * GQ:(g + 1) * GQ],
                                     sel[0:m, s, g, j, KVW + g * HD:KVW + (g + 1) * HD],
                                     pT[0:m, s % 2, j * NH + g * GQ:j * NH + (g + 1) * GQ], start=j == 0, stop=j == 7)
            last.then_inc(v_made, 1)

        with pe.Fori(0, HALVES) as half:
            with pe.Fori(0, HEADS) as q:
                r = half * HEADS + q
                pe.wait_ge(staged_q, r + 1)
                pe.wait_ge(o_read, r * ITEMS + 1)
                compressed_scores(r)
                scores(r, 0)
                scores(r, 1)
                compressed_transposes(r)
                for n in range(ITEMS):
                    transposes(r, n)
                    if n + 2 < ITEMS:
                        scores(r, n + 2)
                    values(r, n)
            pe.wait_ge(o_read, half * HEADS * ITEMS + HEADS * ITEMS + 1)
            for s in range(RING + 1):
                if s < RING:
                    keys(half, s)
                    sample_scores(half, s)
                if s:
                    sample_values(half, s - 1)
            pe.wait_ge(v_read, half * RING + RING)
        for x in range(3):
            for h in range(NH):
                last = pe.transpose(psum[0:DB, x, h * HD:(h + 1) * HD], long.oT[:, x, h::NH], ident[0:HD, 0:HD])
        last.then_inc(g_made, 1)

    @block.scalar
    def _(act):
        def exps(r, n):
            g, t, w = item(n)
            act.wait_ge(s_max, r * ITEMS + n + 1)
            for x in range(2):
                last = act.activation(pr[:, n % 2, x, 0:w], psum[:, 2 * (n % 2) + x, 0:w], ACT.Exp,
                                      bias=st[:, n % 4, x, 0:1], accum_out=st[:, n % 4, x, 1:2])
            last.then_inc(s_exp, 1)

        def rows_in(r, n):
            g, t, w = item(n)
            act.wait_ge(t_made, r * ITEMS + n + 1)
            act.copy(prT[:, n % 2, 0, 0:w], psum[:, 5, 0:w]).then_inc(t_act, 1)

        with act.Fori(0, HALVES) as half:
            with act.Fori(0, HEADS) as q:
                r = half * HEADS + q
                act.wait_ge(o_made, r * ITEMS + 1)
                act.copy(qs[:, :], long.qT[:, ds(r, 1), 0:SEQ].rearrange("p a n -> p (a n)")).then_inc(staged_q, 1)
                act.wait_ge(cs_shifted, r + 1)
                act.activation(pc[:, :, 0:PCMP], pc[:, :, 0:PCMP], ACT.Exp).then_inc(cs_exp, 1)
                exps(r, 0)
                act.wait_ge(ct_made, r + 1)
                act.copy(pcT[:, QT:ITEMS, :].rearrange("p n q -> p (n q)"), psum[0:PCMP, 5, :]).then_inc(ct_act, 1)
                for n in range(ITEMS):
                    if n + 1 < ITEMS:
                        exps(r, n + 1)
                    rows_in(r, n)
            for s in range(RING):
                for g in range(NKV):
                    rows = slice(g * HD, (g + 1) * HD)
                    act.wait_ge(k_made, half * 4 * RING + 4 * s + 2 * g + 2)
                    act.copy(ksT[rows, s % 2, 512:SELK], psum[rows, 2 + g, 0:SELK - 512]).then_inc(k_act, 1)
                act.wait_ge(y_max, half * RING + s + 1)
                act.activation(sc[:, s % 2, 0:SELK], sc[:, s % 2, 0:SELK], ACT.Exp, bias=ss[:, s % 2, 0:1],
                               accum_out=ss[:, s % 2, 1:2]).then_inc(y_exp, 1)

    @block.vector
    def _(dve):
        own = Own(dve, own_dve)
        dve.sem_inc(o_read, 1)
        dve.wait_ge(ahead.skew_loaded, 16)

        def compressed_shift(r):
            dve.wait_ge(cs_made, r + 1)
            c = pc[:, :, 0:PCMP]
            then(dve.tensor_tensor(c.rearrange("p (g t) c -> p g t c", g=NKV),
                                   psum[:, 4:6, 0:QT * 32].rearrange("p g (t c) -> p g t c", c=32)[:, :, :, 0:PCMP],
                                   bc[:, :, :, :], ALU.add))
            then(dve.tensor_reduce(cst[:, 0, :], c, AX, ALU.max, negate=True))
            then(dve.tensor_scalar(cst[:, 0, :], cst[:, 0, :], -0.1 * NEG, None, ALU.min))
            dve.tensor_tensor(c, c, cst[:, 0, :].unsqueeze(2).to_broadcast([P, ITEMS, PCMP]), ALU.add
                              ).then_inc(cs_shifted, 1)

        def compressed_weights(r):
            c = pc[:, :, 0:PCMP]
            dve.wait_ge(cs_exp, r + 1)
            then(dve.tensor_reduce(cst[:, 1, :], c, AX, ALU.add))
            then(dve.tensor_scalar(cst[:, 1, :], cst[:, 1, :], 0.5, None, ALU.max))
            then(dve.reciprocal(cst[:, 2, :], cst[:, 1, :]))
            for g in range(NKV):
                own.did(dve.tensor_tensor(cst[:, 3, g * QT:(g + 1) * QT].unsqueeze(2),
                                          cst[:, 2, g * QT:(g + 1) * QT].unsqueeze(2),
                                          long.gates[:, 0:QT, ds(r * 3 + g * GQ * 3, 1)], ALU.mult))
            own.settle()
            dve.tensor_tensor(c, c, cst[:, 3, :].unsqueeze(2).to_broadcast([P, ITEMS, PCMP]), ALU.mult
                              ).then_inc(cs_prob, 1)

        def compressed_in(r):
            dve.wait_ge(ct_made, r + 1)
            dve.tensor_copy(pcT[:, 0:QT, :].rearrange("p n q -> p (n q)"), psum[0:PCMP, 4, :]).then_inc(ct_dve, 1)

        def biases(r, n):
            g, t, w = item(n)
            banks = psum[:, 2 * (n % 2):2 * (n % 2) + 2, :]
            dve.wait_ge(s_made, r * ITEMS + n + 1)
            v = min(w, 2 * P)
            then(dve.tensor_tensor(banks[:, :, w - v:w], banks[:, :, w - v:w],
                                   bs[:, g, 2 * P - v:2 * P].unsqueeze(1).to_broadcast([P, 2, v]), ALU.add))
            dve.tensor_reduce(st[:, n % 4, :, 0:1], banks[:, :, 0:w], AX, ALU.max, negate=True).then_inc(s_max, 1)

        def rows_in(r, n):
            g, t, w = item(n)
            dve.wait_ge(t_made, r * ITEMS + n + 1)
            dve.tensor_copy(prT[:, n % 2, 1, 0:w], psum[:, 6, 0:w]).then_inc(t_dve, 1)

        def merge(r, n):
            g, t, w = item(n)
            s, k = r * ITEMS + n, n % 4
            dve.wait_ge(s_exp, s + 1)
            then(dve.reciprocal(st[:, k, :, 3:4], st[:, k, :, 1:2]))
            then(dve.tensor_tensor(st[:, k, :, 2:3], st[:, k, :, 3:4],
                                   long.gates[:, t, ds(r * 3 + g * GQ * 3 + 1, 2)].unsqueeze(2), ALU.mult))
            dve.wait_ge(o_made, s + 2)
            out = long.otok[:, t, ds(r * HD + g * GQ * HD, HD)]
            bank = psum[:, 4 if n % 2 else 7, :]
            then(dve.tensor_scalar(part[:, 0, :], bank[:, 0:HD], st[:, k, 0, 2:3], None, ALU.mult))
            then(dve.scalar_tensor_tensor(part[:, 1, :], bank[:, HD:2 * HD], st[:, k, 1, 2:3], part[:, 0, :],
                                          ALU.mult, ALU.add))
            dve.tensor_tensor(out, bank[:, 2 * HD:3 * HD], part[:, 1, :], ALU.add).then_inc(o_read, 1)

        def then(instruction):
            own.did(instruction)
            own.settle()

        def score_biases(half, i):
            s = sc[:, i % 2, :]
            then(dve.tensor_tensor(
                s[:, 0:1024].rearrange("p (k n) -> p k n", n=SLC),
                long.flag62[:, ds(half * RING + i, 1), :].rearrange("p a k -> p (a k)").unsqueeze(2).to_broadcast([NH, 16, SLC]),
                long.b_cs[:, NCMP + SLC:NCMP + 2 * SLC].unsqueeze(1).to_broadcast([NH, 16, SLC]), ALU.mult))
            own.did(dve.tensor_copy(s[:, 14 * SLC:15 * SLC], long.b_cs[:, NCMP:NCMP + SLC]))
            then(dve.tensor_copy(s[:, SELK - 1:SELK], long.b_cs[:, NCMP + 2 * SLC:NCMP + 2 * SLC + 1]))

        def probabilities_in(half, i):
            dve.wait_ge(p_made, half * RING + i + 1)
            own.did(dve.tensor_copy(pT[:, i % 2, 0:7 * NH], psum[:, 6, 0:7 * NH]))
            dve.tensor_copy(pT[0:SLC + 1, i % 2, 7 * NH:], psum[0:SLC + 1, 6, 7 * NH:8 * NH]).then_inc(p_read, 1)

        def outputs_in(half, i):
            dve.wait_ge(v_made, half * RING + i + 2)
            dve.tensor_copy(long.oT[:, 2, ds(half * RING * NH + i * NH, NH)], psum[0:HD, 7, 0:NH]).then_inc(v_read, 1)

        start = own.n
        PER_HEAD = NKV * (1 + QT) + 3 + 5 + ITEMS * (1 + 4)
        PER_SAMPLE = 3 + 1 + 1 + 1
        PER_HALF = HEADS * PER_HEAD + RING * PER_SAMPLE
        with dve.Fori(0, HALVES) as half:
            with dve.Fori(0, HEADS) as q:
                r = half * HEADS + q
                own.turn = half * PER_HALF + q * PER_HEAD
                dve.wait_ge(o_read, r * ITEMS + 1)
                for g in range(NKV):
                    head = skew[:, ds(r + g * GQ, 1), :].rearrange("p a y -> p (a y)")
                    own.did(dve.tensor_copy(bs[:, g, ::-1], head[:, 384:640]))
                    for t in range(QT):
                        first = 480 + P * t
                        own.did(dve.tensor_copy(bc[:, g, t, ::-1], head[:, first - 16 * (PCMP - 1):first + 1:16]))
                own.settle()
                compressed_shift(r)
                biases(r, 0)
                compressed_weights(r)
                biases(r, 1)
                compressed_in(r)
                for n in range(ITEMS):
                    rows_in(r, n)
                    if n + 2 < ITEMS:
                        biases(r, n + 2)
                    merge(r, n)
            assert own.n == start + PER_HEAD
            own.turn, own.n = half * PER_HALF + (HEADS - 1) * PER_HEAD, start + PER_HEAD
            for i in range(RING):
                s = sc[:, i % 2, :]
                dve.tensor_copy(q8[:, i % 2, :], long.q8[:, ds(half * RING + i, 1), :].rearrange("p a n -> p (a n)")).then_inc(q_staged, 1)
                score_biases(half, i)
                for g in range(NKV):
                    rows = slice(g * HD, (g + 1) * HD)
                    dve.wait_ge(k_made, half * 4 * RING + 4 * i + 2 * g + 1)
                    dve.tensor_copy(ksT[rows, i % 2, 0:512], psum[rows, g, :]).then_inc(k_dve, 1)
                dve.wait_ge(y_made, half * RING + i + 1)
                own.did(dve.tensor_tensor(s[:, 0:512], psum[0:NH, 4, :], s[:, 0:512], ALU.add))
                dve.tensor_tensor(s[:, 512:SELK], psum[0:NH, 5, 0:SELK - 512], s[:, 512:SELK], ALU.add
                                  ).then_inc(y_biased, 1)
                if i:
                    probabilities_in(half, i - 1)
                own.settle()
                dve.wait_ge(y_biased, half * RING + i + 1)
                dve.tensor_reduce(ss[:, i % 2, 0:1], s[:, 0:SELK], AX, ALU.max, negate=True).then_inc(y_max, 1)
                dve.wait_ge(y_exp, half * RING + i + 1)
                then(dve.reciprocal(ss[:, i % 2, 2:3], ss[:, i % 2, 1:2]))
                dve.tensor_scalar(s[:, 0:SELK], s[:, 0:SELK], ss[:, i % 2, 2:3], None, ALU.mult).then_inc(y_prob, 1)
                if i:
                    outputs_in(half, i - 1)
            probabilities_in(half, RING - 1)
            outputs_in(half, RING - 1)
            assert own.n == start + PER_HEAD + RING * PER_SAMPLE
        own.turn, own.n = None, start + HALVES * PER_HALF
        dve.wait_ge(g_made, 1)
        out = long.otok[0:DB, QT, :].rearrange("p (h d) -> p h d", d=HD)
        gates = long.gates[0:DB, QT, :].rearrange("p (h x) -> p h x", x=3)
        tmp = qs[0:DB, :].rearrange("p (h d) -> p h d", d=HD)
        for x, gate in enumerate((0, 2, 1)):
            own.did(dve.tensor_tensor(out if x == 0 else tmp, psum[0:DB, x, :].rearrange("p (h d) -> p h d", d=HD),
                                      gates[:, :, gate:gate + 1].to_broadcast([DB, NH, HD]), ALU.mult))
            own.settle()
            if x:
                own.did(dve.tensor_tensor(out, out, tmp, ALU.add))
                own.settle()


def mix(nc, ctx, io, psum, long, ahead):
    def sb(name, shape, dt=F32):
        return ctx.enter_context(nc.sbuf_tensor(name + "_mix", shape, dt))

    def sem(name):
        return ctx.enter_context(nc.semaphore(name + "_mix"))

    LOG = NG + EX
    w_out, xa = ahead.w_out, ahead.xa
    zg = sb("zg", [P, CT, TOK])
    zsq = sb("zsq", [P, CT, TOK])
    oT = sb("oT_e", [P, 2, CT, P])
    xT = sb("xT_e", [P, KT, P])
    ln = sb("ln1", [P, 2, D])
    w_r = sb("w_r", [P, KT, LOG])
    w_rg = sb("w_rg_in", [P, KT, NG])
    w_re = sb("w_re_in", [P, KT, EX])
    b_r = sb("b_r", [P, LOG])
    rms = sb("rms", [P, TT, 2])
    stats = sb("stats", [P, 2, 6])
    mv = sb("mv", [P, TT, 4])
    log = sb("log", [P, TT, LOG])
    lg8 = sb("lg8", [P, TT, 8])
    le = sb("le", [P, TT, NE])
    mul_le = sb("mul_le", [P, NE, NG])
    top_g = sb("top_g", [P, TT, 8])
    at_g = sb("at_g", [P, TT, 8], U32)
    top_e = sb("top", [P, TT, 8])
    at_e = sb("at", [P, TT, 8], U32)
    pick = sb("pick", [P, TT, 3])
    hot_g = sb("hot_g", [P, NG])
    hot = sb("hot", [P, TT, 2, EX])
    both = sb("both", [P, TT, EX])
    acc = sb("acc", [P, TT, EX])
    ranks = sb("ranks", [P, TT, 2, EX])
    place = sb("place", [P, 4, TT, 2])
    steps = sb("steps", [P, PASSES - 1])
    over = sb("over", [P, TT * 2, PASSES - 1])
    hot_pos = sb("hot_pos", [P, TT * 2, CAP])
    hot_slot = sb("hot_slot", [P, TT * 2, SLOTS])
    ex = sb("ex", [P, TT, NG + 1])
    share = sb("share", [P, TT, 2])
    junk = sb("junk", [P, TT, DG])
    rms_done = sb("rms_done", [P, 1])
    found = sb("found", [CAP, SLOTS])
    empty = sb("empty", [CAP, SLOTS])
    first = sb("first", [CAP, SLOTS])
    choice = sb("choice", [CAP, SLOTS], I32)
    count = sb("count", [1, EX + PASSES + 2])
    ident = long.c0("ident")
    consts = sb("consts", [P, io.cE.shape[1]])

    def c_e(name):
        at, full = io.where[name]
        return consts[:, at:at + full.shape[1]]

    iota = c_e("slot_iota")

    x_in, wo_z_in, wo_o_in, small_in = ahead.x_in, ahead.wo_z_in, ahead.wo_o_in, sem("small_in")
    x1_out = sem("x1_out")
    rms_clear, o_squared, z_squared = sem("rms_clear"), sem("o_squared"), sem("z_squared")
    msq, root = sem("msq"), sem("root")
    zg_made, xa_ready = sem("zg_made"), sem("xa_ready")
    ssq_made, ssq_read = sem("ssq_made"), sem("ssq_read")
    ot_made, ot_read = sem("ot_made"), sem("ot_read")
    pz_made, pz_read, po_made, po_read = sem("pz_made"), sem("pz_read"), sem("po_made"), sem("po_read")
    var_made, dev_made, norm_scale, normed = sem("var_made"), sem("dev_made"), sem("norm_scale"), sem("normed")
    x1_made = sem("x1_made")
    xt_made, xt_act, xt_dve = sem("xt_made"), sem("xt_act"), sem("xt_dve")
    log_made, log_read = sem("log_made"), sem("log_read")
    w_r_made = sem("w_r_made")
    hot_made, rank_made, rank_read = sem("hot_made"), sem("rank_made"), sem("rank_read")
    exp_asked, exp_made = sem("exp_asked"), sem("exp_made")
    slot_hot, table_made = sem("slot_hot"), sem("table_made")
    own_dve = sem("own_dve")
    block = ctx.enter_context(nc.Block())

    def rows(t):
        return P if t < QT else DB

    @block.sync
    def _(sp):
        for t in range(TT):
            sp.wait_ge(x1_made, t + 1)
            sp.dma_start(io.x1[t * P:t * P + rows(t), :], xa[0:rows(t), t, :]).then_inc(x1_out, 16)
        sp.wait_ge(x1_out, 16 * TT)

    @block.gpsimd
    def _(pool):
        def everywhere(row):
            return bass.AP(row.tensor, row.offset, [[0, P], [1, row.shape[1]]])

        pool.dma_start(consts[:, :], io.cE).then_inc(small_in, 16)
        pool.dma_start(w_rg[:, :, :], io.w_rg.rearrange("(p k) n -> p k n", k=KT)).then_inc(small_in, 16)
        pool.dma_start(w_re[:, :, :], io.w_re.rearrange("(p k) n -> p k n", k=KT)).then_inc(small_in, 16)
        pool.dma_start(b_r[:, 0:NG], everywhere(io.b_rg)).then_inc(small_in, 16)
        pool.dma_start(b_r[:, NG:LOG], everywhere(io.b_re)).then_inc(small_in, 16)
        pool.dma_start(ln[:, 0, :], everywhere(io.ln1_g)).then_inc(small_in, 16)
        pool.dma_start(ln[:, 1, :], everywhere(io.ln1_b)).then_inc(small_in, 16)

    @block.tensor
    def _(pe):
        def turn(t):
            m = rows(t)
            if t:
                pe.wait_ge(ot_read, t)
            for k in range(CT):
                last = pe.transpose(psum[:, 4, k * P:k * P + m], long.otok[0:m, t, k * P:(k + 1) * P], ident[0:m, 0:m])
            last.then_inc(ot_made, 1)

        def product(t, half, x, first, made, read):
            if t:
                pe.wait_ge(read, t)
            for n in range(2):
                for k in range(CT):
                    last = pe.matmul(psum[0:rows(t), 2 * half + n, :], x(k), w_out[:, first + k, n * 512:(n + 1) * 512],
                                     start=k == 0, stop=k == CT - 1)
            last.then_inc(made, 1)

        def transpose_x1(t):
            m = rows(t)
            pe.wait_ge(x1_made, t + 1)
            if t:
                pe.wait_ge(xt_act, t)
                pe.wait_ge(xt_dve, t)
            for k in range(KT):
                last = pe.transpose(psum[:, 6 + k // 4, (k % 4) * P:(k % 4) * P + m], xa[0:m, t, k::KT],
                                    ident[0:m, 0:m])
            last.then_inc(xt_made, 1)

        def logits(t):
            pe.wait_ge(xt_act, t + 1)
            pe.wait_ge(xt_dve, t + 1)
            if t == 0:
                pe.wait_ge(w_r_made, 1)
                pe.wait_ge(ssq_read, 1)
            else:
                pe.wait_ge(log_read, t)
                if t > 1:
                    pe.wait_ge(rank_read, t - 1)
            for k in range(KT):
                last = pe.matmul(psum[0:rows(t), 5, 0:LOG], xT[:, k, 0:rows(t)], w_r[:, k, :],
                                 start=k == 0, stop=k == KT - 1)
            last.then_inc(log_made, 1)

        def rank(t):
            m = rows(t)
            pe.wait_ge(hot_made, t + 1)
            here = psum[0:m, 5, LOG:LOG + EX]
            last = pe.matmul(here, c_e("tri")[0:m, 0:m], both[0:m, t, :], start=True, stop=t == 0)
            if t:
                last = pe.matmul(here, long.c0("ones")[:, 0:m], acc[:, t - 1, :], start=False, stop=True)
            if t == QT:
                last = pe.matmul(psum[0:1, 5, 2 * LOG:2 * LOG + EX], long.c0("ones")[:, 0:1], acc[:, t, :],
                                 start=True, stop=True)
            last.then_inc(rank_made, 1)

        def table(t):
            pe.wait_ge(slot_hot, t + 1)
            for k in range(2):
                n = 2 * t + k
                last = pe.matmul(psum[0:CAP, 4, 0:SLOTS], hot_pos[0:rows(t), n, :], hot_slot[0:rows(t), n, :],
                                 start=n == 0, stop=n == 2 * TT - 1)
            if t == QT:
                last.then_inc(table_made, 1)

        def product_z(t):
            product(t, 1, lambda k: zg[:, k, t * P:t * P + rows(t)], CT, pz_made, pz_read)

        def product_o(t):
            pe.wait_ge(ot_read, t + 1)
            product(t, 0, lambda k: oT[:, t % 2, k, 0:rows(t)], 0, po_made, po_read)

        turn(0)
        pe.wait_ge(zg_made, 1)
        pe.wait_ge(wo_z_in, 32)
        product_z(0)
        pe.wait_ge(z_squared, 1)
        for t in range(TT):
            for k in range(CT):
                last = pe.matmul(psum[0:rows(t), 5, t:t + 1], zsq[:, k, t * P:t * P + rows(t)],
                                 long.c0("ones")[:, 0:1], start=k == 0, stop=k == CT - 1)
        last.then_inc(ssq_made, 1)
        pe.wait_ge(wo_o_in, 32)
        product_o(0)
        for t in range(1, TT):
            turn(t)
            product_z(t)
            if t > 1:
                rank(t - 2)
            transpose_x1(t - 1)
            product_o(t)
            logits(t - 1)
        pe.wait_ge(ot_read, TT)
        for t in range(TT - 2):
            table(t)
        rank(TT - 2)
        transpose_x1(TT - 1)
        logits(TT - 1)
        table(TT - 2)
        rank(TT - 1)
        table(TT - 1)

    @block.scalar
    def _(act):
        def squares(t):
            m = rows(t)
            return act.activation(junk[0:m, t, :], long.otok[0:m, t, :], ACT.Square, accum_out=rms[0:m, t, 0:1])

        act.activation(zsq[:, :, :], long.zT[:, :, :], ACT.Square).then_inc(z_squared, 1)
        for t in range(TT):
            act.wait_ge(x_in[t], 16)
            act.mul(xa[0:rows(t), t, :], xa[0:rows(t), t, :], ALPHA).then_inc(xa_ready, 1)
            if t == 0:
                act.wait_ge(rms_clear, 1)
                for u in range(TT):
                    last = squares(u)
                last.then_inc(o_squared, 1)
        act.wait_ge(msq, 1)
        act.sqrt(rms[:, :, :], rms[:, :, :]).then_inc(root, 1)
        for t in range(TT):
            m = rows(t)
            act.wait_ge(var_made, t + 1)
            act.sqrt(mv[0:m, t, 2:3], mv[0:m, t, 2:3]).then_inc(dev_made, 1)
            act.wait_ge(norm_scale, t + 1)
            act.activation(xa[0:m, t, :], xa[0:m, t, :], ACT.Identity, bias=mv[0:m, t, 3:4],
                           scale=mv[0:m, t, 2:3]).then_inc(normed, 1)
            act.wait_ge(xt_made, t + 1)
            if t:
                act.wait_ge(log_made, t)
            act.copy(xT[:, 0:4, 0:m], psum[:, 6, :].rearrange("p (k n) -> p k n", n=P)[:, :, 0:m]).then_inc(xt_act, 1)
        act.wait_ge(exp_asked, 1)
        act.activation(ex[:, :, :], ex[:, :, :], ACT.Exp).then_inc(exp_made, 1)

    @block.vector
    def _(dve):
        own = Own(dve, own_dve)

        def then(instruction):
            own.did(instruction)
            own.settle()

        def gains(half, n):
            return long.gains[:, half * CT:(half + 1) * CT].unsqueeze(2).to_broadcast([P, CT, n])

        def scale_o(t):
            m = rows(t)
            dve.wait_ge(ot_made, t + 1)
            if t > 1:
                dve.wait_ge(po_made, t - 1)
            dve.tensor_tensor(oT[:, t % 2, :, 0:m], psum[:, 4, :].rearrange("p (k n) -> p k n", n=P)[:, :, 0:m],
                              gains(0, m), ALU.mult).then_inc(ot_read, 1)

        def transposed(t):
            dve.wait_ge(xt_made, t + 1)
            if t:
                dve.wait_ge(log_made, t)
            dve.tensor_copy(xT[:, 4:8, 0:rows(t)], psum[:, 7, :].rearrange("p (k n) -> p k n", n=P)[:, :, 0:rows(t)]
                            ).then_inc(xt_dve, 1)

        def route(t):
            m = rows(t)
            dve.wait_ge(log_made, t + 1)
            dve.tensor_tensor(log[0:m, t, :], psum[0:m, 5, 0:LOG], b_r[0:m, :], ALU.add).then_inc(log_read, 1)
            dve.wait_ge(log_read, t + 1)
            then(dve.tensor_copy(lg8[0:m, t, 0:NG], log[0:m, t, 0:NG]))
            then(dve.max(top_g[0:m, t, :], lg8[0:m, t, :]))
            then(dve.max_index(at_g[0:m, t, :], top_g[0:m, t, :], lg8[0:m, t, :]))
            then(dve.tensor_copy(pick[0:m, t, 0:1], at_g[0:m, t, 0:1]))
            then(dve.tensor_scalar(hot_g[0:m, :], iota[0:m, 0:NG], pick[0:m, t, 0:1], None, ALU.is_equal))
            then(dve.tensor_tensor(mul_le[0:m, :, :],
                                   log[0:m, t, NG:LOG].rearrange("p (g e) -> p e g", e=NE),
                                   hot_g[0:m, :].unsqueeze(1).to_broadcast([m, NE, NG]), ALU.mult))
            then(dve.tensor_reduce(le[0:m, t, :], mul_le[0:m, :, :], AX, ALU.add))
            then(dve.max(top_e[0:m, t, :], le[0:m, t, :]))
            then(dve.max_index(at_e[0:m, t, :], top_e[0:m, t, :], le[0:m, t, :]))
            then(dve.tensor_copy(pick[0:m, t, 1:3], at_e[0:m, t, 0:2]))
            then(dve.scalar_tensor_tensor(pick[0:m, t, 1:3], pick[0:m, t, 0:1].to_broadcast([m, 2]), float(NE),
                                          pick[0:m, t, 1:3], ALU.mult, ALU.add))
            then(dve.tensor_tensor(hot[0:m, t, :, :], iota[0:m, 0:EX].unsqueeze(1).to_broadcast([m, 2, EX]),
                                   pick[0:m, t, 1:3].unsqueeze(2).to_broadcast([m, 2, EX]), ALU.is_equal))
            then(dve.tensor_tensor(both[0:m, t, :], hot[0:m, t, 0, :], hot[0:m, t, 1, :], ALU.add))
            if t == 0:
                dve.tensor_copy(acc[:, t, :], both[:, t, :]).then_inc(hot_made, 1)
            else:
                dve.tensor_tensor(acc[:, t, :], acc[:, t - 1, :], both[:, t, :], ALU.add).then_inc(hot_made, 1)

        def ranked(t):
            m = rows(t)
            dve.wait_ge(rank_made, t + 1)
            if t == QT:
                own.did(dve.tensor_copy(count[:, 0:EX], psum[0:1, 5, 2 * LOG:2 * LOG + EX]))
            dve.tensor_tensor(ranks[0:m, t, :, :], hot[0:m, t, :, :],
                              psum[0:m, 5, LOG:LOG + EX].unsqueeze(1).to_broadcast([m, 2, EX]),
                              ALU.mult).then_inc(rank_read, 1)

        def placed(t):
            m = rows(t)
            rank_, pass_, pos, slot = (place[0:m, i, t, :] for i in range(4))
            dve.wait_ge(rank_read, t + 1)
            then(dve.tensor_reduce(rank_, ranks[0:m, t, :, :], AX, ALU.add))
            then(dve.tensor_tensor(over[0:m, 2 * t:2 * t + 2, :], rank_.unsqueeze(2).to_broadcast([m, 2, PASSES - 1]),
                                   steps[0:m, :].unsqueeze(1).to_broadcast([m, 2, PASSES - 1]), ALU.is_ge))
            then(dve.tensor_reduce(pass_, over[0:m, 2 * t:2 * t + 2, :], AX, ALU.add))
            own.did(dve.scalar_tensor_tensor(pos, pass_, -float(CAP), rank_, ALU.mult, ALU.add))
            own.did(dve.scalar_tensor_tensor(slot, pass_, float(EX), pick[0:m, t, 1:3], ALU.mult, ALU.add))
            own.settle()
            for k in range(2):
                own.did(dve.tensor_scalar(hot_slot[0:m, 2 * t + k, :], iota[0:m, :], slot[:, k:k + 1],
                                          c_e("choice")[0:m, 2 * t + k:2 * t + k + 1], ALU.is_equal, ALU.mult))
            dve.tensor_tensor(hot_pos[0:m, 2 * t:2 * t + 2, :], iota[0:m, 0:CAP].unsqueeze(1).to_broadcast([m, 2, CAP]),
                              pos.unsqueeze(2).to_broadcast([m, 2, CAP]), ALU.is_equal).then_inc(slot_hot, 1)

        own.did(dve.memset(rms[:, :, :], 1.0 * DG))
        for part in (log, top_g, top_e, pick, hot, both, ranks):
            last = dve.memset(part[:, QT:TT], 0.0)
            own.did(last)
        then(dve.memset(lg8[:, :, :], NEG))
        dve.tensor_copy(rms_done[:, :], rms[:, 0, 0:1]).then_inc(rms_clear, 1)
        dve.tensor_tensor(zg[:, :, :], long.zT[:, :, :], gains(1, TOK), ALU.mult).then_inc(zg_made, 1)
        scale_o(0)
        dve.wait_ge(small_in, 112)
        own.did(dve.tensor_copy(w_r[:, :, 0:NG], w_rg[:, :, :]))
        dve.tensor_copy(w_r[:, :, NG:LOG], w_re[:, :, :]).then_inc(w_r_made, 1)
        own.did(dve.tensor_scalar(steps[:, :], iota[:, 1:PASSES], float(CAP), None, ALU.mult))
        dve.wait_ge(ssq_made, 1)
        own.did(dve.tensor_copy(rms[:, 0:QT, 1:2], psum[:, 5, 0:QT].unsqueeze(2)))
        dve.tensor_copy(rms[0:DB, QT, 1:2], psum[0:DB, 5, QT:TT]).then_inc(ssq_read, 1)
        dve.wait_ge(ssq_read, 1)
        dve.wait_ge(o_squared, 1)
        dve.tensor_scalar(rms[:, :, :], rms[:, :, :], 1.0 / DG, 1e-6, ALU.mult, ALU.add).then_inc(msq, 1)
        dve.wait_ge(root, 1)
        then(dve.reciprocal(rms[:, :, :], rms[:, :, :]))
        for t in range(TT):
            m = rows(t)
            x = xa[0:m, t, :].rearrange("p (h n) -> p h n", h=2)
            dve.wait_ge(xa_ready, t + 1)
            dve.wait_ge(pz_made, t + 1)
            dve.scalar_tensor_tensor(x, psum[0:m, 2:4, :], rms[0:m, t, 1:2], x, ALU.mult, ALU.add).then_inc(pz_read, 1)
            if t > 1:
                ranked(t - 2)
            if t:
                transposed(t - 1)
            dve.wait_ge(pz_read, t + 1)
            dve.wait_ge(po_made, t + 1)
            dve.scalar_tensor_tensor(x, psum[0:m, 0:2, :], rms[0:m, t, 0:1], x, ALU.mult, ALU.add).then_inc(po_read, 1)
            dve.wait_ge(po_read, t + 1)
            for h in range(2):
                own.did(dve.bn_stats(stats[0:m, h, :], xa[0:m, t, h * 512:(h + 1) * 512]))
            own.settle()
            then(dve.bn_aggr(mv[0:m, t, 0:2], stats[0:m, :, :]))
            dve.tensor_scalar(mv[0:m, t, 2:3], mv[0:m, t, 1:2], 1e-5, None, ALU.add).then_inc(var_made, 1)
            if t + 1 < TT:
                scale_o(t + 1)
            dve.wait_ge(dev_made, t + 1)
            then(dve.reciprocal(mv[0:m, t, 2:3], mv[0:m, t, 2:3]))
            dve.scalar_tensor_tensor(mv[0:m, t, 3:4], mv[0:m, t, 0:1], -1.0, mv[0:m, t, 2:3],
                                     ALU.mult, ALU.mult).then_inc(norm_scale, 1)
            if t:
                route(t - 1)
            if t > 1:
                placed(t - 2)
            dve.wait_ge(normed, t + 1)
            then(dve.tensor_tensor(xa[0:m, t, :], xa[0:m, t, :], ln[0:m, 0, :], ALU.mult))
            dve.tensor_tensor(xa[0:m, t, :], xa[0:m, t, :], ln[0:m, 1, :], ALU.add).then_inc(x1_made, 1)
        ranked(TT - 2)
        transposed(TT - 1)
        placed(TT - 2)
        route(TT - 1)
        ranked(TT - 1)
        placed(TT - 1)
        then(dve.tensor_reduce(count[:, EX:EX + 1], count[:, 0:EX], AX, ALU.max))
        then(dve.tensor_scalar(count[:, EX + 2:EX + 1 + PASSES], steps[0:1, :], count[:, EX:EX + 1], None, ALU.is_lt))
        then(dve.tensor_reduce(count[:, EX + 1:EX + 2], count[:, EX + 2:EX + 1 + PASSES], AX, ALU.add))
        own.did(dve.tensor_scalar(long.passes[:, 0:1], count[:, EX + 1:EX + 2], 1.0, None, ALU.add))
        own.did(dve.tensor_scalar(long.passes[:, 1:2], count[:, EX + 1:EX + 2], 1.0, float(EX // RING_EX), ALU.add, ALU.mult))
        own.did(dve.tensor_tensor(ex[:, :, 0:NG], log[:, :, 0:NG], top_g[:, :, 0:1].to_broadcast([P, TT, NG]),
                                  ALU.subtract))
        dve.tensor_tensor(ex[:, :, NG:NG + 1], top_e[:, :, 1:2], top_e[:, :, 0:1], ALU.subtract).then_inc(exp_asked, 1)
        dve.wait_ge(table_made, 1)
        then(dve.tensor_copy(found[:, :], psum[0:CAP, 4, 0:SLOTS]))
        own.did(dve.scalar_tensor_tensor(empty[:, :], found[:, :], 0.0, c_e("spare")[0:CAP, :],
                                         ALU.is_equal, ALU.mult))
        own.did(dve.tensor_scalar(first[:, :], found[:, :], 1.0, 1.0, ALU.max, ALU.subtract))
        own.settle()
        own.did(dve.scalar_tensor_tensor(long.dest[:, :], found[:, :], 1.0, empty[:, :], ALU.subtract, ALU.add))
        then(dve.tensor_copy(choice[:, :], first[:, :]))
        own.did(dve.tensor_scalar(long.table[:, 0:SLOTS], choice[:, :], 1, None, ALU.logical_shift_right))
        own.did(dve.memset(long.table[:, SLOTS:], 0))
        dve.wait_ge(exp_made, 1)
        own.did(dve.tensor_reduce(share[:, :, 0:1], ex[:, :, 0:NG], AX, ALU.add))
        own.did(dve.tensor_scalar(share[:, :, 1:2], ex[:, :, NG:NG + 1], 1.0, None, ALU.add))
        own.settle()
        then(dve.tensor_tensor(share[:, :, 0:1], share[:, :, 0:1], share[:, :, 1:2], ALU.mult))
        then(dve.reciprocal(long.weights[:, :, 0:1], share[:, :, 0:1]))
        then(dve.tensor_tensor(long.weights[:, :, 1:2], long.weights[:, :, 0:1], ex[:, :, NG:NG + 1], ALU.mult))


def experts(nc, io, psum, long, ahead):
    with ExitStack() as ctx:
        def sb(name, shape, dt=F32):
            return ctx.enter_context(nc.sbuf_tensor(name + "_exp", shape, dt))

        def sem(name):
            return ctx.enter_context(nc.semaphore(name + "_exp"))

        RING = RING_EX
        TURNS = EX // RING
        FT = FF // P
        wg = sb("wg", [P, RING, KT, FF])
        wu = sb("wu", [P, RING, KT, FF])
        wd = sb("wd", [P, RING, FT, D])
        x = sb("x", [CAP, RING, D])
        stage = sb("stage", [CAP, RING], I32)
        to = sb("to", [CAP, RING], I32)
        apart = sb("apart", [P, 2 + RING])
        xT = sb("xT", [P, KT, CAP])
        sg = sb("sg", [P, FT * CAP])
        gs = sb("gs", [P, FT * CAP])
        hT = sb("hT", [P, FT, CAP])
        y = sb("y", [CAP, RING, D])
        ident = long.c0("ident")[0:CAP, 0:CAP]
        half = KT // 2 * CAP

        w_in = [sem(f"w_in{s}") for s in range(RING)]
        x_in = [sem(f"x_in{s}") for s in range(RING)]
        staged, to_staged = sem("staged"), sem("to_staged")
        t_made = [sem(f"t_made{s}") for s in range(RING)]
        xt_act, xt_dve = sem("xt_act"), sem("xt_dve")
        gu_made, sg_made, gs_made, h_made = sem("gu_made"), sem("sg_made"), sem("gs_made"), sem("h_made")
        y_made = [sem(f"y_made{s}") for s in range(RING)]
        y_act, y_dve = sem("y_act"), sem("y_dve")
        y_free = sem("y_free")
        y_out = [sem(f"y_out{s}") for s in range(RING)]
        block = ctx.enter_context(nc.Block())

        @block.sync
        def _(sp):
            passes = sp.value_load(long.passes[0:1, 0:1], min_val=1, max_val=PASSES)
            with sp.Fori(0, passes) as p:
                with sp.Fori(0, TURNS) as turn:
                    for s in range(RING):
                        if s == 1:
                            sp.wait_ge(x_in[RING - 1], 16)
                        sp.wait_ge(y_made[s], p * TURNS + turn + 1)
                        e = turn * RING + s
                        sp.dma_start(wg[:, s, :, :], io.w_eg[ds(e, 1), :, :].rearrange("a (p k) f -> p (a k) f", k=KT)
                                     ).then_inc(w_in[s], 16)
                        sp.dma_start(wu[:, s, :, :], io.w_eu[ds(e, 1), :, :].rearrange("a (p k) f -> p (a k) f", k=KT)
                                     ).then_inc(w_in[s], 16)
                        sp.dma_start(wd[:, s, :, :], io.w_ed[ds(e, 1), :, :].rearrange("a (p j) n -> p (a j) n", j=FT)
                                     ).then_inc(w_in[s], 16)
            def everywhere(row):
                return bass.AP(row.tensor, row.offset, [[0, P], [1, row.shape[1]]])

            for t in range(TT):
                m = P if t < QT else DB
                sp.dma_start(ahead.x[0:m, t, :], io.x1[t * P:t * P + m, :]).then_inc(ahead.x_in[t], 16)
            sp.dma_start(ahead.ln[:, 0, :], everywhere(io.ln2_g)).then_inc(ahead.ln_in, 16)
            sp.dma_start(ahead.ln[:, 1, :], everywhere(io.ln2_b)).then_inc(ahead.ln_in, 16)

        @block.gpsimd
        def _(pool):
            turns = pool.value_load(long.passes[0:1, 1:2], min_val=TURNS, max_val=PASSES * TURNS)

            def fetch(s):
                pool.indirect_dma_start(x[:, s, :], None, io.x1,
                                        bass.IndirectOffsetOnAxis(ap=stage[:, s:s + 1], axis=0)).then_inc(x_in[s], 16)

            pool.tensor_copy(stage[:, :], long.table[:, 0:RING]).then_inc(staged, 1)
            pool.sem_inc(y_free, RING)
            pool.wait_ge(staged, 1)
            for s in range(RING):
                fetch(s)
            with pool.Fori(0, turns) as turn:
                for u in range(RING):
                    pool.wait_ge(t_made[u], turn + 2)
                    pool.tensor_copy(stage[:, u:u + 1], long.table[:, ds(turn * RING + u + RING, 1)]).then_inc(staged, 1)
                    pool.wait_ge(staged, turn * RING + u + 2)
                    pool.tensor_tensor(apart[:, 0:1], long.consts[:, 0:1], long.consts[:, 1:2], ALU.add)
                    fetch(u)
                    n = turn * RING + u
                    pool.tensor_copy(to[:, u:u + 1], long.dest[:, ds(n, 1)]).then_inc(to_staged, 1)
                    pool.wait_ge(to_staged, n + 1)
                    pool.wait_ge(y_act, n + 2)
                    pool.wait_ge(y_dve, n + 2)
                    pool.tensor_tensor(apart[:, 1:2], long.consts[:, 0:1], long.consts[:, 1:2], ALU.add)
                    pool.indirect_dma_start(io.yrows, bass.IndirectOffsetOnAxis(ap=to[:, u:u + 1], axis=0),
                                            y[:, u, :], None).then_inc(y_out[u], 16)
                for s in range(RING):
                    pool.wait_ge(y_out[s], turn * 16 + 16)
                    pool.tensor_tensor(apart[:, 2 + s:3 + s], long.consts[:, 0:1], long.consts[:, 1:2], ALU.add
                                       ).then_inc(y_free, 1)

        @block.tensor
        def _(pe):
            turns = pe.value_load(long.passes[0:1, 1:2], min_val=TURNS, max_val=PASSES * TURNS)

            def turned(s, fills, before):
                pe.wait_ge(x_in[s], fills * 16)
                pe.wait_ge(xt_act, before)
                pe.wait_ge(xt_dve, before)
                for k in range(KT):
                    bank, col = k // 4, (k % 4) * CAP
                    out, rows = psum[:, bank, col:col + CAP], x[:, s, k::KT]
                    if k == 0:
                        last = pe.matmul(out, rows, ident, start=True, stop=True)
                    else:
                        last = pe.transpose(out, rows, ident)
                last.then_inc(t_made[s], 1)

            for s in range(RING):
                pe.sem_inc(y_made[s], 1)
                pe.sem_inc(t_made[s], 1)
            pe.wait_ge(x_in[0], 16)
            for k in range(KT):
                last = pe.transpose(psum[:, k // 4, (k % 4) * CAP:(k % 4 + 1) * CAP], x[:, 0, k::KT], ident)
            last.then_inc(t_made[0], 1)
            with pe.Fori(0, turns) as turn:
                for s in range(RING):
                    n = turn * RING + s
                    pe.wait_ge(xt_act, n + 1)
                    pe.wait_ge(xt_dve, n + 1)
                    pe.wait_ge(w_in[s], (turn + 1) * 48)
                    for bank, w in ((2, wg), (3, wu)):
                        for j in range(FT):
                            for k in range(KT):
                                last = pe.matmul(psum[:, bank, j * CAP:(j + 1) * CAP], w[:, s, k, j::FT], xT[:, k, :],
                                                 start=k == 0, stop=k == KT - 1)
                    last.then_inc(gu_made, 1)
                    turned((s + 1) % RING, turn + 1 + (s + 1) // RING, n + 1)
                    pe.wait_ge(h_made, n + 1)
                    pe.wait_ge(y_act, n + 1)
                    pe.wait_ge(y_dve, n + 1)
                    for i in range(2):
                        for j in range(FT):
                            last = pe.matmul(psum[0:CAP, 6 + i, :], hT[:, j, :], wd[:, s, j, i * 512:(i + 1) * 512],
                                             start=j == 0, stop=j == FT - 1)
                    last.then_inc(y_made[s], 1)

        @block.scalar
        def _(act):
            turns = act.value_load(long.passes[0:1, 1:2], min_val=TURNS, max_val=PASSES * TURNS)

            def rows_in():
                act.copy(xT[:, 0:KT // 2, :].rearrange("p k n -> p (k n)"), psum[:, 0, 0:half]).then_inc(xt_act, 1)

            act.sem_inc(y_act, 1)
            act.wait_ge(t_made[0], 2)
            rows_in()
            with act.Fori(0, turns) as turn:
                for s in range(RING):
                    n = turn * RING + s
                    act.wait_ge(gu_made, n + 1)
                    act.activation(sg[:, :], psum[:, 2, 0:FT * CAP], ACT.Sigmoid).then_inc(sg_made, 1)
                    act.wait_ge(t_made[(s + 1) % RING], turn + 1 + (s + 1) // RING + 1)
                    rows_in()
                    act.wait_ge(y_made[s], turn + 2)
                    act.wait_ge(y_free, n + 1)
                    act.copy(y[:, s, 0:512], psum[0:CAP, 6, :]).then_inc(y_act, 1)
        @block.vector
        def _(dve):
            turns = dve.value_load(long.passes[0:1, 1:2], min_val=TURNS, max_val=PASSES * TURNS)

            def rows_in():
                dve.tensor_copy(xT[:, KT // 2:KT, :].rearrange("p k n -> p (k n)"), psum[:, 1, 0:half]
                                ).then_inc(xt_dve, 1)

            dve.sem_inc(y_dve, 1)
            dve.wait_ge(t_made[0], 2)
            rows_in()
            with dve.Fori(0, turns) as turn:
                for s in range(RING):
                    n = turn * RING + s
                    dve.wait_ge(sg_made, n + 1)
                    dve.tensor_tensor(gs[:, :], psum[:, 2, 0:FT * CAP], sg[:, :], ALU.mult).then_inc(gs_made, 1)
                    dve.wait_ge(gs_made, n + 1)
                    dve.tensor_tensor(hT[:, :, :].rearrange("p j n -> p (j n)"), gs[:, :], psum[:, 3, 0:FT * CAP],
                                      ALU.mult).then_inc(h_made, 1)
                    dve.wait_ge(t_made[(s + 1) % RING], turn + 1 + (s + 1) // RING + 1)
                    rows_in()
                    dve.wait_ge(y_made[s], turn + 2)
                    dve.wait_ge(y_free, n + 1)
                    dve.tensor_copy(y[:, s, 512:1024], psum[0:CAP, 7, :]).then_inc(y_dve, 1)


def finish(nc, io, psum, long, ahead):
    with ExitStack() as ctx:
        def sb(name, shape, dt=F32):
            return ctx.enter_context(nc.sbuf_tensor(name + "_fin", shape, dt))

        def sem(name):
            return ctx.enter_context(nc.semaphore(name + "_fin"))

        x, ln, x_in, ln_in = ahead.x, ahead.ln, ahead.x_in, ahead.ln_in
        y = sb("y", [P, TT, 2, D])
        stats = sb("stats", [P, 2, 6])
        mv = sb("mv", [P, TT, 4])
        last_made = sem("last_made")
        y_in = [sem(f"y_in{t}") for t in range(TT)]
        xa_ready, var_made, dev_made = sem("xa_ready"), sem("var_made"), sem("dev_made")
        norm_scale, normed, out_made, out_done = sem("norm_scale"), sem("normed"), sem("out_made"), sem("out_done")
        scaled, own_dve = sem("scaled"), sem("own_dve")
        block = ctx.enter_context(nc.Block())

        def rows(t):
            return P if t < QT else DB

        @block.sync
        def _(sp):
            rows_of = io.yrows[0:2 * TOK, :].rearrange("(t k) n -> t k n", k=2)
            for t in range(TT):
                sp.dma_start(y[0:rows(t), t, :, :], rows_of[t * P:t * P + rows(t), :, :]).then_inc(y_in[t], 16)
            for t in range(TT):
                if t < QT:
                    sp.wait_ge(out_made, t + 1)
                else:
                    sp.wait_ge(last_made, 1)
                out = io.y_prompt[t * P:(t + 1) * P, :] if t < QT else io.y_sample
                sp.dma_start(out, x[0:rows(t), t, :]).then_inc(out_done, 16)
            sp.wait_ge(out_done, 16 * TT)

        @block.gpsimd
        def _(pool):
            pool.wait_ge(ln_in, 32)
            for t in range(QT):
                m = rows(t)
                pool.wait_ge(normed, t + 1)
                pool.tensor_tensor(x[0:m, t, :], x[0:m, t, :], ln[0:m, 0, :], ALU.mult).then_inc(scaled, 1)
                pool.wait_ge(scaled, t + 1)
                pool.tensor_tensor(x[0:m, t, :], x[0:m, t, :], ln[0:m, 1, :], ALU.add).then_inc(out_made, 1)

        @block.scalar
        def _(act):
            def scale(t):
                act.wait_ge(x_in[t], 16)
                act.mul(x[0:rows(t), t, :], x[0:rows(t), t, :], ALPHA).then_inc(xa_ready, 1)

            scale(0)
            scale(1)
            for t in range(TT):
                m = rows(t)
                if t + 2 < TT:
                    scale(t + 2)
                act.wait_ge(var_made, t + 1)
                act.sqrt(mv[0:m, t, 2:3], mv[0:m, t, 2:3]).then_inc(dev_made, 1)
                act.wait_ge(norm_scale, t + 1)
                act.activation(x[0:m, t, :], x[0:m, t, :], ACT.Identity, bias=mv[0:m, t, 3:4],
                               scale=mv[0:m, t, 2:3]).then_inc(normed, 1)

        @block.vector
        def _(dve):
            own = Own(dve, own_dve)

            def then(instruction):
                own.did(instruction)
                own.settle()

            for t in range(TT):
                m = rows(t)
                dve.wait_ge(xa_ready, t + 1)
                dve.wait_ge(y_in[t], 16)
                for k in range(2):
                    then(dve.scalar_tensor_tensor(x[0:m, t, :], y[0:m, t, k, :], long.weights[0:m, t, k:k + 1],
                                                  x[0:m, t, :], ALU.mult, ALU.add))
                for h in range(2):
                    own.did(dve.bn_stats(stats[0:m, h, :], x[0:m, t, h * 512:(h + 1) * 512]))
                own.settle()
                then(dve.bn_aggr(mv[0:m, t, 0:2], stats[0:m, :, :]))
                dve.tensor_scalar(mv[0:m, t, 2:3], mv[0:m, t, 1:2], 1e-5, None, ALU.add).then_inc(var_made, 1)
                dve.wait_ge(dev_made, t + 1)
                then(dve.reciprocal(mv[0:m, t, 2:3], mv[0:m, t, 2:3]))
                dve.scalar_tensor_tensor(mv[0:m, t, 3:4], mv[0:m, t, 0:1], -1.0, mv[0:m, t, 2:3],
                                         ALU.mult, ALU.mult).then_inc(norm_scale, 1)
            dve.wait_ge(normed, TT)
            dve.wait_ge(ln_in, 32)
            then(dve.tensor_tensor(x[0:DB, QT, :], x[0:DB, QT, :], ln[0:DB, 0, :], ALU.mult))
            dve.tensor_tensor(x[0:DB, QT, :], x[0:DB, QT, :], ln[0:DB, 1, :], ALU.add).then_inc(last_made, 1)


def rest(nc, whole, attention, io, psum, long):
    def sb(stack, name, shape, dt=F32):
        return stack.enter_context(nc.sbuf_tensor(name, shape, dt))

    with attention:
        long.otok = sb(attention, "otok", [P, TT, DG])
        long.sel_idx = sb(attention, "sel_idx", [P, DB * NKV, 8], I32)
        long.flag62 = sb(attention, "flag62", [NH, DB, 16])
        ahead = Store()
        ahead.w_out = sb(attention, "w_out", [P, KT, D])
        ahead.xa = sb(attention, "xa", [P, TT, D])
        ahead.x_in = [attention.enter_context(nc.semaphore(f"mix_x_in{t}")) for t in range(TT)]
        ahead.wo_z_in = attention.enter_context(nc.semaphore("mix_wo_z_in"))
        ahead.wo_o_in = attention.enter_context(nc.semaphore("mix_wo_o_in"))
        ahead.skew = ahead.w_out[:, :, :].rearrange("p k n -> p (k n)")[:, 0:NH * HW].rearrange(
            "p (h y) -> p h y", y=HW)
        ahead.skew_loaded = attention.enter_context(nc.semaphore("skew_loaded"))
        with ExitStack() as stage:
            select(nc, stage, io, psum, long, ahead)
        with ExitStack() as stage:
            attend(nc, stage, io, psum, long, ahead)
        with ExitStack() as stage:
            mix(nc, stage, io, psum, long, ahead)
    used = sorted(nc.released_uncleared_semaphores)
    assert used == list(range(used[0], used[-1] + 1))
    with nc.Block() as block:
        @block.gpsimd
        def _(pool):
            pool.sem_clear(range(used[0], used[-1] + 1))
    with ExitStack() as tail:
        last = Store()
        last.x = sb(tail, "x_last", [P, TT, D])
        last.ln = sb(tail, "ln2", [P, 2, D])
        last.x_in = [tail.enter_context(nc.semaphore(f"last_x_in{t}")) for t in range(TT)]
        last.ln_in = tail.enter_context(nc.semaphore("last_ln_in"))
        experts(nc, io, psum, long, last)
        finish(nc, io, psum, long, last)


def hybrid_layer(nc, io):
    with ExitStack() as whole:
        def sb(stack, name, shape, dt=F32):
            return stack.enter_context(nc.sbuf_tensor(name, shape, dt))

        psum = whole.enter_context(nc.psum_tensor("psum", [P, 8, 512], F32))
        long, mid = Store(), Store()
        long.consts = sb(whole, "consts", [P, io.c0.shape[1]])
        long.zT = sb(whole, "zT", [P, CT, TOK])
        long.gains = sb(whole, "gains", [P, 2 * CT])
        long.gates = sb(whole, "gates", [P, TT, GATES])

        long.table = sb(whole, "table", [CAP, SLOTS + 4], I32)
        long.dest = sb(whole, "dest", [CAP, SLOTS], I32)
        long.weights = sb(whole, "weights", [P, TT, 2])
        long.passes = sb(whole, "passes", [1, 2], I32)

        def c0(name, rows=P):
            at, full = io.where[name]
            return long.consts[0:rows, at:at + full.shape[1]]

        long.c0 = c0
        with ExitStack() as attention:
            long.qT = sb(attention, "qT", [P, GQ, TOK])
            long.kT = sb(attention, "kT", [P, 2, TOK])
            long.kvtok = sb(attention, "kvtok", [P, TT, 6 * KVW])
            long.q8 = sb(attention, "q8", [P, DB, NH])
            long.b_win = sb(attention, "b_win", [NH, WIN])
            long.b_cs = sb(attention, "b_cs", [NH, NCMP + 129])
            long.pgT = sb(attention, "pgT", [P, 2, 16])
            long.oT = sb(attention, "oT", [HD, 3, DB * NH])
            long.kcp = sb(attention, "kcp", [P, PCMP])
            long.vcp = sb(attention, "vcp", [PCMP, KVW])
            with ExitStack() as cache:
                mid.early = sb(cache, "early", [P, TT, D])
                mid.w1 = mid.early[:, 0:QT, :].rearrange("p t n -> p (t n)").rearrange(
                    "p (n j e) -> p n j e", n=2, j=NJ)
                mid.w2 = sb(cache, "w2", [P, 2, HD])
                mid.w_loaded = cache.enter_context(nc.semaphore("cw_loaded"))
                mid.raw = sb(cache, "raw", [P, 4, STRIDE, 2 * KVW])
                mid.stage = sb(cache, "stage", [P, 4, STRIDE], I32)
                mid.idx = sb(cache, "idx", [P, 16, STRIDE], I32)
                mid.apart = sb(cache, "apart", [P, 1])
                mid.pages = sb(cache, "pages", [P, 16])
                mid.xTp = sb(cache, "xTp", [P, 4, JP, PCH])
                mid.peT = sb(cache, "peT", [P, 2 * NJ])
                mid.pe_in = sb(cache, "pe_in", [16, 2, P])
                mid.gathered = [cache.enter_context(nc.semaphore(f"gathered{s}")) for s in range(4)]
                mid.staged = cache.enter_context(nc.semaphore("staged"))

                def gather(pool, slot, half, fill):
                    pool.tensor_copy(mid.stage[:, slot, :], mid.idx[:, ds(half, 1), :].rearrange(
                        "p a j -> p (a j)")).then_inc(mid.staged, 1)
                    pool.wait_ge(mid.staged, fill + 1)
                    pool.tensor_tensor(mid.apart[:, 0:1], long.consts[:, 0:1], long.consts[:, 1:2], ALU.add)
                    for j in range(STRIDE):
                        pool.indirect_dma_start(mid.raw[:, slot, j, :], None, io.cache_rows,
                                                bass.IndirectOffsetOnAxis(ap=mid.stage[:, slot, j:j + 1], axis=0)
                                                ).then_inc(mid.gathered[slot], 16)

                mid.gather = gather
                with ExitStack() as stage:
                    project(nc, stage, io, psum, long, mid)
                with ExitStack() as stage:
                    compress(nc, stage, io, psum, long, mid)
            rest(nc, whole, attention, io, psum, long)


_OUTS = [((1, SEQ, D), "y_prompt"), ((DB, 1, D), "y_sample"),
         ((1, 1, SEQ, 4, NKV, HD), "new_kv_prompt"), ((1, DB, 1, 4, NKV, HD), "new_kv_sample"),
         ((1, 1, WIN, 2, NKV, HD), "new_win_prompt"), ((1, DB, WIN, 2, NKV, HD), "new_win_sample"),
         ((1, 1, 2, DG), "new_conv_prompt"), ((1, DB, 2, DG), "new_conv_sample")]


def declare(nc, inputs):
    io = Store()
    arrays = {}

    def give(name, a):
        arrays[f"in_{name}_dram"] = a
        return nc.dram_tensor(f"in_{name}_dram", a.shape, mybir.dt.from_np(a.dtype), kind="ExternalInput").ap()

    table = constants()

    def together(group, names):
        at = 0
        for n in names:
            table[n] = (at, table[n][1])
            at += table[n][1].shape[1]
        return give(group, np.concatenate([table[n][1] for n in names], axis=1))

    io.c0 = together("c0", [n for n in table if n not in A_ONLY + C_ONLY + E_ONLY])
    io.cA = together("cA", A_ONLY)
    io.cC = together("cC", C_ONLY)
    io.cE = together("cE", E_ONLY)
    io.where = table
    ap = {name: give(name, np.ascontiguousarray(a)) for name, a in inputs.items()}
    io.x_prompt, io.x_sample = ap["x_prompt"], ap["x_sample"]
    io.cache_rows = ap["cache_kv"].rearrange("l n s (a c) g d -> (l n s a) (c g d)", a=2)
    io.page_table = ap["page_table"]
    io.cache_win = ap["cache_win"].rearrange("l b w c g d -> (l b) w (c g d)")
    io.state_conv = ap["state_conv"].rearrange("l b j c -> (l b) j c")
    io.w_in = ap["w_in"]
    io.conv_w = ap["conv_w"].rearrange("l j c -> (l j) c")
    io.pe_k = ap["pe_k"].rearrange("o l d -> (o l) d")
    io.pe_v = ap["pe_v"].rearrange("o l d -> (o l) d")
    io.w_ck1 = ap["w_ck1"].rearrange("o l d e -> (o l) d e")
    io.w_cv1 = ap["w_cv1"].rearrange("o l d e -> (o l) d e")
    io.w_ck2 = ap["w_ck2"].rearrange("o e d -> (o e) d")
    io.w_cv2 = ap["w_cv2"].rearrange("o e d -> (o e) d")
    io.g_nsa = ap["g_nsa"].rearrange("l c -> (l c)")
    io.g_conv = ap["g_conv"].rearrange("l c -> (l c)")
    io.rel_bias = ap["rel_bias"]
    io.w_out = ap["w_out"].rearrange("l k n -> (l k) n")
    io.w_rg = ap["w_rg"].rearrange("l k n -> (l k) n")
    io.w_re = ap["w_re"].rearrange("l k n -> (l k) n")
    io.b_rg, io.b_re = ap["b_rg"], ap["b_re"]
    io.ln1_g, io.ln1_b, io.ln2_g, io.ln2_b = ap["ln1_g"], ap["ln1_b"], ap["ln2_g"], ap["ln2_b"]
    io.w_eg = ap["w_eg"].rearrange("l g e k f -> (l g e) k f")
    io.w_eu = ap["w_eu"].rearrange("l g e k f -> (l g e) k f")
    io.w_ed = ap["w_ed"].rearrange("l g e f n -> (l g e) f n")
    out = {name: nc.dram_tensor(f"out_{name}_dram", shape, F32, kind="ExternalOutput").ap() for shape, name in _OUTS}
    io.y_prompt = out["y_prompt"].rearrange("b s d -> (b s) d")
    io.y_sample = out["y_sample"].rearrange("b s d -> (b s) d")
    io.new_kv_prompt = out["new_kv_prompt"].rearrange("l b s c g d -> (l b s) (c g d)")
    io.new_kv_sample = out["new_kv_sample"].rearrange("l b s c g d -> (l b s) (c g d)")
    io.new_win_prompt = out["new_win_prompt"].rearrange("l b s c g d -> (l b s) (c g d)")
    io.new_win_sample = out["new_win_sample"].rearrange("l b s c g d -> (l b) s (c g d)")
    io.new_conv_prompt = out["new_conv_prompt"].rearrange("l b j c -> (l b j) c")
    io.new_conv_sample = out["new_conv_sample"].rearrange("l b j c -> (l b) j c")

    def scratch(name, shape, dt=F32):
        return nc.dram_tensor(name, shape, dt, kind="Internal").ap()

    io.fresh = scratch("fresh_rows", (DB, 6 * KVW))
    io.vhan = scratch("bias_by_distance", (NH, HCOLS))
    io.x1 = scratch("x1_rows", (TOK, D))
    io.yrows = scratch("expert_rows", (2 * TOK + RING_EX * CAP, D))
    hybrid_layer(nc, io)
    return arrays


def kernel(**inputs):
    import concourse.bacc as bacc
    from concourse.bass_utils import run_bass_kernel_spmd

    nc = bacc.Bacc("TRN2", target_bir_lowering=False, num_devices=1)
    arrays = declare(nc, {name: np.asarray(a) for name, a in inputs.items()})
    r = run_bass_kernel_spmd(nc, [arrays], core_ids=[0])
    return tuple(r.results[0][f"out_{name}_dram"] for _, name in _OUTS)
```
